# Optimizing a Trainium2 kernel written in Bass

```python
import jax, jax.numpy as jnp
from jax import lax
import numpy as np

D_MODEL = 1024
BATCH = 1
SEQ = 512
DEPTH = 1

MEM_LEN = 256
EPS = 1e-6

POOL_WINDOWS = (2, 4, 8, 16)
POOL_GROUPS = len(POOL_WINDOWS)
POOL_GROUP_DIM = D_MODEL // 8
POOL_WIDTH = POOL_GROUPS * POOL_GROUP_DIM
MAX_WINDOW = max(POOL_WINDOWS)

SWA_HEAD_DIM = 64
SWA_HEADS = D_MODEL // SWA_HEAD_DIM
SWA_KV_HEADS = 2
SWA_GROUP = SWA_HEADS // SWA_KV_HEADS
SWA_WIDTH = SWA_HEADS * SWA_HEAD_DIM
SWA_KV_WIDTH = SWA_KV_HEADS * SWA_HEAD_DIM
WINDOW = 128
BLOCK = 128
ROPE_THETA = 10000.0

MEM_HEADS = 4
MEM_HEAD_DIM = D_MODEL // 8
MEM_WIDTH = MEM_HEADS * MEM_HEAD_DIM

N_BRANCHES = 3
IN_WIDTH = POOL_WIDTH + SWA_WIDTH + 2 * SWA_KV_WIDTH + MEM_WIDTH + N_BRANCHES * D_MODEL

PEER_HEADS = 8
N_KEYS = 128
N_EXPERTS = N_KEYS * N_KEYS
PEER_KEY_DIM = 256
PEER_HALF = PEER_KEY_DIM // 2
PEER_TOPK = 16
PEER_CHUNK = 128

NEG_INF = -1e30

kernel_name = "hybrid_pool_swa_mem_peer_block"

def rmsnorm(x, g):
    xf = x.astype(jnp.float32)
    y = xf * lax.rsqrt(jnp.mean(xf * xf, axis=-1, keepdims=True) + EPS)
    return (y * g.astype(jnp.float32)).astype(x.dtype)

def pool_mixer(u, w_pool, pool_scale):
    B, S, _ = u.shape
    uf = u.astype(jnp.float32)
    cs = jnp.pad(jnp.cumsum(uf, axis=1), ((0, 0), (MAX_WINDOW, 0), (0, 0)))
    t = jnp.arange(S)
    outs = []
    for gi, w in enumerate(POOL_WINDOWS):
        lo_c, hi_c = gi * POOL_GROUP_DIM, (gi + 1) * POOL_GROUP_DIM
        upper = cs[:, MAX_WINDOW:, lo_c:hi_c]
        lower = cs[:, MAX_WINDOW - w:MAX_WINDOW - w + S, lo_c:hi_c]
        cnt = jnp.minimum(t + 1, w).astype(jnp.float32)[None, :, None]
        outs.append((upper - lower) / cnt - uf[..., lo_c:hi_c])
    pooled = jnp.stack(outs, axis=2)
    mixed = jnp.einsum('bsgc,gcd->bsgd', pooled, w_pool.astype(jnp.float32))
    return (mixed.reshape(B, S, POOL_WIDTH) * pool_scale.astype(jnp.float32)).astype(u.dtype)

def rope(x, pos):
    half = x.shape[-1] // 2
    inv = ROPE_THETA ** (-jnp.arange(half, dtype=jnp.float32) / half)
    ang = pos.astype(jnp.float32)[..., None] * inv
    cos = jnp.cos(ang)[:, :, None, :]
    sin = jnp.sin(ang)[:, :, None, :]
    xf = x.astype(jnp.float32)
    x1, x2 = xf[..., :half], xf[..., half:]
    return jnp.concatenate([x1 * cos - x2 * sin, x2 * cos + x1 * sin], axis=-1).astype(x.dtype)

def swa_with_sinks(q, k, v, sinks):
    B, S = q.shape[0], q.shape[1]
    nb = S // BLOCK
    qb = q.reshape(B, nb, BLOCK, SWA_KV_HEADS, SWA_GROUP, SWA_HEAD_DIM)

    def band(a):
        ab = a.reshape(B, nb, BLOCK, SWA_KV_HEADS, SWA_HEAD_DIM)
        prev = jnp.pad(ab, ((0, 0), (1, 0), (0, 0), (0, 0), (0, 0)))[:, :-1]
        return jnp.concatenate([prev, ab], axis=2)

    kband, vband = band(k), band(v)
    s = jnp.einsum('bnqhgd,bnkhd->bnhgqk', qb.astype(jnp.float32), kband.astype(jnp.float32))
    s = s * (SWA_HEAD_DIM ** -0.5)
    qi = jnp.arange(BLOCK)[:, None] + BLOCK
    ki = jnp.arange(2 * BLOCK)[None, :]
    rel = qi - ki
    mask = (rel >= 0) & (rel < WINDOW)
    valid_prev = (jnp.arange(nb)[:, None, None] > 0) | (ki[None] >= BLOCK)
    mask = mask[None] & valid_prev
    s = jnp.where(mask[None, :, None, None], s, NEG_INF)
    sink = sinks.astype(jnp.float32).reshape(SWA_KV_HEADS, SWA_GROUP)[None, None, :, :, None, None]
    m = jnp.maximum(jnp.max(s, axis=-1, keepdims=True), sink)
    p = jnp.exp(s - m)
    p = p / (jnp.sum(p, axis=-1, keepdims=True) + jnp.exp(sink - m))
    o = jnp.einsum('bnhgqk,bnkhd->bnqhgd', p.astype(v.dtype), vband)
    return o.reshape(B, S, SWA_WIDTH)

def mem_attention(qm, mem_n, w_mem_kv):
    B, S, _ = qm.shape
    kv = mem_n @ w_mem_kv
    km, vm = jnp.split(kv, 2, axis=-1)
    M = mem_n.shape[1]
    q = qm.reshape(B, S, MEM_HEADS, MEM_HEAD_DIM)
    km = km.reshape(B, M, MEM_HEADS, MEM_HEAD_DIM)
    vm = vm.reshape(B, M, MEM_HEADS, MEM_HEAD_DIM)
    s = jnp.einsum('bshd,bmhd->bhsm', q.astype(jnp.float32), km.astype(jnp.float32))
    p = jax.nn.softmax(s * (MEM_HEAD_DIM ** -0.5), axis=-1)
    o = jnp.einsum('bhsm,bmhd->bshd', p.astype(vm.dtype), vm)
    return o.reshape(B, S, MEM_WIDTH)

def peer(h, w_q, sub_keys, expert_u, expert_v):
    B, S, D = h.shape
    T = B * S
    hf = h.reshape(T, D)
    q = (hf @ w_q).reshape(T, PEER_HEADS, 2, PEER_HALF)
    sc = jnp.einsum('thpc,hpnc->thpn', q.astype(jnp.float32), sub_keys.astype(jnp.float32))
    s_top, i_top = lax.top_k(sc, PEER_TOPK)
    cand = (s_top[:, :, 0, :, None] + s_top[:, :, 1, None, :]).reshape(T, PEER_HEADS, PEER_TOPK * PEER_TOPK)
    ids_cand = (i_top[:, :, 0, :, None] * N_KEYS + i_top[:, :, 1, None, :]).reshape(T, PEER_HEADS, PEER_TOPK * PEER_TOPK)
    s_fin, pos = lax.top_k(cand, PEER_TOPK)
    ids = jnp.take_along_axis(ids_cand, pos, axis=-1)
    gates = jax.nn.softmax(s_fin, axis=-1).astype(h.dtype)
    nc = T // PEER_CHUNK
    HK = PEER_HEADS * PEER_TOPK

    def expert_chunk(args):
        xc, idc, gc = args
        u = expert_u[idc]
        a = jax.nn.gelu(jnp.einsum('cd,ckd->ck', xc, u))
        vv = expert_v[idc]
        return jnp.einsum('ck,ckd->cd', gc * a, vv)

    y = lax.map(expert_chunk, (hf.reshape(nc, PEER_CHUNK, D),
                               ids.reshape(nc, PEER_CHUNK, HK),
                               gates.reshape(nc, PEER_CHUNK, HK)))
    return y.reshape(B, S, D)

def setup_inputs(seed: int = 0) -> dict:
    key = jax.random.key(seed)
    ks = jax.random.split(key, 24)
    L, D = DEPTH, D_MODEL
    nrm = jax.random.normal
    x = nrm(ks[0], (BATCH, SEQ, D), jnp.float32)
    mem = nrm(ks[1], (BATCH, MEM_LEN, D), jnp.float32)
    positions = (jnp.arange(SEQ, dtype=jnp.int32)[None, :]
                 + jax.random.randint(ks[2], (BATCH, 1), 0, 1024, dtype=jnp.int32))
    return {
        "x": x,
        "mem": mem,
        "positions": positions,
        "norm1_g": 1.0 + 0.05 * nrm(ks[3], (L, D), jnp.float32),
        "mem_norm_g": 1.0 + 0.05 * nrm(ks[4], (L, D), jnp.float32),
        "w_in": nrm(ks[5], (L, D, IN_WIDTH), jnp.float32) * D ** -0.5,
        "w_pool": nrm(ks[6], (L, POOL_GROUPS, POOL_GROUP_DIM, POOL_GROUP_DIM), jnp.float32) * POOL_GROUP_DIM ** -0.5,
        "pool_scale": 1.0 + 0.1 * nrm(ks[7], (L, POOL_WIDTH), jnp.float32),
        "attn_sinks": 0.5 * nrm(ks[8], (L, SWA_HEADS), jnp.float32),
        "w_mem_kv": nrm(ks[9], (L, D, 2 * MEM_WIDTH), jnp.float32) * D ** -0.5,
        "w_branch_pool": nrm(ks[10], (L, POOL_WIDTH, D), jnp.float32) * POOL_WIDTH ** -0.5,
        "w_branch_swa": nrm(ks[11], (L, SWA_WIDTH, D), jnp.float32) * SWA_WIDTH ** -0.5,
        "w_branch_mem": nrm(ks[12], (L, MEM_WIDTH, D), jnp.float32) * MEM_WIDTH ** -0.5,
        "w_out": nrm(ks[13], (L, D, D), jnp.float32) * D ** -0.5,
        "norm2_g": 1.0 + 0.05 * nrm(ks[14], (L, D), jnp.float32),
        "peer_w_q": nrm(ks[15], (L, D, PEER_HEADS * PEER_KEY_DIM), jnp.float32) * D ** -0.5,
        "peer_sub_keys": nrm(ks[16], (L, PEER_HEADS, 2, N_KEYS, PEER_HALF), jnp.float32) * PEER_HALF ** -0.5,
        "peer_u": nrm(ks[17], (L, N_EXPERTS, D), jnp.float32) * D ** -0.5,
        "peer_v": nrm(ks[18], (L, N_EXPERTS, D), jnp.float32) * 0.5,
        "final_norm_g": 1.0 + 0.05 * nrm(ks[19], (D,), jnp.float32),
    }

def reference(x, mem, positions, norm1_g, mem_norm_g, w_in, w_pool, pool_scale, attn_sinks,
              w_mem_kv, w_branch_pool, w_branch_swa, w_branch_mem, w_out, norm2_g,
              peer_w_q, peer_sub_keys, peer_u, peer_v, final_norm_g):
    B, S, D = x.shape
    splits = np.cumsum([POOL_WIDTH, SWA_WIDTH, SWA_KV_WIDTH, SWA_KV_WIDTH, MEM_WIDTH]).tolist()
    for l in range(DEPTH):
        h = rmsnorm(x, norm1_g[l])
        z = h @ w_in[l]
        u_pool, q, k, v, qm, gate_logits = jnp.split(z, splits, axis=-1)
        y_pool = pool_mixer(u_pool, w_pool[l], pool_scale[l])
        q = rope(q.reshape(B, S, SWA_HEADS, SWA_HEAD_DIM), positions)
        k = rope(k.reshape(B, S, SWA_KV_HEADS, SWA_HEAD_DIM), positions)
        v = v.reshape(B, S, SWA_KV_HEADS, SWA_HEAD_DIM)
        y_swa = swa_with_sinks(q, k, v, attn_sinks[l])
        y_mem = mem_attention(qm, rmsnorm(mem, mem_norm_g[l]), w_mem_kv[l])
        g = jax.nn.sigmoid(gate_logits.reshape(B, S, N_BRANCHES, D))
        merged = (g[:, :, 0] * (y_pool @ w_branch_pool[l])
                  + g[:, :, 1] * (y_swa @ w_branch_swa[l])
                  + g[:, :, 2] * (y_mem @ w_branch_mem[l]))
        x = x + merged @ w_out[l]
        h2 = rmsnorm(x, norm2_g[l])
        x = x + peer(h2, peer_w_q[l], peer_sub_keys[l], peer_u[l], peer_v[l])
    return rmsnorm(x, final_norm_g)


_drawn_inputs = setup_inputs


def setup_inputs(seed=0):
    import zlib

    import numpy as np

    out = dict(_drawn_inputs(seed))
    spreads = {}
    factors = {'mem_norm_g': 3.722, 'attn_sinks': 8.0}
    for name, (base, spread) in spreads.items():
        noise = np.random.default_rng([zlib.crc32(name.encode()), seed]).standard_normal(out[name].shape)
        drawn = base * np.exp(spread * noise) if base else spread * noise
        out[name] = __import__('jax').numpy.asarray(drawn.astype(out[name].dtype))
    for name, factor in factors.items():
        out[name] = (out[name] * factor).astype(out[name].dtype)
    return out
```

```python
import math
from contextlib import ExitStack

import concourse.bass as bass
import numpy as np
from concourse import mybir

T, D, P = 512, 1024, 128
TT, KC = T // P, D // P
M = 256
MT = M // P
HEAD, WINDOW = 64, 128
POOL_WINDOWS = (2, 4, 8, 16)
PAD = max(POOL_WINDOWS)
PEER_H, TOPK, NKEYS = 8, 16, 128
HK = PEER_H * TOPK
NEXP = NKEYS * NKEYS
NI = NEXP // P
NEG = -1e30
BELOW = -3.0e38
EPS = 1e-6

S_KM, S_VM, S_K, S_V, S_POOL = 0, 4, 8, 10, 11
S_Q, S_QM, S_GATE = 15, 23, 27
GATE_CHUNKS = 5
S_OUT = S_GATE + GATE_CHUNKS * KC
S_PQ = S_OUT + KC
S_U = S_PQ + 2 * PEER_H
S_EV = S_U + NI
CHUNKS = S_EV + NI
RAW = 4
Q_ORDER = [q // 2 + 4 * (q % 2) for q in range(8)]
R_KM, R_K, R_POOL, R_Q, R_QM, R_PQ, R_U = 0, 4, 6, 10, 18, 22, 38

I_PLAIN = 64
TOK_I = T // (NI - I_PLAIN)
STAGE_T = 64
SMALLS = 7
AHEAD = 6


def build(nc, dram, out):
    f32, f32r, bf16, u32, i32 = (mybir.dt.float32, mybir.dt.float32r, mybir.dt.bfloat16,
                                 mybir.dt.uint32, mybir.dt.int32)
    ACT, ALU, AX = mybir.ActivationFunctionType, mybir.AluOpType, mybir.AxisListType

    with ExitStack() as ctx:
        arena_size = 207 * 1024
        arena = ctx.enter_context(nc.sbuf_tensor("arena", [P, arena_size], mybir.dt.uint8))
        arena_at = int(nc.sbuf_base) - arena_size
        assert arena_at % 32 == 0

        class Place:
            def __init__(self, at):
                self.at = at

            def __call__(self, name, shape, dt=f32):
                t = nc.alloc_sbuf_tensor_at(name, [P] + list(shape), dt, offset=arena_at + self.at)
                size = int(np.prod(shape)) * (2 if dt == bf16 else 4)
                self.at += (size + 31) // 32 * 32
                assert self.at <= arena_size, (name, self.at)
                return t

        keep = Place(0)
        x_sb = keep("x_sb", [TT, D])
        hT_hi = keep("hT_hi", [KC, T], f32r)
        hT_lo = keep("hT_lo", [KC, T], f32r)
        raw = keep("raw", [RAW, D])
        w_hi = keep("w_hi", [2, D], f32r)
        w_lo = keep("w_lo", [2, D], f32r)
        subkeys = keep("subkeys", [2 * PEER_H, NKEYS])
        ident = keep("ident", [P])
        gains = keep("gains", [3, KC])
        pscale = keep("pscale", [4])
        sinks = keep("sinks", [16])
        freq = keep("freq", [2])
        iota_b = keep("iota_b", [NKEYS], bf16)
        iota_k = keep("iota_k", [TOPK])
        eps = keep("eps", [1])
        ssum = keep("ssum", [8])
        std = keep("std", [8])
        rstd = keep("rstd", [8])
        mx = keep("mx", [8])
        mcap = keep("mcap", [8])
        negm = keep("negm", [8])
        sdiff = keep("sdiff", [8])
        sexp = keep("sexp", [8])
        rsum = keep("rsum", [8])
        den = keep("den", [8])
        rinv = keep("rinv", [8])
        front = keep.at

        y = Place(front)
        yT_hi = y("yT_hi", [16, T], f32r)
        yT_lo = y("yT_lo", [16, T], f32r)
        s = Place(front)
        mem_sb = s("mem_sb", [MT, D])
        memn = s("memn", [MT, D])
        memT_hi = s("memT_hi", [KC, M], f32r)
        memT_lo = s("memT_lo", [KC, M], f32r)
        xn = s("xn", [TT, D])
        assert s.at <= y.at
        a = Place(y.at)
        pos_i = a("pos_i", [T], i32)
        cosT = a("cosT", [T])
        sinT = a("sinT", [T])
        mask = a("mask", [2, 2 * WINDOW])
        kdup = a("kdup", [2, WINDOW + T])
        vdup = a("vdup", [2, TT + 1, P])
        kmT = a("kmT", [4, M])
        vm = a("vm", [MT, T])
        qr = a("qr", [2, T])
        swp = a("swp", [T])
        prob = a("prob", [TT, 2, 2 * WINDOW])
        probT = a("probT", [2, T])
        g = Place(y.at)
        mg_hi = g("mg_hi", [KC, T], f32r)
        mg_lo = g("mg_lo", [KC, T], f32r)
        sg = g("sg", [3, T])
        part = g("part", [3, T])
        p = Place(max(a.at, g.at))
        ub = p("ub", [PAD + T])
        sA = p("sA", [PAD + T])
        sB = p("sB", [PAD + T])
        rcnt = p("rcnt", [4, PAD])
        wpool = p("wpool", [4, P])

        r = Place(front)
        abuf = r("abuf", [2, T])
        IF = r("IF", [TT, HK])
        JF = r("JF", [TT, HK])
        FV = r("FV", [TT, HK])
        IT = r("IT", [T])
        JT = r("JT", [T])
        GT = r("GT", [T])
        R1 = r("R1", [T])
        R2 = r("R2", [T])
        gsm = r("gsm", [TT * PEER_H])
        gbf = r("gbf", [T], bf16)
        ohJ = r("ohJ", [2, TOK_I, NKEYS], bf16)
        ohI = r("ohI", [2, TOK_I, 3, NKEYS], bf16)
        late = r.at
        sc = r("sc", [TT, 2 * PEER_H, NKEYS])
        cand = r("cand", [PEER_H, TOPK * TOPK])
        cand2 = r("cand2", [PEER_H, TOPK * TOPK])
        top = r("top", [PEER_H, 2, TOPK])
        topi = r("topi", [PEER_H, 2, TOPK], u32)
        topf = r("topf", [PEER_H, 2, TOPK])
        fin = r("fin", [PEER_H, TOPK])
        fpos = r("fpos", [HK], u32)
        fsel = r("fsel", [HK], u32)
        fself = r("fself", [HK])
        scur = cand
        scur2 = cand2
        qs = r("qs", [2, T])
        x2n = Place(late)("x2n", [TT, D])
        gstage = Place(late)("gstage", [2, NKEYS, STAGE_T])
        v = Place(late)
        a_in = v("a_in", [4, T])
        g_in = v("g_in", [4, T])
        wf = v("wf", [2, T])
        wT_hi = v("wT_hi", [2, T], f32r)
        wT_lo = v("wT_lo", [2, T], f32r)
        gfin = v("gfin", [D])
        junk = v("junk", [D])

        bank = [ctx.enter_context(nc.psum_tensor(f"bank{b}", [P, 512], f32)) for b in range(8)]

        def sem(name):
            return ctx.enter_context(nc.semaphore(name))

        raw_loaded = [sem(f"raw_loaded{i}") for i in range(RAW)]
        hi_ready, lo_ready, chunk_used = sem("hi_ready"), sem("lo_ready"), sem("chunk_used")
        proj_read = sem("proj_read")
        mem_loaded, x_loaded, small_loaded = sem("mem_loaded"), sem("x_loaded"), sem("small_loaded")
        consts = sem("consts")
        pool_step, dve_step, act_step = sem("pool_step"), sem("dve_step"), sem("act_step")
        eps_set = sem("eps_set")
        std_ready = sem("std_ready")
        normed = sem("normed")
        turned = sem("turned")
        turned_hi, turned_lo = sem("turned_hi"), sem("turned_lo")
        vm_read = sem("vm_read")
        angles, sines = sem("angles"), sem("sines")
        swapped, rotated = sem("swapped"), sem("rotated")
        v_ready = sem("v_ready")
        pooled, mixed = sem("pooled"), sem("mixed")
        y_hi, y_lo = sem("y_hi"), sem("y_lo")
        scored, score_read, capped = sem("scored"), sem("score_read"), sem("capped")
        expd, prob_ready = sem("expd"), sem("prob_ready")
        probT_done, probT_read = sem("probT_done"), sem("probT_read")
        attended = sem("attended")
        gated, branch_read = sem("gated"), sem("branch_read")
        merged, merged_hi, merged_lo = sem("merged"), sem("merged_hi"), sem("merged_lo")
        x2_ready = sem("x2_ready")
        sub_done, sub_read = sem("sub_done"), sem("sub_read")
        shifted, exp_final, retrieved = sem("shifted"), sem("exp_final"), sem("retrieved")
        spread, spread_read = sem("spread"), sem("spread_read")
        hot_ready, gate_mm, gate_read = sem("hot_ready"), sem("gate_mm"), sem("gate_read")
        a_stored = [sem("a_stored0"), sem("a_stored1")]
        g_stored = [sem("g_stored0"), sem("g_stored1")]
        ag_loaded = [sem(f"ag_loaded{i}") for i in range(4)]
        gfin_loaded = sem("gfin_loaded")
        weighted, weighted_hi, weighted_lo = sem("weighted"), sem("weighted_hi"), sem("weighted_lo")
        x3_ready, final_std, final_ready, out_stored = (sem("x3_ready"), sem("final_std"),
                                                        sem("final_ready"), sem("out_stored"))

        block = ctx.enter_context(nc.Block())

        class Steps:
            def __init__(self, eng, own):
                self.eng, self.own, self.value, self.made = eng, own, 0, 0

            def __call__(self, ins):
                ins.then_inc(self.own, 1)
                self.value, self.made = self.value + 1, self.made + 1
                self.eng.wait_ge(self.own, self.value)

        @block.sync
        def _(sp):
            stream = dram["stream"]
            a_rows = dram["a"]
            g_rows = dram["g"]

            def load(n, slot, fresh=False):
                if not fresh:
                    sp.wait_ge(lo_ready, n - RAW + 1)
                sp.dma_start(raw[:, slot, :], stream[bass.ds(n, 1), :, :].rearrange("n p c -> p (n c)")
                             ).then_inc(raw_loaded[slot], 16)

            for n in range(RAW):
                load(n, n, fresh=True)
            first_u = S_U + AHEAD
            with sp.Fori(RAW, first_u // RAW * RAW - RAW + 1, RAW) as n0:
                for k in range(RAW):
                    load(n0 + k, k)
            for n in range(first_u // RAW * RAW, first_u):
                load(n, n % RAW)

            def store_a(i, parity):
                sp.wait_ge(proj_read, i + (R_U + 1))
                sp.dma_start(a_rows[bass.ds(i, 1), :, :].rearrange("n p c -> p (n c)"),
                             abuf[:, parity, :]).then_inc(a_stored[parity], 16)

            with sp.Fori(0, I_PLAIN - RAW + 1, RAW) as i0:
                for k in range(RAW):
                    load(i0 + (first_u + k), (first_u + k) % RAW)
                    store_a(i0 + k, k % 2)
            per = STAGE_T // TOK_I
            with sp.Fori(0, T // STAGE_T - 2 + 1, 2) as b0:
                for half in range(2):
                    for k in range(per):
                        at = I_PLAIN + half * per + k
                        load(b0 * per + (first_u + at), (first_u + at) % RAW)
                        store_a(b0 * per + at, at % 2)
                    sp.wait_ge(gate_read, (b0 + (half + 1)) * (2 * per) + 2)
                    sp.dma_start(g_rows[:, :, bass.ds((b0 + half) * STAGE_T, STAGE_T)].rearrange("i j t -> j i t"),
                                 gstage[:, half, :, :]).then_inc(g_stored[half], 16)
            for parity in range(2):
                sp.wait_ge(a_stored[parity], 16 * NI // 2)
                sp.wait_ge(g_stored[parity], 16 * (T // STAGE_T) // 2)

            def reload(i, slot, fresh=False):
                if not fresh:
                    sp.wait_ge(weighted, i - 3)
                sp.dma_start(a_in[:, slot, :], a_rows[bass.ds(i, 1), :, :].rearrange("n p c -> p (n c)")
                             ).then_inc(ag_loaded[slot], 16)
                sp.dma_start(g_in[:, slot, :], g_rows[bass.ds(i, 1), :, :].rearrange("n p c -> p (n c)")
                             ).then_inc(ag_loaded[slot], 16)

            for i in range(4):
                reload(i, i, fresh=True)
            sp.dma_start(gfin[:, :], dram["gfin"].broadcast_to([P, D])).then_inc(gfin_loaded, 16)
            nxt = first_u + NI
            left = CHUNKS - nxt
            looped = left // 4 * 4
            with sp.Fori(0, looped - 4 + 1, 4) as i0:
                for k in range(4):
                    load(i0 + (nxt + k), (nxt + k) % RAW)
                    reload(i0 + (k + 4), k)
            for i in range(looped, NI):
                if i < left:
                    load(nxt + i, (nxt + i) % RAW)
                if i + 4 < NI:
                    reload(i + 4, i % 4)

            for t in range(TT):
                sp.wait_ge(final_ready, t + 1)
                sp.dma_start(out[t * P:(t + 1) * P, :], x_sb[:, t, :]).then_inc(out_stored, 16)
            sp.wait_ge(out_stored, 16 * TT)

        @block.gpsimd
        def _(pool):
            step = Steps(pool, pool_step)
            step(pool.memset(ident[:, :], 0.0))
            pool.affine_select(out=ident[:, :], in_=ident[:, :], compare_op=ALU.not_equal, fill=1.0,
                               base=0, pattern=[[-1, P]], channel_multiplier=1).then_inc(consts, 1)
            step(pool.memset(mask[:, :, :], 0.0))
            for f in range(2):
                step(pool.affine_select(out=mask[:, f, :], in_=mask[:, f, :], compare_op=ALU.is_ge, fill=NEG,
                                        base=WINDOW, pattern=[[-1, 2 * WINDOW]], channel_multiplier=1))
                step(pool.affine_select(out=mask[:, f, :], in_=mask[:, f, :], compare_op=ALU.is_ge, fill=NEG,
                                        base=-1, pattern=[[1, 2 * WINDOW]], channel_multiplier=-1))
            step(pool.affine_select(out=mask[:, 0, :], in_=mask[:, 0, :], compare_op=ALU.is_ge, fill=NEG,
                                    base=-WINDOW, pattern=[[1, 2 * WINDOW]], channel_multiplier=0))
            pool.iota(iota_b[:, :], pattern=[[1, NKEYS]], base=0, channel_multiplier=0,
                      allow_small_or_imprecise_dtypes=True)
            pool.iota(iota_k[:, :], pattern=[[1, TOPK]], base=0, channel_multiplier=0,
                      allow_small_or_imprecise_dtypes=True)
            pool.iota(rcnt[:, :, :], pattern=[[0, 4], [1, PAD]], base=1, channel_multiplier=0,
                      allow_small_or_imprecise_dtypes=True).then_inc(consts, 1)

            def low(n, k):
                pool.wait_ge(hi_ready, n + 1)
                pool.tensor_tensor(w_lo[:, k % 2, :], raw[:, k % RAW, :], w_hi[:, k % 2, :].bitcast(f32),
                                   ALU.subtract).then_inc(lo_ready, 1)

            with pool.Fori(0, CHUNKS // RAW * RAW - RAW + 1, RAW) as n0:
                for k in range(RAW):
                    low(n0 + k, k)
            for n in range(CHUNKS // RAW * RAW, CHUNKS):
                low(n, n)

        @block.tensor
        def _(pe):
            passes = ((w_hi, 0), (w_hi, 1), (w_lo, 0))

            def chunk(n):
                pe.wait_ge(lo_ready, n + 1)

            def product(dst, slot, rhs, k0=0, k1=KC, r0=0, used=True):
                for k in range(k0, k1):
                    for wi, (w, low) in enumerate(passes):
                        last = pe.matmul(dst, w[:, slot, k * P:(k + 1) * P], rhs[low][:, r0 + k - k0, :],
                                         start=(k == k0 and wi == 0), stop=(k == k1 - 1 and wi == 2))
                if used:
                    last.then_inc(chunk_used, 1)
                return last

            hT = (hT_hi, hT_lo)
            memT = (memT_hi, memT_lo)
            yT = (yT_hi, yT_lo)

            def project(n, rn, rhs, cols=T, strict=False):
                chunk(n)
                if strict:
                    pe.wait_ge(proj_read, rn)
                elif rn >= 2:
                    pe.wait_ge(proj_read, rn - 1)
                product(bank[rn % 2][:, 0:cols], n % 2, rhs)

            pe.wait_ge(consts, 1)
            pe.wait_ge(normed, 1)
            for k in range(KC):
                for t in range(MT):
                    last = pe.transpose(bank[k][:, t * P:(t + 1) * P],
                                        memn[:, t, k * P:(k + 1) * P], ident[:, :])
                last.then_inc(turned, 1)
            pe.wait_ge(turned_lo, KC)
            for h in range(4):
                project(S_KM + h, R_KM + h, memT, cols=M)
            for q in range(4):
                chunk(S_VM + q)
                for k in range(2):
                    for m in range(MT):
                        for low_m, w in ((0, w_hi), (0, w_lo), (1, w_hi)):
                            last = pe.matmul(bank[2 + m][:, :], memT[low_m][:, 2 * q + k, m * P:(m + 1) * P],
                                             w[:, q % 2, k * T:(k + 1) * T],
                                             start=(q == 0 and k == 0 and low_m == 0 and w is w_hi),
                                             stop=(q == 3 and k == 1 and low_m == 1))
                last.then_inc(chunk_used, 1)

            def turn(src, tok_ready, first, base):
                for k in range(KC):
                    if k >= 4 or not first:
                        pe.wait_ge(turned_lo, base + max(k - 3, 0))
                    for t in range(TT):
                        if k == 0:
                            pe.wait_ge(normed, tok_ready + t)
                        last = pe.transpose(bank[4 + k % 4][:, t * P:(t + 1) * P],
                                            src[:, t, k * P:(k + 1) * P], ident[:, :])
                    last.then_inc(turned, 1)

            turn(xn, 2, True, KC)
            pe.wait_ge(turned_lo, 2 * KC)
            for j in range(2):
                project(S_K + j, R_K + j, hT, strict=(j == 0))
            chunk(S_V)
            for t in range(TT):
                for k in range(KC):
                    for low_h, w in ((0, w_hi), (0, w_lo), (1, w_hi)):
                        last = pe.matmul(bank[4][:, t * P:(t + 1) * P], hT[low_h][:, k, t * P:(t + 1) * P],
                                         w[:, S_V % 2, k * P:(k + 1) * P],
                                         start=(k == 0 and low_h == 0 and w is w_hi), stop=(k == KC - 1 and low_h == 1))
            last.then_inc(chunk_used, 1)

            def mix(gi):
                pe.wait_ge(pooled, gi + 1)
                if gi >= 2:
                    pe.wait_ge(y_lo, gi - 1)
                if gi < 2:
                    pe.wait_ge(vm_read, 1)
                pe.matmul(bank[2 + gi % 2][:, :], wpool[:, gi, :], ub[:, PAD:], start=True,
                          stop=True).then_inc(mixed, 1)

            for gi in range(4):
                project(S_POOL + gi, R_POOL + gi, hT)
                if gi >= 1:
                    mix(gi - 1)
            project(S_Q, R_Q, hT)
            mix(3)
            for u in range(8):
                kv = u % 2
                pe.wait_ge(rotated, 2 + u + 1)
                if u == 0:
                    pe.wait_ge(y_lo, 4)
                else:
                    pe.wait_ge(y_lo, 4 + u)
                for n in range(TT):
                    for h in range(2):
                        last = pe.matmul(bank[2 + 2 * h + n // 2][:, n % 2 * 2 * WINDOW:(n % 2 + 1) * 2 * WINDOW],
                                         qr[h * HEAD:(h + 1) * HEAD, u % 2, n * P:(n + 1) * P],
                                         kdup[h * HEAD:(h + 1) * HEAD, kv, n * P:n * P + 2 * WINDOW],
                                         start=True, stop=True)
                        if n % 2:
                            last.then_inc(scored, 1)
                project(S_Q + u + 1, R_Q + u + 1, hT)
                if u == 0:
                    pe.wait_ge(v_ready, 1)
                pe.wait_ge(score_read, 4 * (u + 1))
                for n in range(TT + 1):
                    if n < TT:
                        pe.wait_ge(prob_ready, 4 * u + n + 1)
                        if 4 * u + n >= 2:
                            pe.wait_ge(probT_read, 4 * u + n - 1)
                        for h in range(2):
                            for half in range(2):
                                last = pe.transpose(bank[6 + n % 2][:, (2 * h + half) * P:(2 * h + half + 1) * P],
                                                    prob[:, n, h, half * P:(half + 1) * P], ident[:, :])
                        last.then_inc(probT_done, 1)
                    if n >= 1:
                        pe.wait_ge(probT_read, 4 * u + n)
                        for h in range(2):
                            for half in range(2):
                                last = pe.matmul(bank[2 + h][:, (n - 1) * P:n * P], vdup[:, kv, n - 1 + half, :],
                                                 probT[:, (n - 1) % 2, (2 * h + half) * P:(2 * h + half + 1) * P],
                                                 start=(half == 0), stop=(half == 1))
                last.then_inc(attended, 1)
            for u in range(4):
                pe.wait_ge(proj_read, R_QM + u + 1)
                pe.wait_ge(y_lo, 12 + u)
                for n in range(TT):
                    pe.matmul(bank[2 + n][:, 0:M], qr[:, u % 2, n * P:(n + 1) * P], kmT[:, u, :],
                              start=True, stop=True).then_inc(scored, 1)
                if u < 3:
                    project(S_QM + u + 1, R_QM + u + 1, hT)
                pe.wait_ge(score_read, 32 + 4 * (u + 1))
                for j in range(2):
                    pe.wait_ge(prob_ready, 32 + 4 * u + 2 * j + 2)
                    pe.wait_ge(probT_read, 32 + 2 * u + j - 1)
                    for n in (2 * j, 2 * j + 1):
                        for half in range(2):
                            last = pe.transpose(bank[6 + j][:, (n % 2 * 2 + half) * P:(n % 2 * 2 + half + 1) * P],
                                                prob[:, n, 0, half * P:(half + 1) * P], ident[:, :])
                    last.then_inc(probT_done, 1)
                for j in range(2):
                    pe.wait_ge(probT_read, 32 + 2 * u + j + 1)
                    for n in (2 * j, 2 * j + 1):
                        for half in range(2):
                            last = pe.matmul(bank[2][:, n * P:(n + 1) * P], vm[:, half, u * P:(u + 1) * P],
                                             probT[:, j, (n % 2 * 2 + half) * P:(n % 2 * 2 + half + 1) * P],
                                             start=(half == 0), stop=(half == 1))
                last.then_inc(attended, 1)
            pe.wait_ge(y_lo, 16)
            with pe.Fori(0, KC - 2 + 1, 2) as c0:
                for dc in range(2):
                    for b in range(3):
                        n = S_GATE + GATE_CHUNKS * dc + b
                        chunk(c0 * GATE_CHUNKS + n)
                        if b == 0:
                            pe.wait_ge(gated, c0 * 3 + (3 * dc + 3))
                        product(bank[b][:, :], n % 2, hT)
                    n = S_GATE + GATE_CHUNKS * dc + 3
                    pe.wait_ge(branch_read, c0 * 3 + (3 * dc + 3))
                    chunk(c0 * GATE_CHUNKS + n)
                    product(bank[3][:, :], n % 2, yT, 0, 4, 0, used=False)
                    product(bank[4][:, :], n % 2, yT, 4, 8, 4)
                    chunk(c0 * GATE_CHUNKS + (n + 1))
                    product(bank[5][:, :], (n + 1) % 2, yT, 0, 8, 8)
            pe.wait_ge(gated, 3 * KC + 3)
            pe.wait_ge(branch_read, 3 * KC + 3)
            pe.wait_ge(merged_lo, KC)

            def spread_sum(slot, lhs, first, final):
                for t in range(TT):
                    for w, low_l in ((w_hi, 0), (w_lo, 0), (w_hi, 1)):
                        for half in range(2):
                            last = pe.matmul(bank[2 * t + half][:, :], lhs[low_l][:, t * P:(t + 1) * P],
                                             w[:, slot, half * 512:(half + 1) * 512],
                                             start=first and low_l == 0 and w is w_hi, stop=final and low_l == 1)
                last.then_inc(chunk_used, 1)
                return last

            for k in range(KC):
                chunk(S_OUT + k)
                spread_sum((S_OUT + k) % 2, (mg_hi[:, k, :], mg_lo[:, k, :]), k == 0, k == KC - 1)
            turn_ready = 2 + TT
            pe.wait_ge(x2_ready, TT)
            turn(x2n, turn_ready, False, 2 * KC)
            pe.wait_ge(turned_lo, 3 * KC)
            with pe.Fori(0, 2 * PEER_H - 2 + 1, 2) as c0:
                for dc in range(2):
                    n, rn = S_PQ + dc, R_PQ + dc
                    chunk(n + c0)
                    pe.wait_ge(proj_read, rn - 1 + c0)
                    product(bank[rn % 2][:, :], n % 2, hT)
                for dc in range(2):
                    pe.wait_ge(proj_read, c0 + (R_PQ + dc + 1))
                    pe.wait_ge(sub_read, c0 + (dc + 1))
                    for t in range(TT):
                        last = pe.matmul(bank[2 + dc][:, t * P:(t + 1) * P], qs[:, dc, t * P:(t + 1) * P],
                                         subkeys[:, bass.ds(c0 + dc, 1), :], start=True, stop=True)
                    last.then_inc(sub_done, 1)

            def experts(i0, di):
                n, rn = S_U + di, R_U + di
                chunk(n + i0)
                pe.wait_ge(proj_read, rn - 1 + i0)
                product(bank[rn % 2][:, :], n % 2, hT)

            with pe.Fori(0, I_PLAIN - 2 + 1, 2) as i0:
                for di in range(2):
                    experts(i0, di)
            pe.wait_ge(sub_read, 2 * PEER_H + 2)
            pe.wait_ge(retrieved, 1)
            for j, src in enumerate((IF, JF, FV)):
                for t in range(TT):
                    last = pe.transpose(bank[2 + j][:, t * P:(t + 1) * P], src[:, t, :], ident[:, :])
                last.then_inc(spread, 1)
            pe.wait_ge(spread_read, 1)
            with pe.Fori(0, NI - I_PLAIN - 2 + 1, 2) as i0:
                for di in range(2):
                    experts(i0 + I_PLAIN, di)
                    for b in range(2):
                        pe.wait_ge(gate_read, i0 * 2 + (2 * di + b + 1))
                        pe.wait_ge(hot_ready, i0 * 2 + (2 * di + b + 1))
                        for tk in range(TOK_I // 2):
                            at = b * (TOK_I // 2) + tk
                            for q in range(3):
                                last = pe.matmul(bank[2 + b][:, tk * P:(tk + 1) * P], ohJ[:, di, at, :],
                                                 ohI[:, di, at, q, :], start=(q == 0), stop=(q == 2))
                        last.then_inc(gate_mm, 1)
            pe.wait_ge(gate_read, 2 * (NI - I_PLAIN) + 2)
            pe.wait_ge(proj_read, R_U + NI)

            def weigh(i0, di, first=False, final=False):
                n = S_EV + di
                chunk(n + i0)
                pe.wait_ge(weighted_lo, i0 + (di + 1))
                return spread_sum(n % 2, (wT_hi[:, di % 2, :], wT_lo[:, di % 2, :]), first, final)

            for i in range(2):
                weigh(0, i, first=(i == 0))
            with pe.Fori(2, NI - 2 - 2 + 1, 2) as i0:
                for di in range(2):
                    weigh(i0, di)
            for i in range(NI - 2, NI):
                weigh(0, i, final=(i == NI - 1))

        @block.scalar
        def _(act):
            step = Steps(act, act_step)
            for t in range(MT):
                act.dma_start(mem_sb[:, t, :], dram["mem"][t * P:(t + 1) * P, :]).then_inc(mem_loaded, 16)
            for t in range(TT):
                act.dma_start(x_sb[:, t, :], dram["x"][t * P:(t + 1) * P, :]).then_inc(x_loaded, 16)
            smalls = [(gains[:, :, :], dram["gains"]), (pscale[:, :], dram["pscale"]),
                      (wpool[:, :, :], dram["wpool"]), (sinks[:, :], dram["sinks"].broadcast_to([P, 16])),
                      (freq[:, :], dram["freq"]), (pos_i[:, :], dram["positions"].broadcast_to([P, T])),
                      (subkeys[:, :, :], dram["subkeys"])]
            assert len(smalls) == SMALLS
            for dst, src in smalls:
                act.dma_start(dst, src).then_inc(small_loaded, 16)

            def split(base, loop=0):
                slot = base % RAW
                act.wait_ge(raw_loaded[slot], loop * (16 // RAW) + (base // RAW + 1) * 16)
                if base >= 2:
                    act.wait_ge(chunk_used, loop + (base - 1))
                act.activation(w_hi[:, base % 2, :], raw[:, slot, :], ACT.Copy).then_inc(hi_ready, 1)

            act.wait_ge(eps_set, 1)
            act.wait_ge(mem_loaded, 16 * MT)
            for t in range(MT):
                last = act.activation(memn[:, t, :], mem_sb[:, t, :], ACT.Square, accum_out=ssum[:, t:t + 1])
            step(last)
            act.activation(std[:, 0:MT], ssum[:, 0:MT], ACT.Sqrt, scale=1.0 / D,
                           bias=eps[:, :]).then_inc(std_ready, 1)
            split(0)
            split(1)
            act.wait_ge(x_loaded, 16 * TT)
            for t in range(TT):
                last = act.activation(xn[:, t, :], x_sb[:, t, :], ACT.Square, accum_out=ssum[:, 2 + t:3 + t])
            step(last)
            act.activation(std[:, 2:2 + TT], ssum[:, 2:2 + TT], ACT.Sqrt, scale=1.0 / D,
                           bias=eps[:, :]).then_inc(std_ready, 1)
            act.wait_ge(small_loaded, 16 * SMALLS)
            for k in range(KC):
                act.wait_ge(turned, k + 1)
                act.activation(memT_hi[:, k, :], bank[k][:, 0:M], ACT.Copy,
                               scale=gains[:, 1, k:k + 1]).then_inc(turned_hi, 1)
            act.wait_ge(angles, 2)
            act.activation(cosT[:, :], cosT[:, :], ACT.Sin).then_inc(sines, 1)
            act.activation(sinT[:, :], sinT[:, :], ACT.Sin, scale=freq[:, 1:2]).then_inc(sines, 1)
            for h in range(4):
                act.wait_ge(chunk_used, S_KM + h + 1)
                split(S_KM + h + 2)
                act.activation(kmT[:, h, :], bank[(R_KM + h) % 2][:, 0:M], ACT.Copy).then_inc(proj_read, 1)
            for q in range(4):
                split(S_VM + q + 2)
            for m in range(MT):
                last = act.activation(vm[:, m, :], bank[2 + m][:, :], ACT.Copy)
            last.then_inc(vm_read, 1)

            def turn_high(gain, base):
                for k in range(KC):
                    act.wait_ge(turned, base + k + 1)
                    act.activation(hT_hi[:, k, :], bank[4 + k % 4][:, :], ACT.Copy,
                                   scale=gains[:, gain, k:k + 1]).then_inc(turned_hi, 1)

            turn_high(0, KC)

            def swap(j, rn, n):
                act.wait_ge(chunk_used, n + 1)
                if j >= 1:
                    act.wait_ge(rotated, j)
                for qd in range(4):
                    last = act.activation(swp[32 * qd:32 * qd + 32, :],
                                          bank[rn % 2][32 * (qd ^ 1):32 * (qd ^ 1) + 32, :], ACT.Copy)
                last.then_inc(swapped, 1)

            for j in range(2):
                split(S_K + j + 2)
                swap(j, R_K + j, S_K + j)
            split(S_V + 2)
            act.wait_ge(chunk_used, S_V + 1)
            act.wait_ge(eps_set, 2)
            vb = bank[4][:, :].rearrange("p (t c) -> p t c", t=TT)
            for kv in range(2):
                for dup in range(2):
                    last = act.activation(vdup[:, kv, 1:, dup * HEAD:(dup + 1) * HEAD],
                                          vb[:, :, kv * HEAD:(kv + 1) * HEAD], ACT.Copy)
            last.then_inc(v_ready, 1)

            def mix_high(gi):
                act.wait_ge(mixed, gi + 1)
                act.activation(yT_hi[:, gi, :], bank[2 + gi % 2][:, :], ACT.Copy,
                               scale=pscale[:, gi:gi + 1]).then_inc(y_hi, 1)

            for gi in range(4):
                split(S_POOL + gi + 2)
                if gi >= 1:
                    mix_high(gi - 1)
            split(S_Q + 2)
            swap(2, R_Q, S_Q)
            mix_high(3)

            for u in range(8):
                act.wait_ge(capped, u + 1)
                for n in range(TT):
                    for h in range(2):
                        last = act.activation(prob[:, n, h, :], prob[:, n, h, :], ACT.Exp, scale=HEAD ** -0.5,
                                              bias=negm[:, 2 * n + h:2 * n + h + 1],
                                              accum_out=rsum[:, 2 * n + h:2 * n + h + 1])
                act.activation(sexp[:, :], sdiff[:, :], ACT.Exp).then_inc(expd, 1)
                split(S_Q + u + 3)
                if u < 7:
                    swap(3 + u, R_Q + u + 1, S_Q + u + 1)
                else:
                    act.wait_ge(chunk_used, S_QM + 1)
                    act.activation(qr[:, 0, :], bank[R_QM % 2][:, :], ACT.Copy).then_inc(proj_read, 1)
                for n in range(TT):
                    act.wait_ge(probT_done, 4 * u + n + 1)
                    act.activation(probT[:, n % 2, :], bank[6 + n % 2][:, :], ACT.Copy).then_inc(probT_read, 1)
                act.wait_ge(attended, u + 1)
                for h in range(2):
                    rows = slice(h * HEAD, (h + 1) * HEAD)
                    last = act.activation(yT_hi[rows, 8 + u, :], bank[2 + h][rows, :], ACT.Copy)
                last.then_inc(y_hi, 1)
            for u in range(4):
                act.wait_ge(capped, 8 + u + 1)
                for n in range(TT):
                    last = act.activation(prob[:, n, 0, :], bank[2 + n][:, 0:M], ACT.Exp, scale=P ** -0.5,
                                          bias=negm[:, n:n + 1], accum_out=rsum[:, n:n + 1])
                    last.then_inc(score_read, 1)
                if u < 3:
                    split(S_QM + u + 3)
                    act.wait_ge(chunk_used, S_QM + u + 2)
                    act.activation(qr[:, (u + 1) % 2, :], bank[(R_QM + u + 1) % 2][:, :],
                                   ACT.Copy).then_inc(proj_read, 1)
                for j in range(2):
                    act.wait_ge(probT_done, 32 + 2 * u + j + 1)
                    act.activation(probT[:, j, :], bank[6 + j][:, :], ACT.Copy).then_inc(probT_read, 1)
                act.wait_ge(attended, 8 + u + 1)
                act.activation(yT_hi[:, 4 + u, :], bank[2][:, :], ACT.Copy).then_inc(y_hi, 1)
            act.sem_inc(gated, 3)
            with act.Fori(0, KC - 4 + 1, 4) as c0:
                for dc in range(4):
                    for q in range(GATE_CHUNKS):
                        base = S_GATE + GATE_CHUNKS * dc + q
                        split(base + 2, loop=c0 * GATE_CHUNKS)
                        if q == 0:
                            act.wait_ge(branch_read, c0 * 3 + (3 * dc + 3))
                        if q < 3:
                            act.wait_ge(chunk_used, c0 * GATE_CHUNKS + (base + 1))
                            act.activation(sg[:, q, :], bank[q][:, :], ACT.Sigmoid).then_inc(gated, 1)
                    act.wait_ge(merged, c0 + (dc + 1))
                    act.activation(mg_hi[:, bass.ds(c0 + dc, 1), :], part[:, 0:1, :], ACT.Copy).then_inc(merged_hi, 1)
            for k in range(KC):
                split(S_OUT + k + 2)
            for t in range(TT):
                act.wait_ge(x2_ready, t + 1)
                last = act.activation(x2n[:, t, :], x_sb[:, t, :], ACT.Square, accum_out=ssum[:, t:t + 1])
            step(last)
            act.activation(std[:, 0:TT], ssum[:, 0:TT], ACT.Sqrt, scale=1.0 / D,
                           bias=eps[:, :]).then_inc(std_ready, 1)
            turn_high(2, 2 * KC)
            with act.Fori(0, 2 * PEER_H - 4 + 1, 4) as c0:
                for dc in range(4):
                    base = S_PQ + dc
                    act.wait_ge(chunk_used, base + 1 + c0)
                    split(base + 2, loop=c0)
                    act.activation(qs[:, dc % 2, :], bank[(R_PQ + dc) % 2][:, :], ACT.Copy).then_inc(proj_read, 1)

            def gelu(i0, di):
                base = S_U + di
                split(base + 2, loop=i0)
                act.wait_ge(chunk_used, base + 1 + i0)
                if not (isinstance(i0, int) and i0 + di < 2):
                    act.wait_ge(a_stored[di % 2], (i0 + (di - di % 2)) * 8)
                act.activation(abuf[:, di % 2, :], bank[(R_U + di) % 2][:, :],
                               ACT.Gelu_apprx_tanh).then_inc(proj_read, 1)

            for i in range(4):
                gelu(0, i)
            with act.Fori(4, I_PLAIN - 4 + 1, 4) as i0:
                for di in range(4):
                    gelu(i0, di)
            act.wait_ge(shifted, 1)
            act.activation(FV[:, :, :], FV[:, :, :], ACT.Exp).then_inc(exp_final, 1)
            per = STAGE_T // TOK_I
            act.sem_inc(gate_read, 2)

            def gates_out(i0, first=False):
                for half in range(2):
                    if not first:
                        act.wait_ge(g_stored[half], i0 * (8 // per))
                    for k in range(per):
                        di = half * per + k
                        gelu(i0 + I_PLAIN, di)
                        for b in range(2):
                            act.wait_ge(gate_mm, i0 * 2 + (2 * di + b + 1))
                            t0 = k * TOK_I + b * TOK_I // 2
                            act.activation(gstage[:, half, :, t0:t0 + TOK_I // 2].rearrange("p i t -> p t i"),
                                           bank[2 + b][:, :].rearrange("p (t i) -> p t i", i=NKEYS),
                                           ACT.Copy).then_inc(gate_read, 1)

            gates_out(0, first=True)
            with act.Fori(2 * per, NI - I_PLAIN - 2 * per + 1, 2 * per) as i0:
                gates_out(i0)

            def weigh_high(i0, di):
                act.wait_ge(weighted, i0 + (di + 1))
                act.activation(wT_hi[:, di % 2, :], wf[:, di % 2, :], ACT.Copy).then_inc(weighted_hi, 1)

            weigh_high(0, 0)
            with act.Fori(0, NI - 4 - 4 + 1, 4) as i0:
                for di in range(4):
                    weigh_high(i0, di + 1)
                    split(S_EV + di + 2, loop=i0)
            for i in range(NI - 4, NI - 1):
                weigh_high(0, i + 1)
                if i < NI - 2:
                    split(S_EV + i + 2)
            for t in range(TT):
                act.wait_ge(x3_ready, t + 1)
                step(act.activation(junk[:, :], x_sb[:, t, :], ACT.Square, accum_out=ssum[:, t:t + 1]))
                act.activation(std[:, t:t + 1], ssum[:, t:t + 1], ACT.Sqrt, scale=1.0 / D,
                               bias=eps[:, :]).then_inc(final_std, 1)

        @block.vector
        def _(dve):
            step = Steps(dve, dve_step)
            dve.memset(eps[:, :], EPS).then_inc(eps_set, 1)
            dve.memset(kdup[:, :, 0:WINDOW], 0.0)
            for buf in (ub, sA, sB):
                dve.memset(buf[:, 0:PAD], 0.0)
            dve.memset(vdup[:, :, 0, :], 0.0).then_inc(eps_set, 1)

            def normalise(dst, src, nt, col, ready):
                dve.wait_ge(std_ready, ready)
                step(dve.reciprocal(rstd[:, col:col + nt], std[:, col:col + nt]))
                for t in range(nt):
                    last = dve.tensor_scalar(dst[:, t, :], src[:, t, :], rstd[:, col + t:col + t + 1], None, ALU.mult)
                    if nt == TT or t == nt - 1:
                        last.then_inc(normed, 1)

            normalise(memn, mem_sb, MT, 0, 1)
            dve.wait_ge(small_loaded, 16 * SMALLS)
            two_pi = 2 * math.pi
            c1 = 6.28125
            c2 = float(np.float32(np.floor((two_pi - c1) * 2 ** 21) / 2 ** 21))
            c3 = float(np.float32(two_pi - c1 - c2))
            magic = 1.5 * 2 ** 23
            limit = 3.1415925
            posf, ang, turns = sg[:, 0, :], sg[:, 1, :], sg[:, 2, :]
            step(dve.tensor_copy(posf, pos_i[:, :]))
            step(dve.tensor_scalar(ang, posf, freq[:, 0:1], None, ALU.mult))
            for made, (dst, quarter) in enumerate(((sinT, 0.0), (cosT, 0.25))):
                step(dve.tensor_scalar(turns, ang, 1.0 / two_pi, quarter, ALU.mult, ALU.add))
                step(dve.tensor_scalar(turns, turns, magic, None, ALU.add))
                step(dve.tensor_scalar(turns, turns, -magic, None, ALU.add))
                step(dve.scalar_tensor_tensor(out=posf, in0=turns, scalar=-c1, in1=ang, op0=ALU.mult, op1=ALU.add))
                step(dve.scalar_tensor_tensor(out=dst[:, :], in0=turns, scalar=-c2, in1=posf, op0=ALU.mult, op1=ALU.add))
                step(dve.scalar_tensor_tensor(out=posf, in0=turns, scalar=-c3, in1=dst[:, :], op0=ALU.mult, op1=ALU.add))
                step(dve.tensor_scalar(turns, posf, quarter * two_pi, limit, ALU.add, ALU.min))
                dve.tensor_scalar(dst[:, :], turns, -limit, None, ALU.max).then_inc(angles, 1)
                dve.wait_ge(angles, made + 1)
            for k in range(KC):
                dve.wait_ge(turned_hi, k + 1)
                dve.scalar_tensor_tensor(out=memT_lo[:, k, :], in0=bank[k][:, 0:M],
                                         scalar=gains[:, 1, k:k + 1], in1=memT_hi[:, k, :].bitcast(f32),
                                         op0=ALU.mult, op1=ALU.subtract).then_inc(turned_lo, 1)
            normalise(xn, x_sb, TT, 2, 2)
            dve.wait_ge(consts, 2)
            for gi, w in enumerate(POOL_WINDOWS):
                last = dve.tensor_scalar(rcnt[:, gi, :], rcnt[:, gi, :], float(w), None, ALU.min)
            step(last)
            step(dve.reciprocal(rcnt[:, :, :], rcnt[:, :, :]))

            def turn_low(gain, base):
                for k in range(KC):
                    dve.wait_ge(turned_hi, base + k + 1)
                    dve.scalar_tensor_tensor(out=hT_lo[:, k, :], in0=bank[4 + k % 4][:, :],
                                             scalar=gains[:, gain, k:k + 1], in1=hT_hi[:, k, :].bitcast(f32),
                                             op0=ALU.mult, op1=ALU.subtract).then_inc(turned_lo, 1)

            turn_low(0, KC)
            dve.wait_ge(sines, 2)

            def rotate(j, rn, dst):
                dve.wait_ge(swapped, j + 1)
                dve.tensor_tensor(dst, bank[rn % 2][:, :], cosT[:, :], ALU.mult).then_inc(proj_read, 1)
                step(dve.tensor_tensor(swp[:, :], swp[:, :], sinT[:, :], ALU.mult))
                dve.tensor_tensor(dst, dst, swp[:, :], ALU.add).then_inc(rotated, 1)

            for j in range(2):
                rotate(j, R_K + j, kdup[:, j, WINDOW:])

            def window(gi):
                dve.wait_ge(chunk_used, S_POOL + gi + 1)
                if gi >= 1:
                    dve.wait_ge(pooled, gi)
                dve.tensor_copy(sA[:, PAD:], bank[(R_POOL + gi) % 2][:, :]).then_inc(proj_read, 1)
                dve.wait_ge(proj_read, R_POOL + gi + 1)
                if gi >= 1:
                    dve.wait_ge(mixed, gi)
                step(dve.tensor_scalar(ub[:, PAD:], sA[:, PAD:], -1.0, None, ALU.mult))
                src, dst = sA, sB
                for lv in range(gi + 1):
                    sh = 1 << lv
                    step(dve.tensor_tensor(dst[:, PAD:], src[:, PAD:], src[:, PAD - sh:PAD + T - sh], ALU.add))
                    src, dst = dst, src
                w = POOL_WINDOWS[gi]
                step(dve.tensor_tensor(dst[:, PAD:2 * PAD], src[:, PAD:2 * PAD], rcnt[:, gi, :], ALU.mult))
                step(dve.scalar_tensor_tensor(out=ub[:, 2 * PAD:], in0=src[:, 2 * PAD:], scalar=1.0 / w,
                                              in1=ub[:, 2 * PAD:], op0=ALU.mult, op1=ALU.add))
                dve.tensor_tensor(ub[:, PAD:2 * PAD], dst[:, PAD:2 * PAD], ub[:, PAD:2 * PAD],
                                  ALU.add).then_inc(pooled, 1)

            def mix_low(gi):
                dve.wait_ge(y_hi, gi + 1)
                dve.scalar_tensor_tensor(out=yT_lo[:, gi, :], in0=bank[2 + gi % 2][:, :],
                                         scalar=pscale[:, gi:gi + 1], in1=yT_hi[:, gi, :].bitcast(f32),
                                         op0=ALU.mult, op1=ALU.subtract).then_inc(y_lo, 1)
            for gi in range(4):
                window(gi)
                if gi >= 1:
                    mix_low(gi - 1)
            rotate(2, R_Q, qr[:, 0, :])
            mix_low(3)
            for u in range(8):
                pair = [b[:, :].rearrange("p (n h) -> p n h", h=2) for b in (mx, mcap, sdiff)]
                if u >= 1:
                    dve.wait_ge(probT_done, 4 * u)
                for b in range(4):
                    j, h = b // 2, b % 2
                    dve.wait_ge(scored, 4 * u + b + 1)
                    seen = mask[:, :, :] if j == 0 else mask[:, 1:2, :].broadcast_to([P, 2, 2 * WINDOW])
                    dve.tensor_tensor(prob[:, 2 * j:2 * j + 2, h, :],
                                      bank[2 + 2 * h + j][:, :].rearrange("p (n k) -> p n k", n=2), seen,
                                      ALU.add).then_inc(score_read, 1)
                    dve.wait_ge(score_read, 4 * u + b + 1)
                    last = dve.reduce_max(pair[0][:, 2 * j:2 * j + 2, h:h + 1], prob[:, 2 * j:2 * j + 2, h, :], AX.X)
                step(last)
                if u >= 1:
                    dve.wait_ge(expd, u)
                snk = sinks[:, 2 * u:2 * u + 2].unsqueeze(1).broadcast_to([P, TT, 2])
                step(dve.scalar_tensor_tensor(out=pair[1], in0=pair[0], scalar=HEAD ** -0.5, in1=snk,
                                              op0=ALU.mult, op1=ALU.max))
                dve.tensor_scalar(negm[:, :], mcap[:, :], -1.0, None, ALU.mult)
                dve.tensor_tensor(pair[2], snk, pair[1], ALU.subtract).then_inc(capped, 1)
                dve.wait_ge(expd, u + 1)
                step(dve.tensor_tensor(den[:, :], rsum[:, :], sexp[:, :], ALU.add))
                step(dve.reciprocal(rinv[:, :], den[:, :]))
                for n in range(TT):
                    for h in range(2):
                        last = dve.tensor_scalar(prob[:, n, h, :], prob[:, n, h, :],
                                                 rinv[:, 2 * n + h:2 * n + h + 1], None, ALU.mult)
                    last.then_inc(prob_ready, 1)
                if u < 7:
                    rotate(3 + u, R_Q + u + 1, qr[:, (u + 1) % 2, :])
                dve.wait_ge(y_hi, 4 + u + 1)
                for h in range(2):
                    rows = slice(h * HEAD, (h + 1) * HEAD)
                    last = dve.tensor_tensor(yT_lo[rows, 8 + u, :], bank[2 + h][rows, :],
                                             yT_hi[rows, 8 + u, :].bitcast(f32), ALU.subtract)
                last.then_inc(y_lo, 1)
            for u in range(4):
                for n in range(TT):
                    dve.wait_ge(scored, 32 + 4 * u + n + 1)
                    last = dve.reduce_max(mx[:, n:n + 1], bank[2 + n][:, 0:M], AX.X)
                step(last)
                dve.wait_ge(probT_done, 32 + 2 * u)
                dve.tensor_scalar(negm[:, 0:TT], mx[:, 0:TT], -(P ** -0.5), None, ALU.mult).then_inc(capped, 1)
                dve.wait_ge(score_read, 32 + 4 * (u + 1))
                step(dve.reciprocal(rinv[:, 0:TT], rsum[:, 0:TT]))
                for n in range(TT):
                    dve.tensor_scalar(prob[:, n, 0, :], prob[:, n, 0, :], rinv[:, n:n + 1], None,
                                      ALU.mult).then_inc(prob_ready, 1)
                dve.wait_ge(y_hi, 12 + u + 1)
                dve.tensor_tensor(yT_lo[:, 4 + u, :], bank[2][:, :], yT_hi[:, 4 + u, :].bitcast(f32),
                                  ALU.subtract).then_inc(y_lo, 1)
            dve.sem_inc(branch_read, 3)
            first_step, per_turn = step.value, 1
            with dve.Fori(0, KC) as c:
                step.value, step.made = c * per_turn + first_step, 0
                dve.wait_ge(gated, c * 3 + 6)
                dve.wait_ge(chunk_used, c * GATE_CHUNKS + (S_GATE + GATE_CHUNKS))
                for q, b in enumerate((3, 5, 4)):
                    dve.tensor_tensor(part[:, q, :], sg[:, q, :], bank[b][:, :], ALU.mult).then_inc(branch_read, 1)
                dve.wait_ge(branch_read, c * 3 + 6)
                step(dve.tensor_tensor(part[:, 1, :], part[:, 1, :], part[:, 2, :], ALU.add))
                dve.tensor_tensor(part[:, 0, :], part[:, 0, :], part[:, 1, :], ALU.add).then_inc(merged, 1)
                dve.wait_ge(merged_hi, c + 1)
                dve.tensor_tensor(mg_lo[:, bass.ds(c, 1), :], part[:, 0:1, :],
                                  mg_hi[:, bass.ds(c, 1), :].bitcast(f32), ALU.subtract).then_inc(merged_lo, 1)
                dve.wait_ge(merged_lo, c + 1)
                assert step.made == per_turn
            step.value = first_step + per_turn * KC
            dve.wait_ge(chunk_used, S_PQ)
            for t in range(TT):
                for half in range(2):
                    cols = slice(half * 512, (half + 1) * 512)
                    last = dve.tensor_tensor(x_sb[:, t, cols], x_sb[:, t, cols], bank[2 * t + half][:, :], ALU.add)
                last.then_inc(x2_ready, 1)
            normalise(x2n, x_sb, TT, 0, 3)
            turn_low(2, 2 * KC)
            dve.sem_inc(sub_read, 2)
            with dve.Fori(0, 2 * PEER_H - 2 + 1, 2) as c0:
                for dc in range(2):
                    dve.wait_ge(sub_done, c0 + (dc + 1))
                    dve.tensor_copy(sc[:, :, bass.ds(c0 + dc, 1), :],
                                    bank[2 + dc][:, :].rearrange("p (t a n) -> p t a n", t=TT, a=1)
                                    ).then_inc(sub_read, 1)
            dve.wait_ge(sub_read, 2 * PEER_H + 2)

            halves = [(h, q) for h in range(PEER_H) for q in range(2)]
            hrow = lambda buf, h: buf[:, h, :]
            s1 = lambda buf, h, q: buf[:, h, q * NKEYS:(q + 1) * NKEYS]
            all2 = "p h (a b) -> p h a b"

            def best(src, spare, vals, inds):
                for s_, v_ in zip(src, vals):
                    last = dve.max(v_[:, 0:8], s_)
                dve.drain()
                for s_, z_, v_, i_ in zip(src, spare, vals, inds):
                    dve.max_index(i_[:, 0:8], v_[:, 0:8], s_)
                    last = dve.match_replace(z_, v_[:, 0:8], s_, BELOW)
                dve.drain()
                for z_, v_ in zip(spare, vals):
                    last = dve.max(v_[:, 8:16], z_)
                dve.drain()
                for z_, v_, i_ in zip(spare, vals, inds):
                    last = dve.max_index(i_[:, 8:16], v_[:, 8:16], z_)
                dve.drain()

            with dve.Fori(0, TT) as t:
                scur4 = scur[:, :, :].rearrange("p h (q n) -> p (h q) n", q=2)
                dve.tensor_copy(scur4.unsqueeze(1), sc[:, bass.ds(t, 1), :, :])
                dve.drain()
                best([s1(scur, h, q) for h, q in halves], [s1(scur2, h, q) for h, q in halves],
                     [top[:, h, q, :] for h, q in halves], [topi[:, h, q, :] for h, q in halves])
                dve.tensor_copy(topf[:, :, :, :], topi[:, :, :, :])
                grid = [P, PEER_H, TOPK, TOPK]
                dve.tensor_tensor(cand[:, :, :].rearrange(all2, a=TOPK),
                                  top[:, :, 0, :].unsqueeze(3).broadcast_to(grid),
                                  top[:, :, 1, :].unsqueeze(2).broadcast_to(grid), ALU.add)
                dve.drain()
                best([hrow(cand, h) for h in range(PEER_H)], [hrow(cand2, h) for h in range(PEER_H)],
                     [hrow(fin, h) for h in range(PEER_H)],
                     [fpos[:, h * TOPK:(h + 1) * TOPK] for h in range(PEER_H)])
                dve.tensor_tensor(FV[:, bass.ds(t, 1), :].rearrange("p a (h k) -> p (a h) k", h=PEER_H), fin[:, :, :],
                                  fin[:, :, 0:1].broadcast_to([P, PEER_H, TOPK]), ALU.subtract)
                for q, dst in ((0, IF), (1, JF)):
                    if q == 0:
                        dve.tensor_scalar(fsel[:, :], fpos[:, :], 4, None, ALU.logical_shift_right)
                        dve.drain()
                    else:
                        dve.tensor_scalar(fsel[:, :], fpos[:, :], TOPK - 1, None, ALU.bitwise_and)
                        dve.drain()
                    dve.tensor_copy(fself[:, :], fsel[:, :])
                    dve.drain()
                    flat = [P, HK, TOPK]
                    pick = cand[:, :, :].rearrange("p h (k a) -> p (h k) a", a=TOPK)
                    dve.tensor_tensor(pick, fself[:, :].unsqueeze(2).broadcast_to(flat),
                                      iota_k[:, :].unsqueeze(1).broadcast_to(flat), ALU.is_equal)
                    dve.drain()
                    pick4 = cand[:, :, :].rearrange(all2, a=TOPK)
                    dve.tensor_tensor(pick4, pick4, topf[:, :, q, :].unsqueeze(2).broadcast_to(grid), ALU.mult)
                    dve.drain()
                    dve.tensor_reduce(dst[:, bass.ds(t, 1), :].rearrange("p a n -> p (a n)"), pick,
                                      AX.X, ALU.add)
                    dve.drain()
            dve.drain().then_inc(shifted, 1)
            dve.wait_ge(exp_final, 1)
            rows3 = FV[:, :, :].rearrange("p t (h k) -> p (t h) k", k=TOPK)
            step(dve.reduce_sum(gsm[:, :], rows3, AX.X))
            step(dve.reciprocal(gsm[:, :], gsm[:, :]))
            dve.tensor_tensor(rows3, rows3, gsm[:, :].unsqueeze(2).broadcast_to([P, TT * PEER_H, TOPK]),
                              ALU.mult).then_inc(retrieved, 1)
            dve.wait_ge(spread, 3)
            dve.tensor_copy(IT[:, :], bank[2][:, :])
            dve.tensor_copy(JT[:, :], bank[3][:, :])
            dve.tensor_copy(GT[:, :], bank[4][:, :]).then_inc(spread_read, 1)
            dve.wait_ge(spread_read, 1)
            step(dve.tensor_copy(gbf[:, :], GT[:, :]))
            step(dve.tensor_tensor(R1[:, :], GT[:, :], gbf[:, :], ALU.subtract))
            step(dve.tensor_copy(gbf[:, :], R1[:, :]))
            step(dve.tensor_tensor(R2[:, :], R1[:, :], gbf[:, :], ALU.subtract))

            def one_hots(i0, di, first=False):
                for b in range(2):
                    if not first:
                        dve.wait_ge(gate_mm, i0 * 2 + (2 * di + b - 3))
                    for tk in range(TOK_I // 2):
                        at = b * (TOK_I // 2) + tk
                        col = bass.ds(i0 * TOK_I + (di * TOK_I + at), 1)
                        dve.tensor_scalar(ohJ[:, di, at, :], iota_b[:, :], JT[:, col], None, ALU.is_equal)
                        for q, gate in enumerate((GT, R1, R2)):
                            last = dve.tensor_scalar(ohI[:, di, at, q, :], iota_b[:, :], IT[:, col], gate[:, col],
                                                     ALU.is_equal, ALU.mult)
                    last.then_inc(hot_ready, 1)

            for di in range(2):
                one_hots(0, di, first=True)
            with dve.Fori(2, NI - I_PLAIN - 2 + 1, 2) as i0:
                for di in range(2):
                    one_hots(i0, di)

            def weigh(i0, di, first=False):
                dve.wait_ge(ag_loaded[di], i0 * 8 + 32)
                if not first:
                    dve.wait_ge(chunk_used, i0 + (S_EV + di - 1))
                dve.tensor_tensor(wf[:, di % 2, :], a_in[:, di, :], g_in[:, di, :], ALU.mult).then_inc(weighted, 1)
                dve.wait_ge(weighted_hi, i0 + (di + 1))
                dve.tensor_tensor(wT_lo[:, di % 2, :], wf[:, di % 2, :], wT_hi[:, di % 2, :].bitcast(f32),
                                  ALU.subtract).then_inc(weighted_lo, 1)

            for i in range(4):
                weigh(0, i, first=(i < 2))
            with dve.Fori(4, NI - 4 + 1, 4) as i0:
                for di in range(4):
                    weigh(i0, di)
            dve.wait_ge(chunk_used, CHUNKS)
            dve.wait_ge(gfin_loaded, 16)
            for t in range(TT):
                for half in range(2):
                    cols = slice(half * 512, (half + 1) * 512)
                    last = dve.tensor_tensor(x_sb[:, t, cols], x_sb[:, t, cols], bank[2 * t + half][:, :], ALU.add)
                last.then_inc(x3_ready, 1)
            for t in range(TT):
                dve.wait_ge(final_std, t + 1)
                step(dve.reciprocal(rstd[:, t:t + 1], std[:, t:t + 1]))
                dve.scalar_tensor_tensor(out=x_sb[:, t, :], in0=x_sb[:, t, :], scalar=rstd[:, t:t + 1],
                                         in1=gfin[:, :], op0=ALU.mult, op1=ALU.mult).then_inc(final_ready, 1)


def layout(inputs):
    f = lambda n: np.ascontiguousarray(inputs[n])
    w_in, w_kv = f("w_in")[0], f("w_mem_kv")[0]
    pool_w, swa_w, kv_w = 4 * P, D, 2 * HEAD
    q0 = pool_w
    k0 = q0 + swa_w
    v0 = k0 + kv_w
    m0 = v0 + kv_w
    g0 = m0 + 4 * P

    def cols(w, idx):
        w = w[:, idx]
        return w.reshape(-1, P, P).transpose(1, 0, 2).reshape(P, -1)

    chunks = [cols(w_kv, slice(h * P, (h + 1) * P)) for h in range(4)]
    vals = w_kv[:, 4 * P:].reshape(KC, P, T)
    chunks += [vals[2 * q:2 * q + 2].transpose(1, 0, 2).reshape(P, D) for q in range(4)]
    for kv in range(2):
        one = list(range(k0 + kv * HEAD, k0 + (kv + 1) * HEAD))
        chunks.append(cols(w_in, one + one))
    chunks.append(cols(w_in, slice(v0, v0 + P)))
    chunks += [cols(w_in, slice(gi * P, (gi + 1) * P)) for gi in range(4)]
    chunks += [cols(w_in, slice(q0 + c * P, q0 + (c + 1) * P)) for c in Q_ORDER]
    chunks += [cols(w_in, slice(m0 + h * P, m0 + (h + 1) * P)) for h in range(4)]
    pm = np.concatenate([f("w_branch_pool")[0], f("w_branch_mem")[0]], axis=0)
    sw = f("w_branch_swa")[0].reshape(8, P, D)[Q_ORDER].reshape(D, D)
    for c in range(KC):
        for b in range(3):
            chunks.append(cols(w_in, slice(g0 + b * D + c * P, g0 + b * D + (c + 1) * P)))
        chunks.append(cols(pm, slice(c * P, (c + 1) * P)))
        chunks.append(cols(sw, slice(c * P, (c + 1) * P)))
    chunks += list(f("w_out")[0].reshape(KC, P, D))
    chunks += [cols(f("peer_w_q")[0], slice(c * P, (c + 1) * P)) for c in range(2 * PEER_H)]
    u = f("peer_u")[0].reshape(NI, P, KC, P).transpose(0, 3, 2, 1).reshape(NI, P, D)
    stream = np.concatenate([np.stack(chunks), u, f("peer_v")[0].reshape(NI, P, D)], axis=0)
    assert stream.shape == (CHUNKS, P, D)
    half = HEAD // 2
    inv = (10000.0 ** (-np.arange(half, dtype=np.float64) / half)).astype(np.float32)
    sign = np.where(np.arange(P) % HEAD < half, -1.0, 1.0).astype(np.float32)
    freq = np.stack([inv[np.arange(P) % half], sign], axis=1)
    gains = np.stack([f(n)[0].reshape(KC, P).T for n in ("norm1_g", "mem_norm_g", "norm2_g")], axis=1)
    return {
        "stream": stream,
        "x": f("x")[0], "mem": f("mem")[0], "positions": f("positions"),
        "gains": gains, "pscale": f("pool_scale")[0].reshape(4, P).T,
        "wpool": f("w_pool")[0].transpose(1, 0, 2),
        "sinks": f("attn_sinks").reshape(8, 2)[Q_ORDER].reshape(1, 16),
        "freq": freq,
        "subkeys": f("peer_sub_keys")[0].reshape(2 * PEER_H, NKEYS, P).transpose(2, 0, 1),
        "gfin": f("final_norm_g").reshape(1, D),
    }


def kernel(**inputs):
    import concourse.bacc as _bacc
    from concourse.bass_utils import run_bass_kernel_spmd as _run

    nc = _bacc.Bacc("TRN2", target_bir_lowering=False, num_devices=1)
    arrays, dram = {}, {}
    for name, a in layout(inputs).items():
        arrays[name] = np.ascontiguousarray(a)
        dram[name] = nc.dram_tensor(name, arrays[name].shape, mybir.dt.from_np(arrays[name].dtype),
                                    kind="ExternalInput").ap()
    for name in ("a", "g"):
        dram[name] = nc.dram_tensor(name + "_rows", (NI, P, T), mybir.dt.float32, kind="Internal").ap()
    out = nc.dram_tensor("out", (T, D), mybir.dt.float32, kind="ExternalOutput").ap()
    build(nc, dram, out)
    r = _run(nc, [arrays], core_ids=[0])
    return r.results[0]["out"].reshape(1, T, D)
```

```python
import math
from contextlib import ExitStack

import concourse.bass as bass
import numpy as np
from concourse import mybir

T, D, P = 512, 1024, 128
TT, KC = T // P, D // P
M = 256
MT = M // P
HEAD, WINDOW = 64, 128
POOL_WINDOWS = (2, 4, 8, 16)
PAD = max(POOL_WINDOWS)
PEER_H, TOPK, NKEYS = 8, 16, 128
HK = PEER_H * TOPK
NEXP = NKEYS * NKEYS
NI = NEXP // P
NEG = -1e30
BELOW = -3.0e38
EPS = 1e-6

S_KM, S_VM, S_K, S_V, S_POOL = 0, 4, 8, 10, 11
S_Q, S_QM, S_GATE = 15, 23, 27
GATE_CHUNKS = 5
S_OUT = S_GATE + GATE_CHUNKS * KC
S_PQ = S_OUT + KC
S_U = S_PQ + 2 * PEER_H
S_EV = S_U + NI
CHUNKS = S_EV + NI
RAW = 4
Q_ORDER = [q // 2 + 4 * (q % 2) for q in range(8)]
R_KM, R_K, R_POOL, R_Q, R_QM, R_PQ, R_U = 0, 4, 6, 10, 18, 22, 38

I_PLAIN, I_GATES = 56, 64
I_TAIL = NI - I_PLAIN - I_GATES
TOK_I = T // I_GATES
STAGE_T = 64
BLOCKS = T // STAGE_T
PER = STAGE_T // TOK_I
GROUP = 8
SMALLS = 7
AHEAD = 6


def build(nc, dram, out):
    f32, f32r, bf16, u32, i32 = (mybir.dt.float32, mybir.dt.float32r, mybir.dt.bfloat16,
                                 mybir.dt.uint32, mybir.dt.int32)
    ACT, ALU, AX = mybir.ActivationFunctionType, mybir.AluOpType, mybir.AxisListType

    with ExitStack() as ctx:
        arena_size = 212800
        arena = ctx.enter_context(nc.sbuf_tensor("arena", [P, arena_size], mybir.dt.uint8))
        arena_at = int(nc.sbuf_base) - arena_size
        assert arena_at % 32 == 0

        class Place:
            def __init__(self, at):
                self.at = at

            def __call__(self, name, shape, dt=f32):
                t = nc.alloc_sbuf_tensor_at(name, [P] + list(shape), dt, offset=arena_at + self.at)
                size = int(np.prod(shape)) * (2 if dt == bf16 else 4)
                self.at += (size + 31) // 32 * 32
                assert self.at <= arena_size, (name, self.at)
                return t

        keep = Place(0)
        x_sb = keep("x_sb", [TT, D])
        hT_hi = keep("hT_hi", [KC, T], f32r)
        hT_lo = keep("hT_lo", [KC, T], f32r)
        raw = keep("raw", [RAW, D])
        w_hi = keep("w_hi", [2, D], f32r)
        w_lo = keep("w_lo", [2, D], f32r)
        subkeys = keep("subkeys", [2 * PEER_H, NKEYS])
        ident = keep("ident", [P])
        gains = keep("gains", [3, KC])
        pscale = keep("pscale", [4])
        sinks = keep("sinks", [16])
        freq = keep("freq", [2])
        iota_b = keep("iota_b", [NKEYS], bf16)
        iota_k = keep("iota_k", [TOPK])
        eps = keep("eps", [1])
        ssum = keep("ssum", [8])
        std = keep("std", [8])
        rstd = keep("rstd", [8])
        mx = keep("mx", [8])
        mcap = keep("mcap", [8])
        negm = keep("negm", [8])
        sdiff = keep("sdiff", [8])
        sexp = keep("sexp", [8])
        rsum = keep("rsum", [8])
        den = keep("den", [8])
        rinv = keep("rinv", [8])
        front = keep.at

        y = Place(front)
        yT_hi = y("yT_hi", [16, T], f32r)
        yT_lo = y("yT_lo", [16, T], f32r)
        s = Place(front)
        mem_sb = s("mem_sb", [MT, D])
        memn = s("memn", [MT, D])
        memT_hi = s("memT_hi", [KC, M], f32r)
        memT_lo = s("memT_lo", [KC, M], f32r)
        xn = s("xn", [TT, D])
        assert s.at <= y.at
        a = Place(y.at)
        cosT = a("cosT", [T])
        sinT = a("sinT", [T])
        mask = a("mask", [2, 2 * WINDOW])
        kdup = a("kdup", [2, WINDOW + T])
        vz = a("vz", [2, TT + 1, 3 * HEAD])
        kmT = a("kmT", [4, M])
        vm = a("vm", [MT, T])
        pos_i = Place(a.at)("pos_i", [T], i32)
        qr = a("qr", [2, T])
        swp = a("swp", [T])
        prob0 = a("prob0", [TT, 2, 2 * WINDOW])
        probT = a("probT", [2, T])
        g = Place(y.at)
        mg_hi = g("mg_hi", [KC, T], f32r)
        mg_lo = g("mg_lo", [KC, T], f32r)
        sg = g("sg", [3, T])
        part = g("part", [3, T])
        p = Place(max(a.at, g.at))
        ub = p("ub", [PAD + T])
        sA = p("sA", [PAD + T])
        sB = p("sB", [PAD + T])
        rcnt = p("rcnt", [4, PAD])
        wpool = p("wpool", [4, P])
        prob1 = Place(max(a.at, g.at))("prob1", [TT, 2, 2 * WINDOW])
        assert TT * 2 * 2 * WINDOW * 4 <= p.at - max(a.at, g.at)
        prob = (prob0, prob1)

        r = Place(front)
        abuf = r("abuf", [2, T])
        IF = r("IF", [TT, HK])
        JF = r("JF", [TT, HK])
        FV = r("FV", [TT, HK])
        IT = r("IT", [T])
        JT = r("JT", [T])
        GT = r("GT", [T])
        R1 = r("R1", [T])
        R2 = r("R2", [T])
        gsm = r("gsm", [TT * PEER_H])
        gbf = r("gbf", [T], bf16)
        ohJ = r("ohJ", [2, TOK_I, NKEYS], bf16)
        ohI = r("ohI", [2, TOK_I, 3, NKEYS], bf16)
        late = r.at
        sc = r("sc", [TT, 2 * PEER_H, NKEYS])
        cand = r("cand", [PEER_H, TOPK * TOPK])
        cand2 = r("cand2", [PEER_H, TOPK * TOPK])
        top = r("top", [PEER_H, 2, TOPK])
        topi = r("topi", [PEER_H, 2, TOPK], u32)
        topf = r("topf", [PEER_H, 2, TOPK])
        fin = r("fin", [PEER_H, TOPK])
        fpos = r("fpos", [HK], u32)
        fsel = r("fsel", [HK], u32)
        fself = r("fself", [HK])
        scur = cand
        scur2 = cand2
        qs = r("qs", [2, T])
        x2n = Place(late)("x2n", [TT, D])
        gstage = Place(late)("gstage", [2, NKEYS, STAGE_T])
        v = Place(late)
        a_in = v("a_in", [4, T])
        g_in = v("g_in", [2, BLOCKS, GROUP, STAGE_T])
        wf = v("wf", [2, T])
        wT_hi = v("wT_hi", [2, T], f32r)
        wT_lo = v("wT_lo", [2, T], f32r)
        gfin = v("gfin", [D])
        junk = v("junk", [D])

        bank = [ctx.enter_context(nc.psum_tensor(f"bank{b}", [P, 512], f32)) for b in range(8)]

        def sem(name):
            return ctx.enter_context(nc.semaphore(name))

        raw_loaded = [sem(f"raw_loaded{i}") for i in range(RAW)]
        hi_ready, lo_ready, chunk_used = sem("hi_ready"), sem("lo_ready"), sem("chunk_used")
        proj_read = sem("proj_read")
        mem_loaded, x_loaded, small_loaded = sem("mem_loaded"), sem("x_loaded"), sem("small_loaded")
        consts = sem("consts")
        pool_step, dve_step, act_step = sem("pool_step"), sem("dve_step"), sem("act_step")
        eps_set = sem("eps_set")
        std_ready = sem("std_ready")
        normed = sem("normed")
        turned = sem("turned")
        turned_hi, turned_lo = sem("turned_hi"), sem("turned_lo")
        vm_read = sem("vm_read")
        angles, sines = sem("angles"), sem("sines")
        swapped, rotated = sem("swapped"), sem("rotated")
        v_ready = sem("v_ready")
        pooled, mixed = sem("pooled"), sem("mixed")
        y_hi, y_lo = sem("y_hi"), sem("y_lo")
        scored, score_read, capped = sem("scored"), sem("score_read"), sem("capped")
        expd, prob_ready = sem("expd"), sem("prob_ready")
        probT_done, probT_read = sem("probT_done"), sem("probT_read")
        attended = sem("attended")
        gated, branch_read = sem("gated"), sem("branch_read")
        merged, merged_hi, merged_lo = sem("merged"), sem("merged_hi"), sem("merged_lo")
        x2_ready = sem("x2_ready")
        sub_done, sub_read = sem("sub_done"), sem("sub_read")
        shifted, exp_final, retrieved = sem("shifted"), sem("exp_final"), sem("retrieved")
        spread, spread_read = sem("spread"), sem("spread_read")
        hot_ready, gate_mm, gate_read = sem("hot_ready"), sem("gate_mm"), sem("gate_read")
        a_stored = [sem("a_stored0"), sem("a_stored1")]
        g_stored = [sem("g_stored0"), sem("g_stored1")]
        a_loaded = [sem(f"a_loaded{i}") for i in range(4)]
        g_loaded = [sem(f"g_loaded{i}") for i in range(2)]
        summed = sem("summed")
        gfin_loaded = sem("gfin_loaded")
        weighted, weighted_hi, weighted_lo = sem("weighted"), sem("weighted_hi"), sem("weighted_lo")
        x3_ready, final_std, final_ready, out_stored = (sem("x3_ready"), sem("final_std"),
                                                        sem("final_ready"), sem("out_stored"))

        block = ctx.enter_context(nc.Block())

        class Steps:
            def __init__(self, eng, own):
                self.eng, self.own, self.value, self.made = eng, own, 0, 0

            def __call__(self, ins):
                ins.then_inc(self.own, 1)
                self.value, self.made = self.value + 1, self.made + 1
                self.eng.wait_ge(self.own, self.value)

        @block.sync
        def _(sp):
            stream = dram["stream"]
            a_rows = dram["a"]
            g_rows = dram["g"]

            def load(n, slot, fresh=False):
                if not fresh:
                    sp.wait_ge(lo_ready, n - RAW + 1)
                sp.dma_start(raw[:, slot, :], stream[bass.ds(n, 1), :, :].rearrange("n p c -> p (n c)")
                             ).then_inc(raw_loaded[slot], 16)

            for n in range(RAW):
                load(n, n, fresh=True)
            first_u = S_U + AHEAD
            with sp.Fori(RAW, first_u // RAW * RAW - RAW + 1, RAW) as n0:
                for k in range(RAW):
                    load(n0 + k, k)
            for n in range(first_u // RAW * RAW, first_u):
                load(n, n % RAW)

            def store_a(i, parity):
                sp.wait_ge(proj_read, i + (R_U + 1))
                sp.dma_start(a_rows[bass.ds(i, 1), :, :].rearrange("n p c -> p (n c)"),
                             abuf[:, parity, :]).then_inc(a_stored[parity], 16)

            def store_g(block, half, piece):
                q = NI // GROUP // 4
                rows = slice(piece * q * GROUP, (piece + 1) * q * GROUP)
                sp.dma_start(g_rows[piece * q:(piece + 1) * q, :, bass.ds(block, 1), :].rearrange(
                                 "g j b c -> j g (b c)"),
                             gstage[:, half, rows, :].rearrange("j (g i) t -> j g (i t)", i=GROUP)
                             ).then_inc(g_stored[half], 16)

            with sp.Fori(0, I_PLAIN - RAW + 1, RAW) as i0:
                for k in range(RAW):
                    load(i0 + (first_u + k), (first_u + k) % RAW)
                    store_a(i0 + k, k % 2)

            def gate_block(b0, half, first=False):
                for k in range(PER):
                    at = I_PLAIN + half * PER + k
                    load(b0 * PER + (first_u + at), (first_u + at) % RAW)
                    store_a(b0 * PER + at, at % 2)
                    if not first:
                        if k == 0:
                            sp.wait_ge(gate_read, b0 * (2 * PER) + (half * 2 * PER + 2))
                        if k < 4:
                            store_g(b0 + (half - 1), 1 - half, k)

            gate_block(0, 0, first=True)
            gate_block(0, 1)
            with sp.Fori(2, BLOCKS - 1, 2) as b0:
                for half in range(2):
                    gate_block(b0, half)

            def reload_a(i, slot, fresh=False):
                if not fresh:
                    sp.wait_ge(weighted, i - 3)
                sp.dma_start(a_in[:, slot, :], a_rows[bass.ds(i, 1), :, :].rearrange("n p c -> p (n c)")
                             ).then_inc(a_loaded[slot], 16)

            def reload_g(group, slot, done=None):
                if done is not None:
                    sp.wait_ge(weighted, done)
                sp.dma_start(g_in[:, slot, :, :, :].rearrange("j b i t -> j (b i t)"),
                             g_rows[bass.ds(group, 1), :, :, :].rearrange("g j b c -> j (g b c)")
                             ).then_inc(g_loaded[slot], 16)

            for k in range(I_TAIL):
                at = I_PLAIN + I_GATES + k
                load(first_u + at, (first_u + at) % RAW)
                store_a(at, at % 2)
                if k == 0:
                    sp.wait_ge(gate_read, BLOCKS * 2 * PER + 2)
                if k < 4:
                    store_g(BLOCKS - 1, 1, k)
                if k == 6:
                    for half in range(2):
                        sp.wait_ge(g_stored[half], 16 * 4 * BLOCKS // 2)
                    reload_g(0, 0)
                    for i in range(4):
                        if i < 2:
                            sp.wait_ge(a_stored[i], 32)
                        reload_a(i, i, fresh=True)
            for parity in range(2):
                sp.wait_ge(a_stored[parity], 16 * NI // 2)
            sp.dma_start(gfin[:, :], dram["gfin"].broadcast_to([P, D])).then_inc(gfin_loaded, 16)
            nxt = first_u + NI
            left = CHUNKS - nxt

            def value_step(i0, k, more=True, again=True):
                if more:
                    load(i0 + (nxt + k), (nxt + k) % RAW)
                if again:
                    reload_a(i0 + (k + 4), k % 4)

            for k in range(16):
                if k == 0:
                    reload_g(1, 1)
                if k == 8:
                    reload_g(2, 0, done=8)
                value_step(0, k)
            with sp.Fori(1, NI // 16 - 1) as b0:
                for k in range(16):
                    if k % 8 == 0:
                        reload_g(b0 * 2 + (k // 8 + 1), (k // 8 + 1) % 2, done=b0 * 16 + k)
                    value_step(b0 * 16, k)
            for k in range(16):
                i = NI - 16 + k
                if k == 0:
                    reload_g(NI // GROUP - 1, 1, done=i)
                value_step(NI - 16, k, more=i < left, again=i + 4 < NI)

            for t in range(TT):
                sp.wait_ge(final_ready, t + 1)
                sp.dma_start(out[t * P:(t + 1) * P, :], x_sb[:, t, :]).then_inc(out_stored, 16)
            sp.wait_ge(out_stored, 16 * TT)

        @block.gpsimd
        def _(pool):
            step = Steps(pool, pool_step)
            step(pool.memset(ident[:, :], 0.0))
            pool.affine_select(out=ident[:, :], in_=ident[:, :], compare_op=ALU.not_equal, fill=1.0,
                               base=0, pattern=[[-1, P]], channel_multiplier=1).then_inc(consts, 1)
            step(pool.memset(mask[:, :, :], 0.0))
            for f in range(2):
                step(pool.affine_select(out=mask[:, f, :], in_=mask[:, f, :], compare_op=ALU.is_ge, fill=NEG,
                                        base=WINDOW, pattern=[[-1, 2 * WINDOW]], channel_multiplier=1))
                step(pool.affine_select(out=mask[:, f, :], in_=mask[:, f, :], compare_op=ALU.is_ge, fill=NEG,
                                        base=-1, pattern=[[1, 2 * WINDOW]], channel_multiplier=-1))
            step(pool.affine_select(out=mask[:, 0, :], in_=mask[:, 0, :], compare_op=ALU.is_ge, fill=NEG,
                                    base=-WINDOW, pattern=[[1, 2 * WINDOW]], channel_multiplier=0))
            pool.iota(iota_b[:, :], pattern=[[1, NKEYS]], base=0, channel_multiplier=0,
                      allow_small_or_imprecise_dtypes=True)
            pool.iota(iota_k[:, :], pattern=[[1, TOPK]], base=0, channel_multiplier=0,
                      allow_small_or_imprecise_dtypes=True)
            pool.iota(rcnt[:, :, :], pattern=[[0, 4], [1, PAD]], base=1, channel_multiplier=0,
                      allow_small_or_imprecise_dtypes=True).then_inc(consts, 1)

            def low(n, k):
                pool.wait_ge(hi_ready, n + 1)
                pool.tensor_tensor(w_lo[:, k % 2, :], raw[:, k % RAW, :], w_hi[:, k % 2, :].bitcast(f32),
                                   ALU.subtract).then_inc(lo_ready, 1)

            with pool.Fori(0, CHUNKS // RAW * RAW - RAW + 1, RAW) as n0:
                for k in range(RAW):
                    low(n0 + k, k)
            for n in range(CHUNKS // RAW * RAW, CHUNKS):
                low(n, n)

        @block.tensor
        def _(pe):
            passes = ((w_hi, 0), (w_hi, 1), (w_lo, 0))

            def chunk(n):
                pe.wait_ge(lo_ready, n + 1)

            def product(dst, slot, rhs, k0=0, k1=KC, r0=0, used=True):
                for k in range(k0, k1):
                    for wi, (w, low) in enumerate(passes):
                        last = pe.matmul(dst, w[:, slot, k * P:(k + 1) * P], rhs[low][:, r0 + k - k0, :],
                                         start=(k == k0 and wi == 0), stop=(k == k1 - 1 and wi == 2))
                if used:
                    last.then_inc(chunk_used, 1)
                return last

            hT = (hT_hi, hT_lo)
            memT = (memT_hi, memT_lo)
            yT = (yT_hi, yT_lo)

            def project(n, rn, rhs, cols=T, strict=False):
                chunk(n)
                if strict:
                    pe.wait_ge(proj_read, rn)
                elif rn >= 2:
                    pe.wait_ge(proj_read, rn - 1)
                product(bank[0 if strict else rn % 2][:, 0:cols], n % 2, rhs)

            pe.wait_ge(consts, 1)
            pe.wait_ge(normed, 1)
            for k in range(KC):
                for t in range(MT):
                    last = pe.transpose(bank[k][:, t * P:(t + 1) * P],
                                        memn[:, t, k * P:(k + 1) * P], ident[:, :])
                last.then_inc(turned, 1)
            pe.wait_ge(turned_lo, KC)
            for h in range(4):
                project(S_KM + h, R_KM + h, memT, cols=M)
            for q in range(4):
                chunk(S_VM + q)
                for k in range(2):
                    for m in range(MT):
                        for low_m, w in ((0, w_hi), (0, w_lo), (1, w_hi)):
                            last = pe.matmul(bank[2 + m][:, :], memT[low_m][:, 2 * q + k, m * P:(m + 1) * P],
                                             w[:, q % 2, k * T:(k + 1) * T],
                                             start=(q == 0 and k == 0 and low_m == 0 and w is w_hi),
                                             stop=(q == 3 and k == 1 and low_m == 1))
                last.then_inc(chunk_used, 1)

            def turn(src, tok_ready, first, base):
                for k in range(KC):
                    if k >= 4 or not first:
                        pe.wait_ge(turned_lo, base + max(k - 3, 0))
                    for t in range(TT):
                        if k == 0:
                            pe.wait_ge(normed, tok_ready + t)
                        last = pe.transpose(bank[4 + k % 4][:, t * P:(t + 1) * P],
                                            src[:, t, k * P:(k + 1) * P], ident[:, :])
                    last.then_inc(turned, 1)

            turn(xn, 2, True, KC)
            pe.wait_ge(turned_lo, 2 * KC)
            for j in range(2):
                project(S_K + j, R_K + j, hT)
            chunk(S_V)
            for t in range(TT):
                for k in range(KC):
                    for low_h, w in ((0, w_hi), (0, w_lo), (1, w_hi)):
                        last = pe.matmul(bank[4][:, t * P:(t + 1) * P], hT[low_h][:, k, t * P:(t + 1) * P],
                                         w[:, S_V % 2, k * P:(k + 1) * P],
                                         start=(k == 0 and low_h == 0 and w is w_hi), stop=(k == KC - 1 and low_h == 1))
            last.then_inc(chunk_used, 1)

            def mix(gi):
                pe.wait_ge(pooled, gi + 1)
                if gi >= 2:
                    pe.wait_ge(y_lo, gi - 1)
                if gi < 2:
                    pe.wait_ge(vm_read, 1)
                pe.matmul(bank[2 + gi % 2][:, :], wpool[:, gi, :], ub[:, PAD:], start=True,
                          stop=True).then_inc(mixed, 1)

            for gi in range(4):
                project(S_POOL + gi, R_POOL + gi, hT)
                if gi >= 1:
                    mix(gi - 1)
            project(S_Q, R_Q, hT, strict=True)
            mix(3)
            project(S_Q + 1, R_Q + 1, hT, strict=True)

            def window_values(u):
                kv = u % 2
                for n in range(TT + 1):
                    if n < TT:
                        pe.wait_ge(prob_ready, 4 * u + n + 1)
                        if 4 * u + n >= 2:
                            pe.wait_ge(probT_read, 4 * u + n - 1)
                        for h in range(2):
                            for half in range(2):
                                last = pe.transpose(bank[6 + n % 2][:, (2 * h + half) * P:(2 * h + half + 1) * P],
                                                    prob[u % 2][:, n, h, half * P:(half + 1) * P], ident[:, :])
                        last.then_inc(probT_done, 1)
                    if n == 0 and u >= 1:
                        pe.wait_ge(y_lo, 4 + u)
                    if n >= 1:
                        pe.wait_ge(probT_read, 4 * u + n)
                        for h in range(2):
                            for half in range(2):
                                last = pe.matmul(bank[1][:, (n - 1) * P:n * P],
                                                 vz[:, kv, n - 1 + half, HEAD * (1 - h):HEAD * (3 - h)],
                                                 probT[:, (n - 1) % 2, (2 * h + half) * P:(2 * h + half + 1) * P],
                                                 start=(h == 0 and half == 0), stop=(h == 1 and half == 1))
                last.then_inc(attended, 1)

            def memory_values(u):
                for j in range(2):
                    pe.wait_ge(prob_ready, 32 + 4 * u + 2 * j + 2)
                    pe.wait_ge(probT_read, 32 + 2 * u + j - 1)
                    for n in (2 * j, 2 * j + 1):
                        for half in range(2):
                            last = pe.transpose(bank[6 + j][:, (n % 2 * 2 + half) * P:(n % 2 * 2 + half + 1) * P],
                                                prob[u % 2][:, n, 0, half * P:(half + 1) * P], ident[:, :])
                    last.then_inc(probT_done, 1)
                pe.wait_ge(y_lo, 12 + u)
                for j in range(2):
                    pe.wait_ge(probT_read, 32 + 2 * u + j + 1)
                    for n in (2 * j, 2 * j + 1):
                        for half in range(2):
                            last = pe.matmul(bank[1][:, n * P:(n + 1) * P], vm[:, half, u * P:(u + 1) * P],
                                             probT[:, j, (n % 2 * 2 + half) * P:(n % 2 * 2 + half + 1) * P],
                                             start=(half == 0), stop=(half == 1))
                last.then_inc(attended, 1)

            pe.wait_ge(y_lo, 4)
            pe.wait_ge(v_ready, 1)
            for u in range(8):
                kv = u % 2
                pe.wait_ge(rotated, 2 + u + 1)
                if u >= 1:
                    pe.wait_ge(score_read, 4 * u)
                for n in range(TT):
                    for h in range(2):
                        last = pe.matmul(bank[2 + 2 * h + n // 2][:, n % 2 * 2 * WINDOW:(n % 2 + 1) * 2 * WINDOW],
                                         qr[h * HEAD:(h + 1) * HEAD, u % 2, n * P:(n + 1) * P],
                                         kdup[h * HEAD:(h + 1) * HEAD, kv, n * P:n * P + 2 * WINDOW],
                                         start=True, stop=True)
                        if n % 2:
                            last.then_inc(scored, 1)
                project(S_Q + u + 2, R_Q + u + 2, hT, strict=True)
                if u >= 1:
                    window_values(u - 1)
            for u in range(4):
                pe.wait_ge(proj_read, R_QM + u + 1)
                pe.wait_ge(score_read, 32 + 4 * u)
                for n in range(TT):
                    pe.matmul(bank[2 + n][:, 0:M], qr[:, u % 2, n * P:(n + 1) * P], kmT[:, u, :],
                              start=True, stop=True).then_inc(scored, 1)
                if u < 2:
                    project(S_QM + u + 2, R_QM + u + 2, hT, strict=True)
                if u == 0:
                    window_values(7)
                else:
                    memory_values(u - 1)
            memory_values(3)
            pe.wait_ge(y_lo, 16)
            with pe.Fori(0, KC - 2 + 1, 2) as c0:
                for dc in range(2):
                    for b in range(3):
                        n = S_GATE + GATE_CHUNKS * dc + b
                        chunk(c0 * GATE_CHUNKS + n)
                        if b == 0:
                            pe.wait_ge(gated, c0 * 3 + (3 * dc + 3))
                        product(bank[b][:, :], n % 2, hT)
                    n = S_GATE + GATE_CHUNKS * dc + 3
                    pe.wait_ge(branch_read, c0 * 3 + (3 * dc + 3))
                    chunk(c0 * GATE_CHUNKS + n)
                    product(bank[3][:, :], n % 2, yT, 0, 4, 0, used=False)
                    product(bank[4][:, :], n % 2, yT, 4, 8, 4)
                    chunk(c0 * GATE_CHUNKS + (n + 1))
                    product(bank[5][:, :], (n + 1) % 2, yT, 0, 8, 8)
            pe.wait_ge(gated, 3 * KC + 3)
            pe.wait_ge(branch_read, 3 * KC + 3)
            pe.wait_ge(merged_lo, KC)

            def spread_sum(slot, lhs, first, final):
                for t in range(TT):
                    for w, low_l in ((w_hi, 0), (w_lo, 0), (w_hi, 1)):
                        for half in range(2):
                            last = pe.matmul(bank[2 * t + half][:, :], lhs[low_l][:, t * P:(t + 1) * P],
                                             w[:, slot, half * 512:(half + 1) * 512],
                                             start=first and low_l == 0 and w is w_hi, stop=final and low_l == 1)
                    if final and t < TT - 1:
                        last.then_inc(summed, 1)
                last.then_inc(chunk_used, 1)

            for k in range(KC):
                chunk(S_OUT + k)
                spread_sum((S_OUT + k) % 2, (mg_hi[:, k, :], mg_lo[:, k, :]), k == 0, k == KC - 1)
            turn_ready = 2 + TT
            pe.wait_ge(x2_ready, TT)
            turn(x2n, turn_ready, False, 2 * KC)
            pe.wait_ge(turned_lo, 3 * KC)
            def queries(c0, dc):
                rn = R_PQ + dc
                chunk(c0 + (S_PQ + dc))
                pe.wait_ge(proj_read, c0 + (rn - 1))
                product(bank[rn % 2][:, :], (S_PQ + dc) % 2, hT)

            def sub_scores(c0, dc):
                b = dc % 2
                pe.wait_ge(proj_read, c0 + (R_PQ + dc + 1))
                pe.wait_ge(sub_read, c0 + (dc + 1))
                for t in range(TT):
                    last = pe.matmul(bank[2 + b][:, t * P:(t + 1) * P], qs[:, b, t * P:(t + 1) * P],
                                     subkeys[:, bass.ds(c0 + dc, 1), :], start=True, stop=True)
                last.then_inc(sub_done, 1)

            queries(0, 0)
            with pe.Fori(0, 2 * PEER_H - 3, 2) as c0:
                for dc in range(2):
                    queries(c0, dc + 1)
                    sub_scores(c0, dc)
            queries(2 * PEER_H - 2, 1)
            for dc in range(2):
                sub_scores(2 * PEER_H - 2, dc)

            def experts(i0, di):
                n, rn = S_U + di, R_U + di
                chunk(n + i0)
                pe.wait_ge(proj_read, rn - 1 + i0)
                product(bank[rn % 2][:, :], n % 2, hT)

            with pe.Fori(0, I_PLAIN - 2 + 1, 2) as i0:
                for di in range(2):
                    experts(i0, di)
            pe.wait_ge(sub_read, 2 * PEER_H + 2)
            pe.wait_ge(retrieved, 1)
            for j, src in enumerate((IF, JF, FV)):
                for t in range(TT):
                    last = pe.transpose(bank[2 + j][:, t * P:(t + 1) * P], src[:, t, :], ident[:, :])
                last.then_inc(spread, 1)
            pe.wait_ge(spread_read, 1)
            with pe.Fori(0, I_GATES - 2 + 1, 2) as i0:
                for di in range(2):
                    experts(i0 + I_PLAIN, di)
                    for b in range(2):
                        pe.wait_ge(gate_read, i0 * 2 + (2 * di + b + 1))
                        pe.wait_ge(hot_ready, i0 * 2 + (2 * di + b + 1))
                        for tk in range(TOK_I // 2):
                            at = b * (TOK_I // 2) + tk
                            for q in range(3):
                                last = pe.matmul(bank[2 + b][:, tk * P:(tk + 1) * P], ohJ[:, di, at, :],
                                                 ohI[:, di, at, q, :], start=(q == 0), stop=(q == 2))
                        last.then_inc(gate_mm, 1)
            with pe.Fori(I_PLAIN + I_GATES, NI - 1, 2) as i0:
                for di in range(2):
                    experts(i0, di)
            pe.wait_ge(gate_read, 2 * I_GATES + 2)
            pe.wait_ge(proj_read, R_U + NI)

            def weigh(i0, di, first=False, final=False):
                n = S_EV + di
                chunk(n + i0)
                pe.wait_ge(weighted_lo, i0 + (di + 1))
                spread_sum(n % 2, (wT_hi[:, di % 2, :], wT_lo[:, di % 2, :]), first, final)

            for i in range(2):
                weigh(0, i, first=(i == 0))
            with pe.Fori(2, NI - 2 - 2 + 1, 2) as i0:
                for di in range(2):
                    weigh(i0, di)
            for i in range(NI - 2, NI):
                weigh(0, i, final=(i == NI - 1))

        @block.scalar
        def _(act):
            step = Steps(act, act_step)
            for t in range(MT):
                act.dma_start(mem_sb[:, t, :], dram["mem"][t * P:(t + 1) * P, :]).then_inc(mem_loaded, 16)
            for t in range(TT):
                act.dma_start(x_sb[:, t, :], dram["x"][t * P:(t + 1) * P, :]).then_inc(x_loaded, 16)
            smalls = [(gains[:, :, :], dram["gains"]), (pscale[:, :], dram["pscale"]),
                      (wpool[:, :, :], dram["wpool"]), (sinks[:, :], dram["sinks"].broadcast_to([P, 16])),
                      (freq[:, :], dram["freq"]), (pos_i[:, :], dram["positions"].broadcast_to([P, T])),
                      (subkeys[:, :, :], dram["subkeys"])]
            assert len(smalls) == SMALLS
            for dst, src in smalls:
                act.dma_start(dst, src).then_inc(small_loaded, 16)

            def split(base, loop=0):
                slot = base % RAW
                act.wait_ge(raw_loaded[slot], loop * (16 // RAW) + (base // RAW + 1) * 16)
                if base >= 2:
                    act.wait_ge(chunk_used, loop + (base - 1))
                act.activation(w_hi[:, base % 2, :], raw[:, slot, :], ACT.Copy).then_inc(hi_ready, 1)

            act.wait_ge(eps_set, 1)
            act.wait_ge(mem_loaded, 16 * MT)
            for t in range(MT):
                last = act.activation(memn[:, t, :], mem_sb[:, t, :], ACT.Square, accum_out=ssum[:, t:t + 1])
            step(last)
            act.activation(std[:, 0:MT], ssum[:, 0:MT], ACT.Sqrt, scale=1.0 / D,
                           bias=eps[:, :]).then_inc(std_ready, 1)
            split(0)
            split(1)
            act.wait_ge(x_loaded, 16 * TT)
            for t in range(TT):
                last = act.activation(xn[:, t, :], x_sb[:, t, :], ACT.Square, accum_out=ssum[:, 2 + t:3 + t])
            step(last)
            act.activation(std[:, 2:2 + TT], ssum[:, 2:2 + TT], ACT.Sqrt, scale=1.0 / D,
                           bias=eps[:, :]).then_inc(std_ready, 1)
            act.wait_ge(small_loaded, 16 * SMALLS)
            for k in range(KC):
                act.wait_ge(turned, k + 1)
                act.activation(memT_hi[:, k, :], bank[k][:, 0:M], ACT.Copy,
                               scale=gains[:, 1, k:k + 1]).then_inc(turned_hi, 1)
            act.wait_ge(angles, 2)
            act.activation(cosT[:, :], cosT[:, :], ACT.Sin).then_inc(sines, 1)
            act.activation(sinT[:, :], sinT[:, :], ACT.Sin, scale=freq[:, 1:2]).then_inc(sines, 1)
            for h in range(4):
                act.wait_ge(chunk_used, S_KM + h + 1)
                split(S_KM + h + 2)
                act.activation(kmT[:, h, :], bank[(R_KM + h) % 2][:, 0:M], ACT.Copy).then_inc(proj_read, 1)
            for q in range(4):
                split(S_VM + q + 2)
            for m in range(MT):
                last = act.activation(vm[:, m, :], bank[2 + m][:, :], ACT.Copy)
            last.then_inc(vm_read, 1)

            def turn_high(gain, base):
                for k in range(KC):
                    act.wait_ge(turned, base + k + 1)
                    act.activation(hT_hi[:, k, :], bank[4 + k % 4][:, :], ACT.Copy,
                                   scale=gains[:, gain, k:k + 1]).then_inc(turned_hi, 1)

            turn_high(0, KC)

            def swap(j, rn, n):
                act.wait_ge(chunk_used, n + 1)
                if j >= 1:
                    act.wait_ge(rotated, j)
                b = rn % 2 if j < 2 else 0
                for qd in range(4):
                    last = act.activation(swp[32 * qd:32 * qd + 32, :],
                                          bank[b][32 * (qd ^ 1):32 * (qd ^ 1) + 32, :], ACT.Copy)
                last.then_inc(swapped, 1)

            for j in range(2):
                split(S_K + j + 2)
                swap(j, R_K + j, S_K + j)
            split(S_V + 2)
            act.wait_ge(chunk_used, S_V + 1)
            act.wait_ge(eps_set, 2)
            vb = bank[4][:, :].rearrange("p (t c) -> p t c", t=TT)
            for kv in range(2):
                last = act.activation(vz[:, kv, 1:, HEAD:2 * HEAD], vb[:, :, kv * HEAD:(kv + 1) * HEAD], ACT.Copy)
            last.then_inc(v_ready, 1)

            def mix_high(gi):
                act.wait_ge(mixed, gi + 1)
                act.activation(yT_hi[:, gi, :], bank[2 + gi % 2][:, :], ACT.Copy,
                               scale=pscale[:, gi:gi + 1]).then_inc(y_hi, 1)

            for gi in range(4):
                split(S_POOL + gi + 2)
                if gi >= 1:
                    mix_high(gi - 1)
            split(S_Q + 2)
            swap(2, R_Q, S_Q)
            mix_high(3)
            split(S_Q + 3)
            swap(3, R_Q + 1, S_Q + 1)

            def next_q(n):
                split(S_Q + n + 4)
                if n + 2 < 8:
                    swap(4 + n, R_Q + n + 2, S_Q + n + 2)
                else:
                    act.wait_ge(chunk_used, S_Q + n + 3)
                    act.activation(qr[:, n % 2, :], bank[0][:, :], ACT.Copy).then_inc(proj_read, 1)

            def turn_probs(count, made):
                for n in range(count):
                    act.wait_ge(probT_done, made + n + 1)
                    act.activation(probT[:, n % 2, :], bank[6 + n % 2][:, :], ACT.Copy).then_inc(probT_read, 1)

            def outputs_high(row, made):
                act.wait_ge(attended, made)
                act.activation(yT_hi[:, row, :], bank[1][:, :], ACT.Copy).then_inc(y_hi, 1)

            for u in range(8):
                next_q(u)
                if u >= 1:
                    turn_probs(TT, 4 * (u - 1))
                    outputs_high(8 + u - 1, u)
                act.wait_ge(capped, u + 1)
                pr = prob[u % 2]
                for n in range(TT):
                    for h in range(2):
                        act.activation(pr[:, n, h, :], pr[:, n, h, :], ACT.Exp, scale=HEAD ** -0.5,
                                       bias=negm[:, 2 * n + h:2 * n + h + 1],
                                       accum_out=rsum[:, 2 * n + h:2 * n + h + 1])
                act.activation(sexp[:, :], sdiff[:, :], ACT.Exp).then_inc(expd, 1)
            for u in range(4):
                if u < 2:
                    next_q(8 + u)
                if u == 0:
                    turn_probs(TT, 4 * 7)
                    outputs_high(8 + 7, 8)
                else:
                    turn_probs(2, 32 + 2 * (u - 1))
                    outputs_high(4 + u - 1, 8 + u)
                act.wait_ge(capped, 8 + u + 1)
                for n in range(TT):
                    act.activation(prob[u % 2][:, n, 0, :], bank[2 + n][:, 0:M], ACT.Exp, scale=P ** -0.5,
                                   bias=negm[:, n:n + 1], accum_out=rsum[:, n:n + 1]).then_inc(score_read, 1)
            turn_probs(2, 32 + 2 * 3)
            outputs_high(4 + 3, 12)
            act.sem_inc(gated, 3)
            with act.Fori(0, KC - 4 + 1, 4) as c0:
                for dc in range(4):
                    for q in range(GATE_CHUNKS):
                        base = S_GATE + GATE_CHUNKS * dc + q
                        split(base + 2, loop=c0 * GATE_CHUNKS)
                        if q == 0:
                            act.wait_ge(branch_read, c0 * 3 + (3 * dc + 3))
                        if q < 3:
                            act.wait_ge(chunk_used, c0 * GATE_CHUNKS + (base + 1))
                            act.activation(sg[:, q, :], bank[q][:, :], ACT.Sigmoid).then_inc(gated, 1)
                    act.wait_ge(merged, c0 + (dc + 1))
                    act.activation(mg_hi[:, bass.ds(c0 + dc, 1), :], part[:, 0:1, :], ACT.Copy).then_inc(merged_hi, 1)
            for k in range(KC):
                split(S_OUT + k + 2)
            for t in range(TT):
                act.wait_ge(x2_ready, t + 1)
                step(act.activation(x2n[:, t, :], x_sb[:, t, :], ACT.Square, accum_out=ssum[:, t:t + 1]))
                act.activation(std[:, t:t + 1], ssum[:, t:t + 1], ACT.Sqrt, scale=1.0 / D,
                               bias=eps[:, :]).then_inc(std_ready, 1)
            turn_high(2, 2 * KC)
            with act.Fori(0, 2 * PEER_H - 4 + 1, 4) as c0:
                for dc in range(4):
                    base = S_PQ + dc
                    act.wait_ge(chunk_used, base + 1 + c0)
                    split(base + 2, loop=c0)
                    act.activation(qs[:, dc % 2, :], bank[(R_PQ + dc) % 2][:, :], ACT.Copy).then_inc(proj_read, 1)

            def gelu(i0, di):
                base = S_U + di
                split(base + 2, loop=i0)
                act.wait_ge(chunk_used, base + 1 + i0)
                if not (isinstance(i0, int) and i0 + di < 2):
                    act.wait_ge(a_stored[di % 2], (i0 + (di - di % 2)) * 8)
                act.activation(abuf[:, di % 2, :], bank[(R_U + di) % 2][:, :],
                               ACT.Gelu_apprx_tanh).then_inc(proj_read, 1)

            for i in range(4):
                gelu(0, i)
            with act.Fori(4, I_PLAIN - 4 + 1, 4) as i0:
                for di in range(4):
                    gelu(i0, di)
            act.wait_ge(shifted, 1)
            act.activation(FV[:, :, :], FV[:, :, :], ACT.Exp).then_inc(exp_final, 1)
            act.sem_inc(gate_read, 2)

            def gates_out(i0, first=False):
                for half in range(2):
                    if not first:
                        act.wait_ge(g_stored[half], i0 * (4 * 16 // (2 * PER)))
                    for k in range(PER):
                        di = half * PER + k
                        gelu(i0 + I_PLAIN, di)
                        for b in range(2):
                            act.wait_ge(gate_mm, i0 * 2 + (2 * di + b + 1))
                            t0 = k * TOK_I + b * TOK_I // 2
                            act.activation(gstage[:, half, :, t0:t0 + TOK_I // 2].rearrange("p i t -> p t i"),
                                           bank[2 + b][:, :].rearrange("p (t i) -> p t i", i=NKEYS),
                                           ACT.Copy).then_inc(gate_read, 1)

            gates_out(0, first=True)
            with act.Fori(2 * PER, I_GATES - 2 * PER + 1, 2 * PER) as i0:
                gates_out(i0)
            with act.Fori(I_PLAIN + I_GATES, NI - 3, 4) as i0:
                for di in range(4):
                    gelu(i0, di)

            def weigh_high(i0, di):
                act.wait_ge(weighted, i0 + (di + 1))
                act.activation(wT_hi[:, di % 2, :], wf[:, di % 2, :], ACT.Copy).then_inc(weighted_hi, 1)

            weigh_high(0, 0)
            with act.Fori(0, NI - 4 - 4 + 1, 4) as i0:
                for di in range(4):
                    weigh_high(i0, di + 1)
                    split(S_EV + di + 2, loop=i0)
            for i in range(NI - 4, NI - 1):
                weigh_high(0, i + 1)
                if i < NI - 2:
                    split(S_EV + i + 2)
            for t in range(TT):
                act.wait_ge(x3_ready, t + 1)
                step(act.activation(junk[:, :], x_sb[:, t, :], ACT.Square, accum_out=ssum[:, t:t + 1]))
                act.activation(std[:, t:t + 1], ssum[:, t:t + 1], ACT.Sqrt, scale=1.0 / D,
                               bias=eps[:, :]).then_inc(final_std, 1)

        @block.vector
        def _(dve):
            step = Steps(dve, dve_step)
            dve.memset(eps[:, :], EPS).then_inc(eps_set, 1)
            dve.memset(kdup[:, :, 0:WINDOW], 0.0)
            for buf in (ub, sA, sB):
                dve.memset(buf[:, 0:PAD], 0.0)
            dve.memset(vz[:, :, :, :], 0.0).then_inc(eps_set, 1)

            def normalise(dst, src, nt, col, ready):
                dve.wait_ge(std_ready, ready)
                step(dve.reciprocal(rstd[:, col:col + nt], std[:, col:col + nt]))
                for t in range(nt):
                    last = dve.tensor_scalar(dst[:, t, :], src[:, t, :], rstd[:, col + t:col + t + 1], None, ALU.mult)
                    if nt == TT or t == nt - 1:
                        last.then_inc(normed, 1)

            normalise(memn, mem_sb, MT, 0, 1)
            dve.wait_ge(small_loaded, 16 * SMALLS)
            two_pi = 2 * math.pi
            c1 = 6.28125
            c2 = float(np.float32(np.floor((two_pi - c1) * 2 ** 21) / 2 ** 21))
            c3 = float(np.float32(two_pi - c1 - c2))
            magic = 1.5 * 2 ** 23
            limit = 3.1415925
            posf, ang, turns = sg[:, 0, :], sg[:, 1, :], sg[:, 2, :]
            step(dve.tensor_copy(posf, pos_i[:, :]))
            step(dve.tensor_scalar(ang, posf, freq[:, 0:1], None, ALU.mult))
            for made, (dst, quarter) in enumerate(((sinT, 0.0), (cosT, 0.25))):
                step(dve.tensor_scalar(turns, ang, 1.0 / two_pi, quarter, ALU.mult, ALU.add))
                step(dve.tensor_scalar(turns, turns, magic, None, ALU.add))
                step(dve.tensor_scalar(turns, turns, -magic, None, ALU.add))
                step(dve.scalar_tensor_tensor(out=posf, in0=turns, scalar=-c1, in1=ang, op0=ALU.mult, op1=ALU.add))
                step(dve.scalar_tensor_tensor(out=dst[:, :], in0=turns, scalar=-c2, in1=posf, op0=ALU.mult, op1=ALU.add))
                step(dve.scalar_tensor_tensor(out=posf, in0=turns, scalar=-c3, in1=dst[:, :], op0=ALU.mult, op1=ALU.add))
                step(dve.tensor_scalar(turns, posf, quarter * two_pi, limit, ALU.add, ALU.min))
                dve.tensor_scalar(dst[:, :], turns, -limit, None, ALU.max).then_inc(angles, 1)
                dve.wait_ge(angles, made + 1)
            for k in range(KC):
                dve.wait_ge(turned_hi, k + 1)
                dve.scalar_tensor_tensor(out=memT_lo[:, k, :], in0=bank[k][:, 0:M],
                                         scalar=gains[:, 1, k:k + 1], in1=memT_hi[:, k, :].bitcast(f32),
                                         op0=ALU.mult, op1=ALU.subtract).then_inc(turned_lo, 1)
            normalise(xn, x_sb, TT, 2, 2)
            dve.wait_ge(consts, 2)
            for gi, w in enumerate(POOL_WINDOWS):
                last = dve.tensor_scalar(rcnt[:, gi, :], rcnt[:, gi, :], float(w), None, ALU.min)
            step(last)
            step(dve.reciprocal(rcnt[:, :, :], rcnt[:, :, :]))

            def turn_low(gain, base):
                for k in range(KC):
                    dve.wait_ge(turned_hi, base + k + 1)
                    dve.scalar_tensor_tensor(out=hT_lo[:, k, :], in0=bank[4 + k % 4][:, :],
                                             scalar=gains[:, gain, k:k + 1], in1=hT_hi[:, k, :].bitcast(f32),
                                             op0=ALU.mult, op1=ALU.subtract).then_inc(turned_lo, 1)

            turn_low(0, KC)
            dve.wait_ge(sines, 2)

            def rotate(j, rn, dst):
                dve.wait_ge(swapped, j + 1)
                dve.tensor_tensor(dst, bank[rn % 2 if j < 2 else 0][:, :], cosT[:, :], ALU.mult).then_inc(proj_read, 1)
                step(dve.tensor_tensor(swp[:, :], swp[:, :], sinT[:, :], ALU.mult))
                dve.tensor_tensor(dst, dst, swp[:, :], ALU.add).then_inc(rotated, 1)

            for j in range(2):
                rotate(j, R_K + j, kdup[:, j, WINDOW:])

            def window(gi):
                dve.wait_ge(chunk_used, S_POOL + gi + 1)
                if gi >= 1:
                    dve.wait_ge(pooled, gi)
                dve.tensor_copy(sA[:, PAD:], bank[(R_POOL + gi) % 2][:, :]).then_inc(proj_read, 1)
                dve.wait_ge(proj_read, R_POOL + gi + 1)
                if gi >= 1:
                    dve.wait_ge(mixed, gi)
                step(dve.tensor_scalar(ub[:, PAD:], sA[:, PAD:], -1.0, None, ALU.mult))
                src, dst = sA, sB
                for lv in range(gi + 1):
                    sh = 1 << lv
                    step(dve.tensor_tensor(dst[:, PAD:], src[:, PAD:], src[:, PAD - sh:PAD + T - sh], ALU.add))
                    src, dst = dst, src
                w = POOL_WINDOWS[gi]
                step(dve.tensor_tensor(dst[:, PAD:2 * PAD], src[:, PAD:2 * PAD], rcnt[:, gi, :], ALU.mult))
                step(dve.scalar_tensor_tensor(out=ub[:, 2 * PAD:], in0=src[:, 2 * PAD:], scalar=1.0 / w,
                                              in1=ub[:, 2 * PAD:], op0=ALU.mult, op1=ALU.add))
                dve.tensor_tensor(ub[:, PAD:2 * PAD], dst[:, PAD:2 * PAD], ub[:, PAD:2 * PAD],
                                  ALU.add).then_inc(pooled, 1)

            def mix_low(gi):
                dve.wait_ge(y_hi, gi + 1)
                dve.scalar_tensor_tensor(out=yT_lo[:, gi, :], in0=bank[2 + gi % 2][:, :],
                                         scalar=pscale[:, gi:gi + 1], in1=yT_hi[:, gi, :].bitcast(f32),
                                         op0=ALU.mult, op1=ALU.subtract).then_inc(y_lo, 1)
            for gi in range(4):
                window(gi)
                if gi >= 1:
                    mix_low(gi - 1)
            rotate(2, R_Q, qr[:, 0, :])
            mix_low(3)
            rotate(3, R_Q + 1, qr[:, 1, :])

            def outputs_low(row, made):
                dve.wait_ge(y_hi, made)
                dve.tensor_tensor(yT_lo[:, row, :], bank[1][:, :], yT_hi[:, row, :].bitcast(f32),
                                  ALU.subtract).then_inc(y_lo, 1)

            for u in range(8):
                pr = prob[u % 2]
                pair = [b[:, :].rearrange("p (n h) -> p n h", h=2) for b in (mx, mcap, sdiff)]
                if u >= 2:
                    dve.wait_ge(probT_done, 4 * (u - 1))
                for b in range(4):
                    j, h = b // 2, b % 2
                    dve.wait_ge(scored, 4 * u + b + 1)
                    seen = mask[:, :, :] if j == 0 else mask[:, 1:2, :].broadcast_to([P, 2, 2 * WINDOW])
                    dve.tensor_tensor(pr[:, 2 * j:2 * j + 2, h, :],
                                      bank[2 + 2 * h + j][:, :].rearrange("p (n k) -> p n k", n=2), seen,
                                      ALU.add).then_inc(score_read, 1)
                for b in range(4):
                    j, h = b // 2, b % 2
                    if b == 0:
                        dve.wait_ge(score_read, 4 * (u + 1))
                    last = dve.reduce_max(pair[0][:, 2 * j:2 * j + 2, h:h + 1], pr[:, 2 * j:2 * j + 2, h, :], AX.X)
                step(last)
                snk = sinks[:, 2 * u:2 * u + 2].unsqueeze(1).broadcast_to([P, TT, 2])
                step(dve.scalar_tensor_tensor(out=pair[1], in0=pair[0], scalar=HEAD ** -0.5, in1=snk,
                                              op0=ALU.mult, op1=ALU.max))
                dve.tensor_scalar(negm[:, :], mcap[:, :], -1.0, None, ALU.mult)
                dve.tensor_tensor(pair[2], snk, pair[1], ALU.subtract).then_inc(capped, 1)
                if u < 6:
                    rotate(4 + u, R_Q + u + 2, qr[:, u % 2, :])
                if u >= 1:
                    outputs_low(8 + u - 1, 4 + u)
                dve.wait_ge(expd, u + 1)
                step(dve.tensor_tensor(den[:, :], rsum[:, :], sexp[:, :], ALU.add))
                step(dve.reciprocal(rinv[:, :], den[:, :]))
                for n in range(TT):
                    for h in range(2):
                        last = dve.tensor_scalar(pr[:, n, h, :], pr[:, n, h, :],
                                                 rinv[:, 2 * n + h:2 * n + h + 1], None, ALU.mult)
                    last.then_inc(prob_ready, 1)
            for u in range(4):
                for n in range(TT):
                    dve.wait_ge(scored, 32 + 4 * u + n + 1)
                    last = dve.reduce_max(mx[:, n:n + 1], bank[2 + n][:, 0:M], AX.X)
                step(last)
                dve.wait_ge(probT_done, 28 if u == 0 else 32 + 2 * (u - 1))
                dve.tensor_scalar(negm[:, 0:TT], mx[:, 0:TT], -(P ** -0.5), None, ALU.mult).then_inc(capped, 1)
                if u == 0:
                    outputs_low(8 + 7, 12)
                else:
                    outputs_low(4 + u - 1, 12 + u)
                dve.wait_ge(score_read, 32 + 4 * (u + 1))
                dve.wait_ge(prob_ready, 32 + 4 * u)
                step(dve.reciprocal(rinv[:, 0:TT], rsum[:, 0:TT]))
                for n in range(TT):
                    dve.tensor_scalar(prob[u % 2][:, n, 0, :], prob[u % 2][:, n, 0, :], rinv[:, n:n + 1], None,
                                      ALU.mult).then_inc(prob_ready, 1)
            outputs_low(4 + 3, 16)
            dve.sem_inc(branch_read, 3)
            first_step, per_turn = step.value, 1
            with dve.Fori(0, KC) as c:
                step.value, step.made = c * per_turn + first_step, 0
                dve.wait_ge(gated, c * 3 + 6)
                dve.wait_ge(chunk_used, c * GATE_CHUNKS + (S_GATE + GATE_CHUNKS))
                for q, b in enumerate((3, 5, 4)):
                    dve.tensor_tensor(part[:, q, :], sg[:, q, :], bank[b][:, :], ALU.mult).then_inc(branch_read, 1)
                dve.wait_ge(branch_read, c * 3 + 6)
                step(dve.tensor_tensor(part[:, 1, :], part[:, 1, :], part[:, 2, :], ALU.add))
                dve.tensor_tensor(part[:, 0, :], part[:, 0, :], part[:, 1, :], ALU.add).then_inc(merged, 1)
                dve.wait_ge(merged_hi, c + 1)
                dve.tensor_tensor(mg_lo[:, bass.ds(c, 1), :], part[:, 0:1, :],
                                  mg_hi[:, bass.ds(c, 1), :].bitcast(f32), ALU.subtract).then_inc(merged_lo, 1)
                dve.wait_ge(merged_lo, c + 1)
                assert step.made == per_turn
            step.value = first_step + per_turn * KC
            for t in range(TT):
                if t < TT - 1:
                    dve.wait_ge(summed, t + 1)
                else:
                    dve.wait_ge(chunk_used, S_PQ)
                for half in range(2):
                    cols = slice(half * 512, (half + 1) * 512)
                    last = dve.tensor_tensor(x_sb[:, t, cols], x_sb[:, t, cols], bank[2 * t + half][:, :], ALU.add)
                last.then_inc(x2_ready, 1)
            for t in range(TT):
                dve.wait_ge(std_ready, 3 + t)
                step(dve.reciprocal(rstd[:, t:t + 1], std[:, t:t + 1]))
                dve.tensor_scalar(x2n[:, t, :], x_sb[:, t, :], rstd[:, t:t + 1], None, ALU.mult).then_inc(normed, 1)
            turn_low(2, 2 * KC)
            dve.sem_inc(sub_read, 2)
            with dve.Fori(0, 2 * PEER_H - 2 + 1, 2) as c0:
                for dc in range(2):
                    dve.wait_ge(sub_done, c0 + (dc + 1))
                    dve.tensor_copy(sc[:, :, bass.ds(c0 + dc, 1), :],
                                    bank[2 + dc][:, :].rearrange("p (t a n) -> p t a n", t=TT, a=1)
                                    ).then_inc(sub_read, 1)
            dve.wait_ge(sub_read, 2 * PEER_H + 2)

            halves = [(h, q) for h in range(PEER_H) for q in range(2)]
            hrow = lambda buf, h: buf[:, h, :]
            s1 = lambda buf, h, q: buf[:, h, q * NKEYS:(q + 1) * NKEYS]
            all2 = "p h (a b) -> p h a b"

            def best(src, spare, vals, inds):
                for s_, v_ in zip(src, vals):
                    last = dve.max(v_[:, 0:8], s_)
                dve.drain()
                for s_, z_, v_, i_ in zip(src, spare, vals, inds):
                    dve.max_index(i_[:, 0:8], v_[:, 0:8], s_)
                    last = dve.match_replace(z_, v_[:, 0:8], s_, BELOW)
                dve.drain()
                for z_, v_ in zip(spare, vals):
                    last = dve.max(v_[:, 8:16], z_)
                dve.drain()
                for z_, v_, i_ in zip(spare, vals, inds):
                    last = dve.max_index(i_[:, 8:16], v_[:, 8:16], z_)
                dve.drain()

            with dve.Fori(0, TT) as t:
                scur4 = scur[:, :, :].rearrange("p h (q n) -> p (h q) n", q=2)
                dve.tensor_copy(scur4.unsqueeze(1), sc[:, bass.ds(t, 1), :, :])
                dve.drain()
                best([s1(scur, h, q) for h, q in halves], [s1(scur2, h, q) for h, q in halves],
                     [top[:, h, q, :] for h, q in halves], [topi[:, h, q, :] for h, q in halves])
                dve.tensor_copy(topf[:, :, :, :], topi[:, :, :, :])
                grid = [P, PEER_H, TOPK, TOPK]
                dve.tensor_tensor(cand[:, :, :].rearrange(all2, a=TOPK),
                                  top[:, :, 0, :].unsqueeze(3).broadcast_to(grid),
                                  top[:, :, 1, :].unsqueeze(2).broadcast_to(grid), ALU.add)
                dve.drain()
                best([hrow(cand, h) for h in range(PEER_H)], [hrow(cand2, h) for h in range(PEER_H)],
                     [hrow(fin, h) for h in range(PEER_H)],
                     [fpos[:, h * TOPK:(h + 1) * TOPK] for h in range(PEER_H)])
                dve.tensor_tensor(FV[:, bass.ds(t, 1), :].rearrange("p a (h k) -> p (a h) k", h=PEER_H), fin[:, :, :],
                                  fin[:, :, 0:1].broadcast_to([P, PEER_H, TOPK]), ALU.subtract)
                for q, dst in ((0, IF), (1, JF)):
                    if q == 0:
                        dve.tensor_scalar(fsel[:, :], fpos[:, :], 4, None, ALU.logical_shift_right)
                        dve.drain()
                    else:
                        dve.tensor_scalar(fsel[:, :], fpos[:, :], TOPK - 1, None, ALU.bitwise_and)
                        dve.drain()
                    dve.tensor_copy(fself[:, :], fsel[:, :])
                    dve.drain()
                    flat = [P, HK, TOPK]
                    pick = cand[:, :, :].rearrange("p h (k a) -> p (h k) a", a=TOPK)
                    dve.tensor_tensor(pick, fself[:, :].unsqueeze(2).broadcast_to(flat),
                                      iota_k[:, :].unsqueeze(1).broadcast_to(flat), ALU.is_equal)
                    dve.drain()
                    pick4 = cand[:, :, :].rearrange(all2, a=TOPK)
                    dve.tensor_tensor(pick4, pick4, topf[:, :, q, :].unsqueeze(2).broadcast_to(grid), ALU.mult)
                    dve.drain()
                    dve.tensor_reduce(dst[:, bass.ds(t, 1), :].rearrange("p a n -> p (a n)"), pick,
                                      AX.X, ALU.add)
                    dve.drain()
            dve.drain().then_inc(shifted, 1)
            dve.wait_ge(exp_final, 1)
            rows3 = FV[:, :, :].rearrange("p t (h k) -> p (t h) k", k=TOPK)
            step(dve.reduce_sum(gsm[:, :], rows3, AX.X))
            step(dve.reciprocal(gsm[:, :], gsm[:, :]))
            dve.tensor_tensor(rows3, rows3, gsm[:, :].unsqueeze(2).broadcast_to([P, TT * PEER_H, TOPK]),
                              ALU.mult).then_inc(retrieved, 1)
            dve.wait_ge(spread, 3)
            dve.tensor_copy(IT[:, :], bank[2][:, :])
            dve.tensor_copy(JT[:, :], bank[3][:, :])
            dve.tensor_copy(GT[:, :], bank[4][:, :]).then_inc(spread_read, 1)
            dve.wait_ge(spread_read, 1)
            step(dve.tensor_copy(gbf[:, :], GT[:, :]))
            step(dve.tensor_tensor(R1[:, :], GT[:, :], gbf[:, :], ALU.subtract))
            step(dve.tensor_copy(gbf[:, :], R1[:, :]))
            step(dve.tensor_tensor(R2[:, :], R1[:, :], gbf[:, :], ALU.subtract))

            def one_hots(i0, di, first=False):
                for b in range(2):
                    if not first:
                        dve.wait_ge(gate_mm, i0 * 2 + (2 * di + b - 3))
                    for tk in range(TOK_I // 2):
                        at = b * (TOK_I // 2) + tk
                        col = bass.ds(i0 * TOK_I + (di * TOK_I + at), 1)
                        dve.tensor_scalar(ohJ[:, di, at, :], iota_b[:, :], JT[:, col], None, ALU.is_equal)
                        for q, gate in enumerate((GT, R1, R2)):
                            last = dve.tensor_scalar(ohI[:, di, at, q, :], iota_b[:, :], IT[:, col], gate[:, col],
                                                     ALU.is_equal, ALU.mult)
                    last.then_inc(hot_ready, 1)

            for di in range(2):
                one_hots(0, di, first=True)
            with dve.Fori(2, I_GATES - 2 + 1, 2) as i0:
                for di in range(2):
                    one_hots(i0, di)

            def weigh(i0, di, first=False):
                dve.wait_ge(a_loaded[di % 4], i0 * 4 + (di // 4 + 1) * 16)
                if di % GROUP == 0:
                    dve.wait_ge(g_loaded[di // GROUP], i0 + 16)
                if not first:
                    dve.wait_ge(chunk_used, i0 + (S_EV + di - 1))
                tiles = "p (b t) -> p b t"
                dve.tensor_tensor(wf[:, di % 2, :].rearrange(tiles, b=BLOCKS),
                                  a_in[:, di % 4, :].rearrange(tiles, b=BLOCKS),
                                  g_in[:, di // GROUP, :, di % GROUP, :], ALU.mult).then_inc(weighted, 1)
                dve.wait_ge(weighted_hi, i0 + (di + 1))
                dve.tensor_tensor(wT_lo[:, di % 2, :], wf[:, di % 2, :], wT_hi[:, di % 2, :].bitcast(f32),
                                  ALU.subtract).then_inc(weighted_lo, 1)

            for i in range(16):
                weigh(0, i, first=(i < 2))
            with dve.Fori(16, NI - 15, 16) as i0:
                for di in range(16):
                    weigh(i0, di)
            dve.wait_ge(gfin_loaded, 16)
            for t in range(TT):
                if t < TT - 1:
                    dve.wait_ge(summed, TT - 1 + t + 1)
                else:
                    dve.wait_ge(chunk_used, CHUNKS)
                for half in range(2):
                    cols = slice(half * 512, (half + 1) * 512)
                    last = dve.tensor_tensor(x_sb[:, t, cols], x_sb[:, t, cols], bank[2 * t + half][:, :], ALU.add)
                last.then_inc(x3_ready, 1)
            for t in range(TT):
                dve.wait_ge(final_std, t + 1)
                step(dve.reciprocal(rstd[:, t:t + 1], std[:, t:t + 1]))
                dve.scalar_tensor_tensor(out=x_sb[:, t, :], in0=x_sb[:, t, :], scalar=rstd[:, t:t + 1],
                                         in1=gfin[:, :], op0=ALU.mult, op1=ALU.mult).then_inc(final_ready, 1)


def layout(inputs):
    f = lambda n: np.ascontiguousarray(inputs[n])
    w_in, w_kv = f("w_in")[0], f("w_mem_kv")[0]
    pool_w, swa_w, kv_w = 4 * P, D, 2 * HEAD
    q0 = pool_w
    k0 = q0 + swa_w
    v0 = k0 + kv_w
    m0 = v0 + kv_w
    g0 = m0 + 4 * P

    def cols(w, idx):
        w = w[:, idx]
        return w.reshape(-1, P, P).transpose(1, 0, 2).reshape(P, -1)

    chunks = [cols(w_kv, slice(h * P, (h + 1) * P)) for h in range(4)]
    vals = w_kv[:, 4 * P:].reshape(KC, P, T)
    chunks += [vals[2 * q:2 * q + 2].transpose(1, 0, 2).reshape(P, D) for q in range(4)]
    for kv in range(2):
        one = list(range(k0 + kv * HEAD, k0 + (kv + 1) * HEAD))
        chunks.append(cols(w_in, one + one))
    chunks.append(cols(w_in, slice(v0, v0 + P)))
    chunks += [cols(w_in, slice(gi * P, (gi + 1) * P)) for gi in range(4)]
    chunks += [cols(w_in, slice(q0 + c * P, q0 + (c + 1) * P)) for c in Q_ORDER]
    chunks += [cols(w_in, slice(m0 + h * P, m0 + (h + 1) * P)) for h in range(4)]
    pm = np.concatenate([f("w_branch_pool")[0], f("w_branch_mem")[0]], axis=0)
    sw = f("w_branch_swa")[0].reshape(8, P, D)[Q_ORDER].reshape(D, D)
    for c in range(KC):
        for b in range(3):
            chunks.append(cols(w_in, slice(g0 + b * D + c * P, g0 + b * D + (c + 1) * P)))
        chunks.append(cols(pm, slice(c * P, (c + 1) * P)))
        chunks.append(cols(sw, slice(c * P, (c + 1) * P)))
    chunks += list(f("w_out")[0].reshape(KC, P, D))
    chunks += [cols(f("peer_w_q")[0], slice(c * P, (c + 1) * P)) for c in range(2 * PEER_H)]
    u = f("peer_u")[0].reshape(NI, P, KC, P).transpose(0, 3, 2, 1).reshape(NI, P, D)
    stream = np.concatenate([np.stack(chunks), u, f("peer_v")[0].reshape(NI, P, D)], axis=0)
    assert stream.shape == (CHUNKS, P, D)
    half = HEAD // 2
    inv = (10000.0 ** (-np.arange(half, dtype=np.float64) / half)).astype(np.float32)
    sign = np.where(np.arange(P) % HEAD < half, -1.0, 1.0).astype(np.float32)
    freq = np.stack([inv[np.arange(P) % half], sign], axis=1)
    gains = np.stack([f(n)[0].reshape(KC, P).T for n in ("norm1_g", "mem_norm_g", "norm2_g")], axis=1)
    return {
        "stream": stream,
        "x": f("x")[0], "mem": f("mem")[0], "positions": f("positions"),
        "gains": gains, "pscale": f("pool_scale")[0].reshape(4, P).T,
        "wpool": f("w_pool")[0].transpose(1, 0, 2),
        "sinks": f("attn_sinks").reshape(8, 2)[Q_ORDER].reshape(1, 16),
        "freq": freq,
        "subkeys": f("peer_sub_keys")[0].reshape(2 * PEER_H, NKEYS, P).transpose(2, 0, 1),
        "gfin": f("final_norm_g").reshape(1, D),
    }


def kernel(**inputs):
    import concourse.bacc as _bacc
    from concourse.bass_utils import run_bass_kernel_spmd as _run

    nc = _bacc.Bacc("TRN2", target_bir_lowering=False, num_devices=1)
    arrays, dram = {}, {}
    for name, a in layout(inputs).items():
        arrays[name] = np.ascontiguousarray(a)
        dram[name] = nc.dram_tensor(name, arrays[name].shape, mybir.dt.from_np(arrays[name].dtype),
                                    kind="ExternalInput").ap()
    for name, shape in (("a", (NI, P, T)),
                        ("g", (NI // GROUP, P, BLOCKS, GROUP * STAGE_T))):
        dram[name] = nc.dram_tensor(name + "_rows", shape, mybir.dt.float32, kind="Internal").ap()
    out = nc.dram_tensor("out", (T, D), mybir.dt.float32, kind="ExternalOutput").ap()
    build(nc, dram, out)
    r = _run(nc, [arrays], core_ids=[0])
    return r.results[0]["out"].reshape(1, T, D)
```

```python
import math
from contextlib import ExitStack

import concourse.bass as bass
import numpy as np
from concourse import mybir

T, D, P = 512, 1024, 128
TT, KC = T // P, D // P
M = 256
MT = M // P
HEAD, WINDOW = 64, 128
POOL_WINDOWS = (2, 4, 8, 16)
PAD = max(POOL_WINDOWS)
PEER_H, TOPK, NKEYS = 8, 16, 128
HK = PEER_H * TOPK
NEXP = NKEYS * NKEYS
NI = NEXP // P
NEG = -1e30
BELOW = -3.0e38
EPS = 1e-6

S_KM, S_VM, S_K, S_V, S_POOL = 0, 4, 8, 9, 10
S_Q, S_QM, S_GATE = 14, 22, 26
GATE_CHUNKS = 5
S_OUT = S_GATE + GATE_CHUNKS * KC
S_PQ = S_OUT + KC
S_U = S_PQ + 2 * PEER_H
S_EV = S_U + NI
CHUNKS = S_EV + NI
RAW = 4
Q_ORDER = [q // 2 + 4 * (q % 2) for q in range(8)]
R_KM, R_K, R_V, R_POOL, R_Q, R_QM, R_PQ, R_U = 0, 4, 5, 6, 10, 18, 22, 38

I_PLAIN, I_GATES = 48, 64
I_SPREAD = 2
I_TAIL = NI - I_PLAIN - I_GATES
TOK_I = T // I_GATES
STAGE_T = 64
BLOCKS = T // STAGE_T
PER = STAGE_T // TOK_I
GROUP = 8
SMALLS = 6
AHEAD = 6


def build(nc, dram, out):
    f32, f32r, bf16, u32, i32 = (mybir.dt.float32, mybir.dt.float32r, mybir.dt.bfloat16,
                                 mybir.dt.uint32, mybir.dt.int32)
    ACT, ALU, AX = mybir.ActivationFunctionType, mybir.AluOpType, mybir.AxisListType

    with ExitStack() as ctx:
        arena_size = 212800
        arena = ctx.enter_context(nc.sbuf_tensor("arena", [P, arena_size], mybir.dt.uint8))
        arena_at = int(nc.sbuf_base) - arena_size
        assert arena_at % 32 == 0

        class Place:
            def __init__(self, at):
                self.at = at

            def __call__(self, name, shape, dt=f32):
                t = nc.alloc_sbuf_tensor_at(name, [P] + list(shape), dt, offset=arena_at + self.at)
                size = int(np.prod(shape)) * (2 if dt == bf16 else 4)
                self.at += (size + 31) // 32 * 32
                assert self.at <= arena_size, (name, self.at)
                return t

        keep = Place(0)
        x_sb = keep("x_sb", [TT, D])
        hT_hi = keep("hT_hi", [KC, T], f32r)
        hT_lo = keep("hT_lo", [KC, T], f32r)
        raw = keep("raw", [RAW, D])
        w_hi = keep("w_hi", [2, D], f32r)
        w_lo = keep("w_lo", [2, D], f32r)
        subkeys = keep("subkeys", [2 * PEER_H, NKEYS])
        ident = keep("ident", [P])
        gains = keep("gains", [3, KC])
        pscale = keep("pscale", [4])
        sinks = keep("sinks", [16])
        freq = keep("freq", [2])
        iota_b = keep("iota_b", [NKEYS], bf16)
        iota_k = keep("iota_k", [TOPK])
        eps = keep("eps", [1])
        ssum = keep("ssum", [8])
        std = keep("std", [8])
        rstd = keep("rstd", [8])
        mx = keep("mx", [8])
        mcap = keep("mcap", [8])
        negm = keep("negm", [8])
        sdiff = keep("sdiff", [8])
        sexp = keep("sexp", [8])
        rsum = keep("rsum", [8])
        den = keep("den", [8])
        rinv = keep("rinv", [8])
        front = keep.at

        y = Place(front)
        yT_hi = y("yT_hi", [16, T], f32r)
        yT_lo = y("yT_lo", [16, T], f32r)
        s = Place(front)
        mem_sb = s("mem_sb", [MT, D])
        memn = s("memn", [MT, D])
        memT_hi = s("memT_hi", [KC, M], f32r)
        memT_lo = s("memT_lo", [KC, M], f32r)
        xn = s("xn", [TT, D])
        assert s.at <= y.at
        a = Place(y.at)
        cosT = a("cosT", [T])
        sinT = a("sinT", [T])
        mask = a("mask", [2, 2 * WINDOW])
        kdup = a("kdup", [2, WINDOW + T])
        v_sb = a("v_sb", [2, TT, HEAD])
        kmT = a("kmT", [4, M])
        vm = a("vm", [MT, T])
        pos_i = Place(a.at)("pos_i", [T], i32)
        vT = Place(a.at + 4 * T)("vT", [T])
        qr = a("qr", [2, T])
        swp = a("swp", [T])
        k_rot = Place(a.at)("k_rot", [T])
        prob0 = a("prob0", [TT, 2, 2 * WINDOW])
        probT = a("probT", [2, T])
        g = Place(y.at)
        mg_hi = g("mg_hi", [KC, T], f32r)
        mg_lo = g("mg_lo", [KC, T], f32r)
        sg = g("sg", [3, T])
        part = g("part", [3, T])
        p = Place(max(a.at, g.at))
        ub = p("ub", [PAD + T])
        sA = p("sA", [PAD + T])
        sB = p("sB", [PAD + T])
        rcnt = p("rcnt", [4, PAD])
        wpool = p("wpool", [4, P])
        prob1 = Place(max(a.at, g.at))("prob1", [TT, 2, 2 * WINDOW])
        assert TT * 2 * 2 * WINDOW * 4 <= p.at - max(a.at, g.at)
        prob = (prob0, prob1)

        r = Place(front)
        abuf = r("abuf", [2, T])
        IF = r("IF", [TT, HK])
        JF = r("JF", [TT, HK])
        FV = r("FV", [TT, HK])
        IT = r("IT", [T])
        JT = r("JT", [T])
        GT = r("GT", [T])
        R1 = r("R1", [T])
        R2 = r("R2", [T])
        gsm = r("gsm", [TT * PEER_H])
        gbf = r("gbf", [T], bf16)
        ohJ = r("ohJ", [2, TOK_I, NKEYS], bf16)
        ohI = r("ohI", [2, TOK_I, 3, NKEYS], bf16)
        late = r.at
        sc = r("sc", [TT, 2 * PEER_H, NKEYS])
        cand = r("cand", [PEER_H, TOPK * TOPK])
        cand2 = r("cand2", [PEER_H, TOPK * TOPK])
        top = r("top", [PEER_H, 2, TOPK])
        topi = r("topi", [PEER_H, 2, TOPK], u32)
        topf = r("topf", [PEER_H, 2, TOPK])
        fin = r("fin", [PEER_H, TOPK])
        fpos = r("fpos", [HK], u32)
        fsel = r("fsel", [HK], u32)
        fself = r("fself", [HK])
        scur = cand
        scur2 = cand2
        qs = r("qs", [2, T])
        x2n = Place(late)("x2n", [TT, D])
        gstage = Place(late)("gstage", [2, NKEYS, STAGE_T])
        v = Place(late)
        a_in = v("a_in", [4, T])
        g_in = v("g_in", [2, BLOCKS, GROUP, STAGE_T])
        wf = v("wf", [2, T])
        wT_hi = v("wT_hi", [2, T], f32r)
        wT_lo = v("wT_lo", [2, T], f32r)
        gfin = v("gfin", [D])
        junk = v("junk", [D])

        bank = [ctx.enter_context(nc.psum_tensor(f"bank{b}", [P, 512], f32)) for b in range(8)]

        def mem_scores(u, n):
            return bank[2 + 2 * (u % 2) + n // 2][:, n % 2 * M:(n % 2 + 1) * M]

        def sem(name):
            return ctx.enter_context(nc.semaphore(name))

        raw_loaded = [sem(f"raw_loaded{i}") for i in range(RAW)]
        hi_ready, lo_ready, chunk_used = sem("hi_ready"), sem("lo_ready"), sem("chunk_used")
        proj_read = sem("proj_read")
        mem_loaded, gains_loaded, small_loaded = sem("mem_loaded"), sem("gains_loaded"), sem("small_loaded")
        x_loaded = [sem(f"x_loaded{t}") for t in range(TT)]
        consts = sem("consts")
        pool_step, dve_step, act_step = sem("pool_step"), sem("dve_step"), sem("act_step")
        eps_set = sem("eps_set")
        std_ready = sem("std_ready")
        normed = sem("normed")
        turned = sem("turned")
        turned_hi, turned_lo = sem("turned_hi"), sem("turned_lo")
        vm_read = sem("vm_read")
        angles, sines = sem("angles"), sem("sines")
        swapped, rotated = sem("swapped"), sem("rotated")
        k_ready, v_ready, v_turned = sem("k_ready"), sem("v_ready"), sem("v_turned")
        pooled, mixed = sem("pooled"), sem("mixed")
        y_hi, y_lo = sem("y_hi"), sem("y_lo")
        scored, score_read, capped = sem("scored"), sem("score_read"), sem("capped")
        expd, prob_ready = sem("expd"), sem("prob_ready")
        probT_done, probT_read = sem("probT_done"), sem("probT_read")
        attended = sem("attended")
        gated, branch_read = sem("gated"), sem("branch_read")
        merged, merged_hi, merged_lo = sem("merged"), sem("merged_hi"), sem("merged_lo")
        x2_ready = sem("x2_ready")
        sub_done, sub_read = sem("sub_done"), sem("sub_read")
        shifted, exp_final, retrieved = sem("shifted"), sem("exp_final"), sem("retrieved")
        spread, spread_read = sem("spread"), sem("spread_read")
        hot_ready, gate_mm, gate_read = sem("hot_ready"), sem("gate_mm"), sem("gate_read")
        a_stored = [sem("a_stored0"), sem("a_stored1")]
        g_stored = [sem("g_stored0"), sem("g_stored1")]
        a_loaded = [sem(f"a_loaded{i}") for i in range(4)]
        g_loaded = [sem(f"g_loaded{i}") for i in range(2)]
        summed = sem("summed")
        gfin_loaded = sem("gfin_loaded")
        weighted, weighted_hi, weighted_lo = sem("weighted"), sem("weighted_hi"), sem("weighted_lo")
        x3_ready, final_std, final_ready, out_stored = (sem("x3_ready"), sem("final_std"),
                                                        sem("final_ready"), sem("out_stored"))

        block = ctx.enter_context(nc.Block())

        class Steps:
            def __init__(self, eng, own):
                self.eng, self.own, self.value, self.made = eng, own, 0, 0

            def __call__(self, ins):
                ins.then_inc(self.own, 1)
                self.value, self.made = self.value + 1, self.made + 1
                self.eng.wait_ge(self.own, self.value)

        @block.sync
        def _(sp):
            stream = dram["stream"]
            a_rows = dram["a"]
            g_rows = dram["g"]

            def load(n, slot, fresh=False):
                if not fresh:
                    sp.wait_ge(lo_ready, n - RAW + 1)
                sp.dma_start(raw[:, slot, :], stream[bass.ds(n, 1), :, :].rearrange("n p c -> p (n c)")
                             ).then_inc(raw_loaded[slot], 16)

            sp.dma_start(mem_sb[:, 0, :], dram["mem"][0:P, :]).then_inc(mem_loaded, 16)
            for n in range(2):
                load(n, n, fresh=True)
            for t in range(TT):
                sp.dma_start(x_sb[:, t, :], dram["x"][t * P:(t + 1) * P, :]).then_inc(x_loaded[t], 16)
            for n in range(2, RAW):
                load(n, n, fresh=True)
            smalls = [(pscale[:, :], dram["pscale"]),
                      (wpool[:, :, :], dram["wpool"]), (sinks[:, :], dram["sinks"].broadcast_to([P, 16])),
                      (freq[:, :], dram["freq"]), (pos_i[:, :], dram["positions"].broadcast_to([P, T])),
                      (subkeys[:, :, :], dram["subkeys"])]
            assert len(smalls) == SMALLS
            for dst, src in smalls:
                sp.dma_start(dst, src).then_inc(small_loaded, 16)
            first_u = S_U + AHEAD
            with sp.Fori(RAW, first_u // RAW * RAW - RAW + 1, RAW) as n0:
                for k in range(RAW):
                    load(n0 + k, k)
            for n in range(first_u // RAW * RAW, first_u):
                load(n, n % RAW)

            def store_a(i, parity):
                sp.wait_ge(proj_read, i + (R_U + 1))
                sp.dma_start(a_rows[bass.ds(i, 1), :, :].rearrange("n p c -> p (n c)"),
                             abuf[:, parity, :]).then_inc(a_stored[parity], 16)

            def store_g(block, half, piece):
                q = NI // GROUP // 4
                rows = slice(piece * q * GROUP, (piece + 1) * q * GROUP)
                sp.dma_start(g_rows[piece * q:(piece + 1) * q, :, bass.ds(block, 1), :].rearrange(
                                 "g j b c -> j g (b c)"),
                             gstage[:, half, rows, :].rearrange("j (g i) t -> j g (i t)", i=GROUP)
                             ).then_inc(g_stored[half], 16)

            with sp.Fori(0, I_PLAIN - RAW + 1, RAW) as i0:
                for k in range(RAW):
                    load(i0 + (first_u + k), (first_u + k) % RAW)
                    store_a(i0 + k, k % 2)

            def gate_block(b0, half, first=False):
                for k in range(PER):
                    at = I_PLAIN + half * PER + k
                    load(b0 * PER + (first_u + at), (first_u + at) % RAW)
                    store_a(b0 * PER + at, at % 2)
                    if not first:
                        if k == 0:
                            sp.wait_ge(gate_read, b0 * (2 * PER) + (half * 2 * PER + 2))
                        if k < 4:
                            store_g(b0 + (half - 1), 1 - half, k)

            gate_block(0, 0, first=True)
            gate_block(0, 1)
            with sp.Fori(2, BLOCKS - 1, 2) as b0:
                for half in range(2):
                    gate_block(b0, half)

            def reload_a(i, slot, fresh=False):
                if not fresh:
                    sp.wait_ge(weighted, i - 3)
                sp.dma_start(a_in[:, slot, :], a_rows[bass.ds(i, 1), :, :].rearrange("n p c -> p (n c)")
                             ).then_inc(a_loaded[slot], 16)

            def reload_g(group, slot, done=None):
                if done is not None:
                    sp.wait_ge(weighted, done)
                sp.dma_start(g_in[:, slot, :, :, :].rearrange("j b i t -> j (b i t)"),
                             g_rows[bass.ds(group, 1), :, :, :].rearrange("g j b c -> j (g b c)")
                             ).then_inc(g_loaded[slot], 16)

            for k in range(I_TAIL):
                at = I_PLAIN + I_GATES + k
                load(first_u + at, (first_u + at) % RAW)
                store_a(at, at % 2)
                if k == 0:
                    sp.wait_ge(gate_read, BLOCKS * 2 * PER + 2)
                if k < 4:
                    store_g(BLOCKS - 1, 1, k)
                if k == 9:
                    for half in range(2):
                        sp.wait_ge(g_stored[half], 16 * 4 * BLOCKS // 2)
                    reload_g(0, 0)
                    for i in range(4):
                        if i < 2:
                            sp.wait_ge(a_stored[i], 32)
                        reload_a(i, i, fresh=True)
            for parity in range(2):
                sp.wait_ge(a_stored[parity], 16 * NI // 2)
            sp.dma_start(gfin[:, :], dram["gfin"].broadcast_to([P, D])).then_inc(gfin_loaded, 16)
            nxt = first_u + NI
            left = CHUNKS - nxt

            def value_step(i0, k, more=True, again=True):
                if more:
                    load(i0 + (nxt + k), (nxt + k) % RAW)
                if again:
                    reload_a(i0 + (k + 4), k % 4)

            for k in range(16):
                if k == 0:
                    reload_g(1, 1)
                if k == 8:
                    reload_g(2, 0, done=8)
                value_step(0, k)
            with sp.Fori(1, NI // 16 - 1) as b0:
                for k in range(16):
                    if k % 8 == 0:
                        reload_g(b0 * 2 + (k // 8 + 1), (k // 8 + 1) % 2, done=b0 * 16 + k)
                    value_step(b0 * 16, k)
            for k in range(16):
                i = NI - 16 + k
                if k == 0:
                    reload_g(NI // GROUP - 1, 1, done=i)
                value_step(NI - 16, k, more=i < left, again=i + 4 < NI)

            for t in range(TT):
                sp.wait_ge(final_ready, t + 1)
                sp.dma_start(out[t * P:(t + 1) * P, :], x_sb[:, t, :]).then_inc(out_stored, 16)
            sp.wait_ge(out_stored, 16 * TT)

        @block.gpsimd
        def _(pool):
            step = Steps(pool, pool_step)
            step(pool.memset(ident[:, :], 0.0))
            pool.affine_select(out=ident[:, :], in_=ident[:, :], compare_op=ALU.not_equal, fill=1.0,
                               base=0, pattern=[[-1, P]], channel_multiplier=1).then_inc(consts, 1)
            step(pool.memset(mask[:, :, :], 0.0))
            for f in range(2):
                step(pool.affine_select(out=mask[:, f, :], in_=mask[:, f, :], compare_op=ALU.is_ge, fill=NEG,
                                        base=WINDOW, pattern=[[-1, 2 * WINDOW]], channel_multiplier=1))
                step(pool.affine_select(out=mask[:, f, :], in_=mask[:, f, :], compare_op=ALU.is_ge, fill=NEG,
                                        base=-1, pattern=[[1, 2 * WINDOW]], channel_multiplier=-1))
            step(pool.affine_select(out=mask[:, 0, :], in_=mask[:, 0, :], compare_op=ALU.is_ge, fill=NEG,
                                    base=-WINDOW, pattern=[[1, 2 * WINDOW]], channel_multiplier=0))
            pool.iota(iota_b[:, :], pattern=[[1, NKEYS]], base=0, channel_multiplier=0,
                      allow_small_or_imprecise_dtypes=True)
            pool.iota(iota_k[:, :], pattern=[[1, TOPK]], base=0, channel_multiplier=0,
                      allow_small_or_imprecise_dtypes=True)
            pool.iota(rcnt[:, :, :], pattern=[[0, 4], [1, PAD]], base=1, channel_multiplier=0,
                      allow_small_or_imprecise_dtypes=True).then_inc(consts, 1)

            def low(n, k):
                pool.wait_ge(hi_ready, n + 1)
                pool.tensor_tensor(w_lo[:, k % 2, :], raw[:, k % RAW, :], w_hi[:, k % 2, :].bitcast(f32),
                                   ALU.subtract).then_inc(lo_ready, 1)

            with pool.Fori(0, CHUNKS // RAW * RAW - RAW + 1, RAW) as n0:
                for k in range(RAW):
                    low(n0 + k, k)
            for n in range(CHUNKS // RAW * RAW, CHUNKS):
                low(n, n)

        @block.tensor
        def _(pe):
            passes = ((w_hi, 0), (w_hi, 1), (w_lo, 0))

            def chunk(n):
                pe.wait_ge(lo_ready, n + 1)

            def product(dst, slot, rhs, k0=0, k1=KC, r0=0, used=True, before=None):
                for k in range(k0, k1):
                    if before is not None:
                        before(k)
                    for wi, (w, low) in enumerate(passes):
                        last = pe.matmul(dst, w[:, slot, k * P:(k + 1) * P], rhs[low][:, r0 + k - k0, :],
                                         start=(k == k0 and wi == 0), stop=(k == k1 - 1 and wi == 2))
                if used:
                    last.then_inc(chunk_used, 1)
                return last

            hT = (hT_hi, hT_lo)
            memT = (memT_hi, memT_lo)
            yT = (yT_hi, yT_lo)

            def project(n, rn, rhs, cols=T, strict=False, before=None):
                chunk(n)
                if strict:
                    pe.wait_ge(proj_read, rn)
                elif rn >= 2:
                    pe.wait_ge(proj_read, rn - 1)
                product(bank[0 if strict else rn % 2][:, 0:cols], n % 2, rhs, before=before)

            def turn(src, tok_ready, base, k, first=False):
                if k >= 4 or not first:
                    pe.wait_ge(turned_lo, base + max(k - 3, 0))
                for t in range(TT):
                    if k == 0:
                        pe.wait_ge(normed, tok_ready + t)
                    last = pe.transpose(bank[4 + k % 4][:, t * P:(t + 1) * P],
                                        src[:, t, k * P:(k + 1) * P], ident[:, :])
                last.then_inc(turned, 1)

            def split_ready(base):
                return lambda k: pe.wait_ge(turned_lo, base + k + 1)

            pe.wait_ge(consts, 1)
            for k in range(KC):
                for t in range(MT):
                    if k == 0:
                        pe.wait_ge(normed, t + 1)
                    last = pe.transpose(bank[k][:, t * P:(t + 1) * P],
                                        memn[:, t, k * P:(k + 1) * P], ident[:, :])
                last.then_inc(turned, 1)
            for h in range(4):
                project(S_KM + h, R_KM + h, memT, cols=M, before=split_ready(0) if h == 0 else None)
                if h >= 1:
                    turn(xn, MT + 1, KC, h - 1, first=True)
            for q in range(4):
                chunk(S_VM + q)
                for k in range(2):
                    for m in range(MT):
                        for low_m, w in ((0, w_hi), (0, w_lo), (1, w_hi)):
                            last = pe.matmul(bank[2 + m][:, :], memT[low_m][:, 2 * q + k, m * P:(m + 1) * P],
                                             w[:, q % 2, k * T:(k + 1) * T],
                                             start=(q == 0 and k == 0 and low_m == 0 and w is w_hi),
                                             stop=(q == 3 and k == 1 and low_m == 1))
                last.then_inc(chunk_used, 1)
                turn(xn, MT + 1, KC, 3 + q, first=True)
            turn(xn, MT + 1, KC, KC - 1, first=True)
            project(S_K, R_K, hT, before=split_ready(KC))
            project(S_V, R_V, hT)

            def turn_values():
                pe.wait_ge(proj_read, R_V + 1)
                for t in range(TT):
                    last = pe.transpose(bank[5][:, t * P:(t + 1) * P], vT[:, t * P:(t + 1) * P], ident[:, :])
                last.then_inc(v_turned, 1)

            def mix(gi):
                pe.wait_ge(pooled, gi + 1)
                if gi >= 2:
                    pe.wait_ge(y_lo, gi - 1)
                pe.matmul(bank[6 + gi % 2][:, :], wpool[:, gi, :], ub[:, PAD:], start=True,
                          stop=True).then_inc(mixed, 1)

            for gi in range(4):
                project(S_POOL + gi, R_POOL + gi, hT)
                if gi == 0:
                    turn_values()
                else:
                    mix(gi - 1)
            for u in range(2):
                project(S_Q + u, R_Q + u, hT)
            mix(3)

            def window_values(u):
                kv = u % 2
                for n in range(TT + 1):
                    if n < TT:
                        pe.wait_ge(prob_ready, 4 * u + n + 1)
                        if 4 * u + n >= 2:
                            pe.wait_ge(probT_read, 4 * u + n - 1)
                        for h in range(2):
                            for half in range(n == 0, 2):
                                last = pe.transpose(bank[6 + n % 2][:, (2 * h + half) * P:(2 * h + half + 1) * P],
                                                    prob[u % 2][:, n, h, half * P:(half + 1) * P], ident[:, :])
                        last.then_inc(probT_done, 1)
                    if n == 0 and u >= 1:
                        pe.wait_ge(y_lo, 4 + u)
                    if n >= 1:
                        pe.wait_ge(probT_read, 4 * u + n)
                        first = int(n == 1)
                        for half in range(first, 2):
                            for h in range(2):
                                last = pe.matmul(bank[1][h * HEAD:(h + 1) * HEAD, (n - 1) * P:n * P],
                                                 v_sb[:, kv, n - 2 + half, :],
                                                 probT[:, (n - 1) % 2, (2 * h + half) * P:(2 * h + half + 1) * P],
                                                 start=(half == first), stop=(half == 1))
                last.then_inc(attended, 1)

            def memory_values(u):
                for j in range(2):
                    pe.wait_ge(prob_ready, 32 + 4 * u + 2 * j + 2)
                    pe.wait_ge(probT_read, 32 + 2 * u + j - 1)
                    for n in (2 * j, 2 * j + 1):
                        for half in range(2):
                            last = pe.transpose(bank[6 + j][:, (n % 2 * 2 + half) * P:(n % 2 * 2 + half + 1) * P],
                                                prob[u % 2][:, n, 0, half * P:(half + 1) * P], ident[:, :])
                    last.then_inc(probT_done, 1)
                pe.wait_ge(y_lo, 12 + u)
                for j in range(2):
                    pe.wait_ge(probT_read, 32 + 2 * u + j + 1)
                    for n in (2 * j, 2 * j + 1):
                        for half in range(2):
                            last = pe.matmul(bank[1][:, n * P:(n + 1) * P], vm[:, half, u * P:(u + 1) * P],
                                             probT[:, j, (n % 2 * 2 + half) * P:(n % 2 * 2 + half + 1) * P],
                                             start=(half == 0), stop=(half == 1))
                last.then_inc(attended, 1)

            pe.wait_ge(vm_read, 1)
            pe.wait_ge(v_ready, 1)
            pe.wait_ge(k_ready, 1)
            for u in range(8):
                kv = u % 2
                pe.wait_ge(rotated, 1 + u + 1)
                if u >= 1:
                    pe.wait_ge(score_read, 4 * u)
                for n in range(TT):
                    for h in range(2):
                        last = pe.matmul(bank[2 + 2 * h + n // 2][:, n % 2 * 2 * WINDOW:(n % 2 + 1) * 2 * WINDOW],
                                         qr[h * HEAD:(h + 1) * HEAD, u % 2, n * P:(n + 1) * P],
                                         kdup[h * HEAD:(h + 1) * HEAD, kv, n * P:n * P + 2 * WINDOW],
                                         start=True, stop=True)
                        if n % 2:
                            last.then_inc(scored, 1)
                if u == 1:
                    pe.wait_ge(y_lo, 4)
                if u >= 1:
                    window_values(u - 1)
                project(S_Q + u + 2, R_Q + u + 2, hT, strict=(u > 0))
            for u in range(4):
                pe.wait_ge(proj_read, R_QM + u + 1)
                pe.wait_ge(score_read, 32 if u < 2 else 32 + 4 * (u - 1))
                for n in range(TT):
                    last = pe.matmul(mem_scores(u, n), qr[:, u % 2, n * P:(n + 1) * P], kmT[:, u, :],
                                     start=True, stop=True)
                    if n % 2:
                        last.then_inc(scored, 1)
                if u in (1, 2):
                    project(S_QM + u + 1, R_QM + u + 1, hT, strict=True)
                if u == 0:
                    window_values(7)
                else:
                    memory_values(u - 1)
            memory_values(3)
            with pe.Fori(0, KC - 2 + 1, 2) as c0:
                for dc in range(2):
                    for b in range(3):
                        n = S_GATE + GATE_CHUNKS * dc + b
                        chunk(c0 * GATE_CHUNKS + n)
                        if b == 0:
                            pe.wait_ge(gated, c0 * 3 + (3 * dc + 3))
                        if b == 1 and dc == 0:
                            pe.wait_ge(y_lo, 16)
                        product(bank[b][:, :], n % 2, hT)
                    n = S_GATE + GATE_CHUNKS * dc + 3
                    pe.wait_ge(branch_read, c0 * 3 + (3 * dc + 3))
                    chunk(c0 * GATE_CHUNKS + n)
                    product(bank[3][:, :], n % 2, yT, 0, 4, 0, used=False)
                    product(bank[4][:, :], n % 2, yT, 4, 8, 4)
                    chunk(c0 * GATE_CHUNKS + (n + 1))
                    product(bank[5][:, :], (n + 1) % 2, yT, 0, 8, 8)
            def spread_sum(slot, lhs, first, final, before=None, order=range(TT)):
                for t in order:
                    if before is not None:
                        before(t)
                    for w, low_l in ((w_hi, 0), (w_lo, 0), (w_hi, 1)):
                        for half in range(2):
                            last = pe.matmul(bank[2 * t + half][:, :], lhs[low_l][:, t * P:(t + 1) * P],
                                             w[:, slot, half * 512:(half + 1) * 512],
                                             start=first and low_l == 0 and w is w_hi, stop=final and low_l == 1)
                    if final and t < TT - 1:
                        last.then_inc(summed, 1)
                last.then_inc(chunk_used, 1)

            def bank_free(t):
                if t == 0:
                    pe.wait_ge(gated, 3 * KC + 3)
                if t == 1:
                    pe.wait_ge(branch_read, 3 * KC + 3)

            for k in range(KC):
                chunk(S_OUT + k)
                pe.wait_ge(merged_lo, k + 1)
                spread_sum((S_OUT + k) % 2, (mg_hi[:, k, :], mg_lo[:, k, :]), k == 0, k == KC - 1,
                           before=bank_free if k == 0 else None, order=(3, 0, 1, 2) if k == 0 else range(TT))
            pe.wait_ge(x2_ready, TT)
            for k in range(4):
                turn(x2n, MT + TT + 1, 2 * KC, k)

            def next_turn(k):
                if k + 4 < KC:
                    turn(x2n, MT + TT + 1, 2 * KC, k + 4)
                pe.wait_ge(turned_lo, 2 * KC + k + 1)

            def queries(c0, dc, before=None):
                rn = R_PQ + dc
                chunk(c0 + (S_PQ + dc))
                pe.wait_ge(proj_read, c0 + (rn - 1))
                product(bank[rn % 2][:, :], (S_PQ + dc) % 2, hT, before=before)

            def sub_scores(c0, dc):
                b = dc % 2
                pe.wait_ge(proj_read, c0 + (R_PQ + dc + 1))
                pe.wait_ge(sub_read, c0 + (dc + 1))
                for t in range(TT):
                    last = pe.matmul(bank[2 + b][:, t * P:(t + 1) * P], qs[:, b, t * P:(t + 1) * P],
                                     subkeys[:, bass.ds(c0 + dc, 1), :], start=True, stop=True)
                last.then_inc(sub_done, 1)

            queries(0, 0, before=next_turn)
            with pe.Fori(0, 2 * PEER_H - 3, 2) as c0:
                for dc in range(2):
                    queries(c0, dc + 1)
                    sub_scores(c0, dc)
            queries(2 * PEER_H - 2, 1)
            for dc in range(2):
                sub_scores(2 * PEER_H - 2, dc)

            def experts(i0, di):
                n, rn = S_U + di, R_U + di
                chunk(n + i0)
                pe.wait_ge(proj_read, rn - 1 + i0)
                product(bank[rn % 2][:, :], n % 2, hT)

            with pe.Fori(0, I_PLAIN - I_SPREAD - 2 + 1, 2) as i0:
                for di in range(2):
                    experts(i0, di)
            pe.wait_ge(sub_read, 2 * PEER_H + 2)
            pe.wait_ge(retrieved, 1)
            for j, src in enumerate((IF, JF, FV)):
                for t in range(TT):
                    last = pe.transpose(bank[2 + j][:, t * P:(t + 1) * P], src[:, t, :], ident[:, :])
                last.then_inc(spread, 1)
            for di in range(I_SPREAD):
                experts(I_PLAIN - I_SPREAD, di)
            pe.wait_ge(spread_read, 1)
            with pe.Fori(0, I_GATES - 2 + 1, 2) as i0:
                for di in range(2):
                    experts(i0 + I_PLAIN, di)
                    for b in range(2):
                        pe.wait_ge(gate_read, i0 * 2 + (2 * di + b + 1))
                        pe.wait_ge(hot_ready, i0 * 2 + (2 * di + b + 1))
                        for tk in range(TOK_I // 2):
                            at = b * (TOK_I // 2) + tk
                            for q in range(3):
                                last = pe.matmul(bank[2 + b][:, tk * P:(tk + 1) * P], ohJ[:, di, at, :],
                                                 ohI[:, di, at, q, :], start=(q == 0), stop=(q == 2))
                        last.then_inc(gate_mm, 1)
            with pe.Fori(I_PLAIN + I_GATES, NI - 1, 2) as i0:
                for di in range(2):
                    experts(i0, di)
            pe.wait_ge(gate_read, 2 * I_GATES + 2)

            def a_read(t):
                if t == 0:
                    pe.wait_ge(proj_read, R_U + NI)

            def weigh(i0, di, first=False, final=False):
                n = S_EV + di
                chunk(n + i0)
                pe.wait_ge(weighted_lo, i0 + (di + 1))
                spread_sum(n % 2, (wT_hi[:, di % 2, :], wT_lo[:, di % 2, :]), first, final,
                           before=a_read if first else None, order=(1, 2, 3, 0) if first else range(TT))

            for i in range(2):
                weigh(0, i, first=(i == 0))
            with pe.Fori(2, NI - 2 - 2 + 1, 2) as i0:
                for di in range(2):
                    weigh(i0, di)
            for i in range(NI - 2, NI):
                weigh(0, i, final=(i == NI - 1))

        @block.scalar
        def _(act):
            step = Steps(act, act_step)
            act.dma_start(mem_sb[:, 1, :], dram["mem"][P:2 * P, :]).then_inc(mem_loaded, 16)
            act.dma_start(gains[:, :, :], dram["gains"]).then_inc(gains_loaded, 16)

            def split(base, loop=0):
                slot = base % RAW
                act.wait_ge(raw_loaded[slot], loop * (16 // RAW) + (base // RAW + 1) * 16)
                if base >= 2:
                    act.wait_ge(chunk_used, loop + (base - 1))
                act.activation(w_hi[:, base % 2, :], raw[:, slot, :], ACT.Copy).then_inc(hi_ready, 1)

            act.wait_ge(eps_set, 1)
            step(act.activation(std[:, 7:8], eps[:, :], ACT.Sqrt))
            act.wait_ge(mem_loaded, 16 * MT)
            for t in range(MT):
                last = act.activation(memn[:, t, :], mem_sb[:, t, :], ACT.Square, accum_out=ssum[:, t:t + 1])
            step(last)
            act.activation(std[:, 0:MT], ssum[:, 0:MT], ACT.Sqrt, scale=1.0 / D,
                           bias=eps[:, :]).then_inc(std_ready, 1)
            split(0)
            split(1)
            act.wait_ge(gains_loaded, 16)
            for k in range(KC):
                act.wait_ge(turned, k + 1)
                act.activation(memT_hi[:, k, :], bank[k][:, 0:M], ACT.Copy,
                               scale=gains[:, 1, k:k + 1]).then_inc(turned_hi, 1)

            def deviation(dst, src, t, col):
                step(act.activation(dst[:, t, :], src[:, t, :], ACT.Square, accum_out=ssum[:, col:col + 1]))
                act.activation(std[:, col:col + 1], ssum[:, col:col + 1], ACT.Sqrt, scale=1.0 / D,
                               bias=eps[:, :]).then_inc(std_ready, 1)

            def turn_high(gain, base, k):
                act.wait_ge(turned, base + k + 1)
                act.activation(hT_hi[:, k, :], bank[4 + k % 4][:, :], ACT.Copy,
                               scale=gains[:, gain, k:k + 1]).then_inc(turned_hi, 1)

            def x_deviation(t):
                act.wait_ge(x_loaded[t], 16)
                deviation(xn, x_sb, t, 2 + t)

            for h in range(4):
                if h < 2:
                    for t in (2 * h, 2 * h + 1):
                        x_deviation(t)
                act.wait_ge(chunk_used, S_KM + h + 1)
                split(S_KM + h + 2)
                act.activation(kmT[:, h, :], bank[(R_KM + h) % 2][:, 0:M], ACT.Copy).then_inc(proj_read, 1)
                if h >= 1:
                    turn_high(0, KC, h - 1)
            for q in range(4):
                split(S_VM + q + 2)
                turn_high(0, KC, 3 + q)
            turn_high(0, KC, KC - 1)
            for m in range(MT):
                last = act.activation(vm[:, m, :], bank[2 + m][:, :], ACT.Copy)
            last.then_inc(vm_read, 1)
            act.wait_ge(angles, 2)
            act.activation(cosT[:, :], cosT[:, :], ACT.Sin).then_inc(sines, 1)
            act.activation(sinT[:, :], sinT[:, :], ACT.Sin, scale=freq[:, 1:2]).then_inc(sines, 1)

            def swap(j, rn, n):
                act.wait_ge(chunk_used, n + 1)
                if j >= 1:
                    act.wait_ge(rotated, j)
                b = rn % 2 if j < 3 else 0
                for qd in range(4):
                    last = act.activation(swp[32 * qd:32 * qd + 32, :],
                                          bank[b][32 * (qd ^ 1):32 * (qd ^ 1) + 32, :], ACT.Copy)
                last.then_inc(swapped, 1)

            split(S_K + 2)
            swap(0, R_K, S_K)
            split(S_V + 2)
            act.wait_ge(chunk_used, S_V + 1)
            act.wait_ge(proj_read, R_K + 1)
            act.activation(vT[:, :], bank[R_V % 2][:, :], ACT.Copy).then_inc(proj_read, 1)

            def double_keys():
                act.wait_ge(rotated, 1)
                for kv in range(2):
                    for h in range(2):
                        last = act.activation(kdup[h * HEAD:(h + 1) * HEAD, kv, WINDOW:],
                                              k_rot[kv * HEAD:(kv + 1) * HEAD, :], ACT.Copy)
                last.then_inc(k_ready, 1)

            def place_values():
                act.wait_ge(v_turned, 1)
                vb = bank[5][:, :].rearrange("p (t c) -> p t c", t=TT)
                for kv in range(2):
                    last = act.activation(v_sb[:, kv, :, :], vb[:, :, kv * HEAD:(kv + 1) * HEAD], ACT.Copy)
                last.then_inc(v_ready, 1)

            def mix_high(gi):
                act.wait_ge(mixed, gi + 1)
                act.activation(yT_hi[:, gi, :], bank[6 + gi % 2][:, :], ACT.Copy,
                               scale=pscale[:, gi:gi + 1]).then_inc(y_hi, 1)

            for gi in range(4):
                split(S_POOL + gi + 2)
                if gi == 0:
                    double_keys()
                if gi == 1:
                    place_values()
                if gi >= 1:
                    mix_high(gi - 1)
            split(S_Q + 2)
            swap(1, R_Q, S_Q)
            mix_high(3)

            def next_q(n, ahead=True):
                if ahead:
                    split(S_Q + n + 3)
                if n + 1 < 8:
                    swap(2 + n, R_Q + n + 1, S_Q + n + 1)
                else:
                    act.wait_ge(chunk_used, S_Q + n + 2)
                    act.activation(qr[:, (n + 1) % 2, :], bank[0][:, :], ACT.Copy).then_inc(proj_read, 1)

            def turn_probs(count, made):
                for n in range(count):
                    act.wait_ge(probT_done, made + n + 1)
                    first = int(count == TT and n == 0)
                    blocks = "p (h f q) -> p h f q"
                    act.activation(probT[:, n % 2, :].rearrange(blocks, h=2, f=2)[:, :, first:, :],
                                   bank[6 + n % 2][:, :].rearrange(blocks, h=2, f=2)[:, :, first:, :],
                                   ACT.Copy).then_inc(probT_read, 1)

            def outputs_high(row, made):
                act.wait_ge(attended, made)
                act.activation(yT_hi[:, row, :], bank[1][:, :], ACT.Copy).then_inc(y_hi, 1)

            for u in range(8):
                next_q(u)
                if u >= 1:
                    turn_probs(TT, 4 * (u - 1))
                    outputs_high(8 + u - 1, u)
                act.wait_ge(capped, u + 1)
                pr = prob[u % 2]
                for n in range(TT):
                    for h in range(2):
                        act.activation(pr[:, n, h, :], pr[:, n, h, :], ACT.Exp, scale=HEAD ** -0.5,
                                       bias=negm[:, 2 * n + h:2 * n + h + 1],
                                       accum_out=rsum[:, 2 * n + h:2 * n + h + 1])
                act.activation(sexp[:, :], sdiff[:, :], ACT.Exp).then_inc(expd, 1)
            for u in range(4):
                if u == 0:
                    next_q(8)
                    turn_probs(TT, 4 * 7)
                    outputs_high(8 + 7, 8)
                act.wait_ge(capped, 8 + u + 1)
                for n in range(TT):
                    act.activation(prob[u % 2][:, n, 0, :], mem_scores(u, n), ACT.Exp, scale=P ** -0.5,
                                   bias=negm[:, n:n + 1], accum_out=rsum[:, n:n + 1]).then_inc(score_read, 1)
                if u in (1, 2):
                    next_q(8 + u, ahead=False)
                if u >= 1:
                    turn_probs(2, 32 + 2 * (u - 1))
                    if u < 3:
                        split(S_Q + 8 + u + 3)
                    outputs_high(4 + u - 1, 8 + u)
            turn_probs(2, 32 + 2 * 3)
            outputs_high(4 + 3, 12)
            act.sem_inc(gated, 3)
            with act.Fori(0, KC - 4 + 1, 4) as c0:
                for dc in range(4):
                    for q in range(GATE_CHUNKS):
                        base = S_GATE + GATE_CHUNKS * dc + q
                        split(base + 2, loop=c0 * GATE_CHUNKS)
                        if q == 0:
                            act.wait_ge(branch_read, c0 * 3 + (3 * dc + 3))
                        if q < 3:
                            act.wait_ge(chunk_used, c0 * GATE_CHUNKS + (base + 1))
                            act.activation(sg[:, q, :], bank[q][:, :], ACT.Sigmoid).then_inc(gated, 1)
                    act.wait_ge(merged, c0 + (dc + 1))
                    act.activation(mg_hi[:, bass.ds(c0 + dc, 1), :], part[:, 0:1, :], ACT.Copy).then_inc(merged_hi, 1)
            for k in range(KC - 1):
                split(S_OUT + k + 2)
            for t in range(TT):
                act.wait_ge(x2_ready, t + 1)
                deviation(x2n, x_sb, t, t)
            split(S_OUT + KC - 1 + 2)
            for k in range(KC):
                turn_high(2, 2 * KC, k)
            with act.Fori(0, 2 * PEER_H - 4 + 1, 4) as c0:
                for dc in range(4):
                    base = S_PQ + dc
                    act.wait_ge(chunk_used, base + 1 + c0)
                    split(base + 2, loop=c0)
                    act.activation(qs[:, dc % 2, :], bank[(R_PQ + dc) % 2][:, :], ACT.Copy).then_inc(proj_read, 1)

            def gelu(i0, di):
                base = S_U + di
                split(base + 2, loop=i0)
                act.wait_ge(chunk_used, base + 1 + i0)
                if not (isinstance(i0, int) and i0 + di < 2):
                    act.wait_ge(a_stored[di % 2], (i0 + (di - di % 2)) * 8)
                act.activation(abuf[:, di % 2, :], bank[(R_U + di) % 2][:, :],
                               ACT.Gelu_apprx_tanh).then_inc(proj_read, 1)

            for i in range(4):
                gelu(0, i)
            with act.Fori(4, I_PLAIN - 8 + 1, 4) as i0:
                for di in range(4):
                    gelu(i0, di)
            act.wait_ge(shifted, 1)
            act.activation(FV[:, :, :], FV[:, :, :], ACT.Exp).then_inc(exp_final, 1)
            for di in range(4):
                gelu(I_PLAIN - 4, di)
            act.sem_inc(gate_read, 2)

            def gates_out(i0, first=False):
                for half in range(2):
                    if not first:
                        act.wait_ge(g_stored[half], i0 * (4 * 16 // (2 * PER)))
                    for k in range(PER):
                        di = half * PER + k
                        gelu(i0 + I_PLAIN, di)
                        for b in range(2):
                            act.wait_ge(gate_mm, i0 * 2 + (2 * di + b + 1))
                            t0 = k * TOK_I + b * TOK_I // 2
                            act.activation(gstage[:, half, :, t0:t0 + TOK_I // 2].rearrange("p i t -> p t i"),
                                           bank[2 + b][:, :].rearrange("p (t i) -> p t i", i=NKEYS),
                                           ACT.Copy).then_inc(gate_read, 1)

            gates_out(0, first=True)
            with act.Fori(2 * PER, I_GATES - 2 * PER + 1, 2 * PER) as i0:
                gates_out(i0)
            def weigh_high(i0, di):
                act.wait_ge(weighted, i0 + (di + 1))
                act.activation(wT_hi[:, di % 2, :], wf[:, di % 2, :], ACT.Copy).then_inc(weighted_hi, 1)

            with act.Fori(I_PLAIN + I_GATES, NI - 7, 4) as i0:
                for di in range(4):
                    gelu(i0, di)
            for di in range(4):
                if di == 3:
                    weigh_high(0, 0)
                gelu(NI - 4, di)

            with act.Fori(0, NI - 4 - 4 + 1, 4) as i0:
                for di in range(4):
                    weigh_high(i0, di + 1)
                    split(S_EV + di + 2, loop=i0)
            for i in range(NI - 4, NI - 1):
                weigh_high(0, i + 1)
                if i < NI - 2:
                    split(S_EV + i + 2)
            for t in range(TT):
                act.wait_ge(x3_ready, t + 1)
                step(act.activation(junk[:, :], x_sb[:, t, :], ACT.Square, accum_out=ssum[:, t:t + 1]))
                act.activation(std[:, t:t + 1], ssum[:, t:t + 1], ACT.Sqrt, scale=1.0 / D,
                               bias=eps[:, :]).then_inc(final_std, 1)

        @block.vector
        def _(dve):
            step = Steps(dve, dve_step)
            dve.memset(eps[:, :], EPS).then_inc(eps_set, 1)
            dve.memset(kdup[:, :, 0:WINDOW], 0.0)
            for buf in (ub, sA, sB):
                dve.memset(buf[:, 0:PAD], 0.0)

            def normalise(dst, src, t, col):
                dve.tensor_scalar(dst[:, t, :], src[:, t, :], rstd[:, col:col + 1], None, ALU.mult).then_inc(normed, 1)

            dve.wait_ge(std_ready, 1)
            step(dve.reciprocal(rstd[:, 0:MT], std[:, 0:MT]))
            for t in range(MT):
                normalise(memn, mem_sb, t, t)
            dve.wait_ge(gains_loaded, 16)
            for k in range(KC):
                dve.wait_ge(turned_hi, k + 1)
                dve.scalar_tensor_tensor(out=memT_lo[:, k, :], in0=bank[k][:, 0:M],
                                         scalar=gains[:, 1, k:k + 1], in1=memT_hi[:, k, :].bitcast(f32),
                                         op0=ALU.mult, op1=ALU.subtract).then_inc(turned_lo, 1)
            for t in range(TT):
                dve.wait_ge(std_ready, 1 + t + 1)
                step(dve.reciprocal(rstd[:, 2 + t:3 + t], std[:, 2 + t:3 + t]))
                normalise(xn, x_sb, t, 2 + t)
            dve.wait_ge(small_loaded, 16 * SMALLS)
            two_pi = 2 * math.pi
            c1 = 6.28125
            c2 = float(np.float32(np.floor((two_pi - c1) * 2 ** 21) / 2 ** 21))
            c3 = float(np.float32(two_pi - c1 - c2))
            magic = 1.5 * 2 ** 23
            limit = 3.1415925
            posf, ang, turns = sg[:, 0, :], sg[:, 1, :], sg[:, 2, :]
            step(dve.tensor_copy(posf, pos_i[:, :]))
            step(dve.tensor_scalar(ang, posf, freq[:, 0:1], None, ALU.mult))
            for made, (dst, quarter) in enumerate(((sinT, 0.0), (cosT, 0.25))):
                step(dve.tensor_scalar(turns, ang, 1.0 / two_pi, quarter, ALU.mult, ALU.add))
                step(dve.tensor_scalar(turns, turns, magic, None, ALU.add))
                step(dve.tensor_scalar(turns, turns, -magic, None, ALU.add))
                step(dve.scalar_tensor_tensor(out=posf, in0=turns, scalar=-c1, in1=ang, op0=ALU.mult, op1=ALU.add))
                step(dve.scalar_tensor_tensor(out=dst[:, :], in0=turns, scalar=-c2, in1=posf, op0=ALU.mult, op1=ALU.add))
                step(dve.scalar_tensor_tensor(out=posf, in0=turns, scalar=-c3, in1=dst[:, :], op0=ALU.mult, op1=ALU.add))
                step(dve.tensor_scalar(turns, posf, quarter * two_pi, limit, ALU.add, ALU.min))
                dve.tensor_scalar(dst[:, :], turns, -limit, None, ALU.max).then_inc(angles, 1)
                dve.wait_ge(angles, made + 1)
            dve.wait_ge(consts, 2)
            for gi, w in enumerate(POOL_WINDOWS):
                last = dve.tensor_scalar(rcnt[:, gi, :], rcnt[:, gi, :], float(w), None, ALU.min)
            step(last)
            step(dve.reciprocal(rcnt[:, :, :], rcnt[:, :, :]))

            def turn_low(gain, base):
                for k in range(KC):
                    dve.wait_ge(turned_hi, base + k + 1)
                    dve.scalar_tensor_tensor(out=hT_lo[:, k, :], in0=bank[4 + k % 4][:, :],
                                             scalar=gains[:, gain, k:k + 1], in1=hT_hi[:, k, :].bitcast(f32),
                                             op0=ALU.mult, op1=ALU.subtract).then_inc(turned_lo, 1)

            turn_low(0, KC)
            dve.wait_ge(sines, 2)

            def rotate_bank(j, rn, dst):
                dve.wait_ge(swapped, j + 1)
                dve.tensor_tensor(dst, bank[rn % 2 if j < 3 else 0][:, :], cosT[:, :], ALU.mult).then_inc(proj_read, 1)

            def rotate(j, rn, dst, bank_done=False):
                if not bank_done:
                    rotate_bank(j, rn, dst)
                step(dve.tensor_tensor(swp[:, :], swp[:, :], sinT[:, :], ALU.mult))
                dve.tensor_tensor(dst, dst, swp[:, :], ALU.add).then_inc(rotated, 1)

            rotate(0, R_K, k_rot[:, :])

            def window(gi):
                dve.wait_ge(chunk_used, S_POOL + gi + 1)
                if gi == 0:
                    dve.wait_ge(proj_read, R_V + 1)
                if gi >= 1:
                    dve.wait_ge(pooled, gi)
                dve.tensor_copy(sA[:, PAD:], bank[(R_POOL + gi) % 2][:, :]).then_inc(proj_read, 1)
                dve.wait_ge(proj_read, R_POOL + gi + 1)
                if gi >= 1:
                    dve.wait_ge(mixed, gi)
                step(dve.tensor_scalar(ub[:, PAD:], sA[:, PAD:], -1.0, None, ALU.mult))
                src, dst = sA, sB
                for lv in range(gi + 1):
                    sh = 1 << lv
                    step(dve.tensor_tensor(dst[:, PAD:], src[:, PAD:], src[:, PAD - sh:PAD + T - sh], ALU.add))
                    src, dst = dst, src
                w = POOL_WINDOWS[gi]
                step(dve.tensor_tensor(dst[:, PAD:2 * PAD], src[:, PAD:2 * PAD], rcnt[:, gi, :], ALU.mult))
                step(dve.scalar_tensor_tensor(out=ub[:, 2 * PAD:], in0=src[:, 2 * PAD:], scalar=1.0 / w,
                                              in1=ub[:, 2 * PAD:], op0=ALU.mult, op1=ALU.add))
                dve.tensor_tensor(ub[:, PAD:2 * PAD], dst[:, PAD:2 * PAD], ub[:, PAD:2 * PAD],
                                  ALU.add).then_inc(pooled, 1)

            def mix_low(gi):
                dve.wait_ge(y_hi, gi + 1)
                dve.scalar_tensor_tensor(out=yT_lo[:, gi, :], in0=bank[6 + gi % 2][:, :],
                                         scalar=pscale[:, gi:gi + 1], in1=yT_hi[:, gi, :].bitcast(f32),
                                         op0=ALU.mult, op1=ALU.subtract).then_inc(y_lo, 1)
            for gi in range(4):
                window(gi)
                if gi >= 1:
                    mix_low(gi - 1)
            rotate(1, R_Q, qr[:, 0, :])
            mix_low(3)

            def outputs_low(row, made):
                dve.wait_ge(y_hi, made)
                dve.tensor_tensor(yT_lo[:, row, :], bank[1][:, :], yT_hi[:, row, :].bitcast(f32),
                                  ALU.subtract).then_inc(y_lo, 1)

            for u in range(8):
                pr = prob[u % 2]
                pair = [b[:, :].rearrange("p (n h) -> p n h", h=2) for b in (mx, mcap, sdiff)]
                if u >= 2:
                    dve.wait_ge(probT_done, 4 * (u - 1))
                for b in range(4):
                    j, h = b // 2, b % 2
                    dve.wait_ge(scored, 4 * u + b + 1)
                    seen = mask[:, :, :] if j == 0 else mask[:, 1:2, :].broadcast_to([P, 2, 2 * WINDOW])
                    dve.tensor_tensor(pr[:, 2 * j:2 * j + 2, h, :],
                                      bank[2 + 2 * h + j][:, :].rearrange("p (n k) -> p n k", n=2), seen,
                                      ALU.add).then_inc(score_read, 1)
                turned_q = (2 + u, R_Q + u + 1, qr[:, (u + 1) % 2, :])
                if u < 7:
                    rotate_bank(*turned_q)
                for b in range(4):
                    j, h = b // 2, b % 2
                    if b == 0:
                        dve.wait_ge(score_read, 4 * (u + 1))
                    last = dve.reduce_max(pair[0][:, 2 * j:2 * j + 2, h:h + 1], pr[:, 2 * j:2 * j + 2, h, :], AX.X)
                step(last)
                snk = sinks[:, 2 * u:2 * u + 2].unsqueeze(1).broadcast_to([P, TT, 2])
                step(dve.scalar_tensor_tensor(out=pair[1], in0=pair[0], scalar=HEAD ** -0.5, in1=snk,
                                              op0=ALU.mult, op1=ALU.max))
                dve.tensor_scalar(negm[:, :], mcap[:, :], -1.0, None, ALU.mult)
                dve.tensor_tensor(pair[2], snk, pair[1], ALU.subtract).then_inc(capped, 1)
                if u < 7:
                    dve.wait_ge(proj_read, R_Q + u + 2)
                    rotate(*turned_q, bank_done=True)
                if u >= 1:
                    outputs_low(8 + u - 1, 4 + u)
                dve.wait_ge(expd, u + 1)
                step(dve.tensor_tensor(den[:, :], rsum[:, :], sexp[:, :], ALU.add))
                step(dve.reciprocal(rinv[:, :], den[:, :]))
                for n in range(TT):
                    for h in range(2):
                        last = dve.tensor_scalar(pr[:, n, h, :], pr[:, n, h, :],
                                                 rinv[:, 2 * n + h:2 * n + h + 1], None, ALU.mult)
                    last.then_inc(prob_ready, 1)
            for u in range(4):
                for n in range(TT):
                    dve.wait_ge(scored, 32 + 2 * u + n // 2 + 1)
                    last = dve.reduce_max(mx[:, n:n + 1], mem_scores(u, n), AX.X)
                step(last)
                dve.wait_ge(probT_done, 28 if u == 0 else 32 + 2 * (u - 1))
                dve.tensor_scalar(negm[:, 0:TT], mx[:, 0:TT], -(P ** -0.5), None, ALU.mult).then_inc(capped, 1)
                if u == 0:
                    outputs_low(8 + 7, 12)
                dve.wait_ge(score_read, 32 + 4 * (u + 1))
                dve.wait_ge(prob_ready, 32 + 4 * u)
                step(dve.reciprocal(rinv[:, 0:TT], rsum[:, 0:TT]))
                for n in range(TT):
                    dve.tensor_scalar(prob[u % 2][:, n, 0, :], prob[u % 2][:, n, 0, :], rinv[:, n:n + 1], None,
                                      ALU.mult).then_inc(prob_ready, 1)
                if u >= 1:
                    outputs_low(4 + u - 1, 12 + u)
            outputs_low(4 + 3, 16)
            dve.sem_inc(branch_read, 3)
            first_step, per_turn = step.value, 1
            with dve.Fori(0, KC) as c:
                step.value, step.made = c * per_turn + first_step, 0
                dve.wait_ge(gated, c * 3 + 6)
                dve.wait_ge(chunk_used, c * GATE_CHUNKS + (S_GATE + GATE_CHUNKS))
                for q, b in enumerate((3, 5, 4)):
                    dve.tensor_tensor(part[:, q, :], sg[:, q, :], bank[b][:, :], ALU.mult).then_inc(branch_read, 1)
                dve.wait_ge(branch_read, c * 3 + 6)
                step(dve.tensor_tensor(part[:, 1, :], part[:, 1, :], part[:, 2, :], ALU.add))
                dve.tensor_tensor(part[:, 0, :], part[:, 0, :], part[:, 1, :], ALU.add).then_inc(merged, 1)
                dve.wait_ge(merged_hi, c + 1)
                dve.tensor_tensor(mg_lo[:, bass.ds(c, 1), :], part[:, 0:1, :],
                                  mg_hi[:, bass.ds(c, 1), :].bitcast(f32), ALU.subtract).then_inc(merged_lo, 1)
                dve.wait_ge(merged_lo, c + 1)
                assert step.made == per_turn
            step.value = first_step + per_turn * KC
            for t in range(TT):
                if t < TT - 1:
                    dve.wait_ge(summed, t + 1)
                else:
                    dve.wait_ge(chunk_used, S_PQ)
                for half in range(2):
                    cols = slice(half * 512, (half + 1) * 512)
                    last = dve.tensor_tensor(x_sb[:, t, cols], x_sb[:, t, cols], bank[2 * t + half][:, :], ALU.add)
                last.then_inc(x2_ready, 1)
            for t in range(TT):
                dve.wait_ge(std_ready, 1 + TT + t + 1)
                step(dve.reciprocal(rstd[:, t:t + 1], std[:, t:t + 1]))
                normalise(x2n, x_sb, t, t)
            turn_low(2, 2 * KC)
            dve.sem_inc(sub_read, 2)
            with dve.Fori(0, 2 * PEER_H - 2 + 1, 2) as c0:
                for dc in range(2):
                    dve.wait_ge(sub_done, c0 + (dc + 1))
                    dve.tensor_copy(sc[:, :, bass.ds(c0 + dc, 1), :],
                                    bank[2 + dc][:, :].rearrange("p (t a n) -> p t a n", t=TT, a=1)
                                    ).then_inc(sub_read, 1)
            dve.wait_ge(sub_read, 2 * PEER_H + 2)

            halves = [(h, q) for h in range(PEER_H) for q in range(2)]
            hrow = lambda buf, h: buf[:, h, :]
            s1 = lambda buf, h, q: buf[:, h, q * NKEYS:(q + 1) * NKEYS]
            all2 = "p h (a b) -> p h a b"

            def best(src, spare, vals, inds):
                for s_, v_ in zip(src, vals):
                    dve.max(v_[:, 0:8], s_)
                dve.drain()
                for s_, z_, v_, i_ in zip(src, spare, vals, inds):
                    dve.max_index(i_[:, 0:8], v_[:, 0:8], s_)
                    dve.match_replace(z_, v_[:, 0:8], s_, BELOW)
                dve.drain()
                for z_, v_ in zip(spare, vals):
                    dve.max(v_[:, 8:16], z_)
                dve.drain()
                for z_, v_, i_ in zip(spare, vals, inds):
                    dve.max_index(i_[:, 8:16], v_[:, 8:16], z_)
                dve.drain()

            with dve.Fori(0, TT) as t:
                scur4 = scur[:, :, :].rearrange("p h (q n) -> p (h q) n", q=2)
                dve.tensor_copy(scur4.unsqueeze(1), sc[:, bass.ds(t, 1), :, :])
                dve.drain()
                best([s1(scur, h, q) for h, q in halves], [s1(scur2, h, q) for h, q in halves],
                     [top[:, h, q, :] for h, q in halves], [topi[:, h, q, :] for h, q in halves])
                dve.tensor_copy(topf[:, :, :, :], topi[:, :, :, :])
                grid = [P, PEER_H, TOPK, TOPK]
                dve.tensor_tensor(cand[:, :, :].rearrange(all2, a=TOPK),
                                  top[:, :, 0, :].unsqueeze(3).broadcast_to(grid),
                                  top[:, :, 1, :].unsqueeze(2).broadcast_to(grid), ALU.add)
                dve.drain()
                best([hrow(cand, h) for h in range(PEER_H)], [hrow(cand2, h) for h in range(PEER_H)],
                     [hrow(fin, h) for h in range(PEER_H)],
                     [fpos[:, h * TOPK:(h + 1) * TOPK] for h in range(PEER_H)])
                dve.tensor_tensor(FV[:, bass.ds(t, 1), :].rearrange("p a (h k) -> p (a h) k", h=PEER_H), fin[:, :, :],
                                  fin[:, :, 0:1].broadcast_to([P, PEER_H, TOPK]), ALU.subtract)
                for q, dst in ((0, IF), (1, JF)):
                    if q == 0:
                        dve.tensor_scalar(fsel[:, :], fpos[:, :], 4, None, ALU.logical_shift_right)
                        dve.drain()
                    else:
                        dve.tensor_scalar(fsel[:, :], fpos[:, :], TOPK - 1, None, ALU.bitwise_and)
                        dve.drain()
                    dve.tensor_copy(fself[:, :], fsel[:, :])
                    dve.drain()
                    flat = [P, HK, TOPK]
                    pick = cand[:, :, :].rearrange("p h (k a) -> p (h k) a", a=TOPK)
                    dve.tensor_tensor(pick, fself[:, :].unsqueeze(2).broadcast_to(flat),
                                      iota_k[:, :].unsqueeze(1).broadcast_to(flat), ALU.is_equal)
                    dve.drain()
                    pick4 = cand[:, :, :].rearrange(all2, a=TOPK)
                    dve.tensor_tensor(pick4, pick4, topf[:, :, q, :].unsqueeze(2).broadcast_to(grid), ALU.mult)
                    dve.drain()
                    dve.tensor_reduce(dst[:, bass.ds(t, 1), :].rearrange("p a n -> p (a n)"), pick,
                                      AX.X, ALU.add)
                    dve.drain()
            dve.drain().then_inc(shifted, 1)
            dve.wait_ge(exp_final, 1)
            rows3 = FV[:, :, :].rearrange("p t (h k) -> p (t h) k", k=TOPK)
            step(dve.reduce_sum(gsm[:, :], rows3, AX.X))
            step(dve.reciprocal(gsm[:, :], gsm[:, :]))
            dve.tensor_tensor(rows3, rows3, gsm[:, :].unsqueeze(2).broadcast_to([P, TT * PEER_H, TOPK]),
                              ALU.mult).then_inc(retrieved, 1)
            dve.wait_ge(spread, 3)
            dve.tensor_copy(IT[:, :], bank[2][:, :])
            dve.tensor_copy(JT[:, :], bank[3][:, :])
            dve.tensor_copy(GT[:, :], bank[4][:, :]).then_inc(spread_read, 1)
            dve.wait_ge(spread_read, 1)
            step(dve.tensor_copy(gbf[:, :], GT[:, :]))
            step(dve.tensor_tensor(R1[:, :], GT[:, :], gbf[:, :], ALU.subtract))
            step(dve.tensor_copy(gbf[:, :], R1[:, :]))
            step(dve.tensor_tensor(R2[:, :], R1[:, :], gbf[:, :], ALU.subtract))

            def one_hots(i0, di, first=False):
                for b in range(2):
                    if not first:
                        dve.wait_ge(gate_mm, i0 * 2 + (2 * di + b - 3))
                    for tk in range(TOK_I // 2):
                        at = b * (TOK_I // 2) + tk
                        col = bass.ds(i0 * TOK_I + (di * TOK_I + at), 1)
                        dve.tensor_scalar(ohJ[:, di, at, :], iota_b[:, :], JT[:, col], None, ALU.is_equal)
                        for q, gate in enumerate((GT, R1, R2)):
                            last = dve.tensor_scalar(ohI[:, di, at, q, :], iota_b[:, :], IT[:, col], gate[:, col],
                                                     ALU.is_equal, ALU.mult)
                    last.then_inc(hot_ready, 1)

            for di in range(2):
                one_hots(0, di, first=True)
            with dve.Fori(2, I_GATES - 2 + 1, 2) as i0:
                for di in range(2):
                    one_hots(i0, di)

            def weigh(i0, di, first=False):
                dve.wait_ge(a_loaded[di % 4], i0 * 4 + (di // 4 + 1) * 16)
                if di % GROUP == 0:
                    dve.wait_ge(g_loaded[di // GROUP], i0 + 16)
                if not first:
                    dve.wait_ge(chunk_used, i0 + (S_EV + di - 1))
                tiles = "p (b t) -> p b t"
                dve.tensor_tensor(wf[:, di % 2, :].rearrange(tiles, b=BLOCKS),
                                  a_in[:, di % 4, :].rearrange(tiles, b=BLOCKS),
                                  g_in[:, di // GROUP, :, di % GROUP, :], ALU.mult).then_inc(weighted, 1)
                dve.wait_ge(weighted_hi, i0 + (di + 1))
                dve.tensor_tensor(wT_lo[:, di % 2, :], wf[:, di % 2, :], wT_hi[:, di % 2, :].bitcast(f32),
                                  ALU.subtract).then_inc(weighted_lo, 1)

            for i in range(16):
                weigh(0, i, first=(i < 2))
            with dve.Fori(16, NI - 15, 16) as i0:
                for di in range(16):
                    weigh(i0, di)
            dve.wait_ge(gfin_loaded, 16)
            for t in range(TT):
                if t < TT - 1:
                    dve.wait_ge(summed, TT - 1 + t + 1)
                else:
                    dve.wait_ge(chunk_used, CHUNKS)
                for half in range(2):
                    cols = slice(half * 512, (half + 1) * 512)
                    last = dve.tensor_tensor(x_sb[:, t, cols], x_sb[:, t, cols], bank[2 * t + half][:, :], ALU.add)
                last.then_inc(x3_ready, 1)
            for t in range(TT):
                dve.wait_ge(final_std, t + 1)
                step(dve.reciprocal(rstd[:, t:t + 1], std[:, t:t + 1]))
                dve.scalar_tensor_tensor(out=x_sb[:, t, :], in0=x_sb[:, t, :], scalar=rstd[:, t:t + 1],
                                         in1=gfin[:, :], op0=ALU.mult, op1=ALU.mult).then_inc(final_ready, 1)


def layout(inputs):
    f = lambda n: np.ascontiguousarray(inputs[n])
    w_in, w_kv = f("w_in")[0], f("w_mem_kv")[0]
    pool_w, swa_w, kv_w = 4 * P, D, 2 * HEAD
    q0 = pool_w
    k0 = q0 + swa_w
    v0 = k0 + kv_w
    m0 = v0 + kv_w
    g0 = m0 + 4 * P

    def cols(w, idx):
        w = w[:, idx]
        return w.reshape(-1, P, P).transpose(1, 0, 2).reshape(P, -1)

    chunks = [cols(w_kv, slice(h * P, (h + 1) * P)) for h in range(4)]
    vals = w_kv[:, 4 * P:].reshape(KC, P, T)
    chunks += [vals[2 * q:2 * q + 2].transpose(1, 0, 2).reshape(P, D) for q in range(4)]
    chunks.append(cols(w_in, slice(k0, k0 + P)))
    chunks.append(cols(w_in, slice(v0, v0 + P)))
    chunks += [cols(w_in, slice(gi * P, (gi + 1) * P)) for gi in range(4)]
    chunks += [cols(w_in, slice(q0 + c * P, q0 + (c + 1) * P)) for c in Q_ORDER]
    chunks += [cols(w_in, slice(m0 + h * P, m0 + (h + 1) * P)) for h in range(4)]
    pm = np.concatenate([f("w_branch_pool")[0], f("w_branch_mem")[0]], axis=0)
    sw = f("w_branch_swa")[0].reshape(8, P, D)[Q_ORDER].reshape(D, D)
    for c in range(KC):
        for b in range(3):
            chunks.append(cols(w_in, slice(g0 + b * D + c * P, g0 + b * D + (c + 1) * P)))
        chunks.append(cols(pm, slice(c * P, (c + 1) * P)))
        chunks.append(cols(sw, slice(c * P, (c + 1) * P)))
    chunks += list(f("w_out")[0].reshape(KC, P, D))
    chunks += [cols(f("peer_w_q")[0], slice(c * P, (c + 1) * P)) for c in range(2 * PEER_H)]
    u = f("peer_u")[0].reshape(NI, P, KC, P).transpose(0, 3, 2, 1).reshape(NI, P, D)
    stream = np.concatenate([np.stack(chunks), u, f("peer_v")[0].reshape(NI, P, D)], axis=0)
    assert stream.shape == (CHUNKS, P, D)
    half = HEAD // 2
    inv = (10000.0 ** (-np.arange(half, dtype=np.float64) / half)).astype(np.float32)
    sign = np.where(np.arange(P) % HEAD < half, -1.0, 1.0).astype(np.float32)
    freq = np.stack([inv[np.arange(P) % half], sign], axis=1)
    gains = np.stack([f(n)[0].reshape(KC, P).T for n in ("norm1_g", "mem_norm_g", "norm2_g")], axis=1)
    return {
        "stream": stream,
        "x": f("x")[0], "mem": f("mem")[0], "positions": f("positions"),
        "gains": gains, "pscale": f("pool_scale")[0].reshape(4, P).T,
        "wpool": f("w_pool")[0].transpose(1, 0, 2),
        "sinks": f("attn_sinks").reshape(8, 2)[Q_ORDER].reshape(1, 16),
        "freq": freq,
        "subkeys": f("peer_sub_keys")[0].reshape(2 * PEER_H, NKEYS, P).transpose(2, 0, 1),
        "gfin": f("final_norm_g").reshape(1, D),
    }


def kernel(**inputs):
    import concourse.bacc as _bacc
    from concourse.bass_utils import run_bass_kernel_spmd as _run

    nc = _bacc.Bacc("TRN2", target_bir_lowering=False, num_devices=1)
    arrays, dram = {}, {}
    for name, a in layout(inputs).items():
        arrays[name] = np.ascontiguousarray(a)
        dram[name] = nc.dram_tensor(name, arrays[name].shape, mybir.dt.from_np(arrays[name].dtype),
                                    kind="ExternalInput").ap()
    for name, shape in (("a", (NI, P, T)),
                        ("g", (NI // GROUP, P, BLOCKS, GROUP * STAGE_T))):
        dram[name] = nc.dram_tensor(name + "_rows", shape, mybir.dt.float32, kind="Internal").ap()
    out = nc.dram_tensor("out", (T, D), mybir.dt.float32, kind="ExternalOutput").ap()
    build(nc, dram, out)
    r = _run(nc, [arrays], core_ids=[0])
    return r.results[0]["out"].reshape(1, T, D)
```
